# Optimizing a Trainium2 kernel written in Bass

```python
import math
import jax
import jax.numpy as jnp
from jax import lax
import numpy as np

D_MODEL = 1024
BATCH = 1
SEQ = 256
DEPTH = 2

CTX_LEN = 256
GRID_W = 64
NORM_EPS = 1e-6
ROPE_THETA = 10000.0

GDN_HEADS = 8
GDN_DK = 64
GDN_DV = 64
GDN_CHUNK = 64
CONV_K = 5

SWA_Q_HEADS = 8
SWA_KV_HEADS = 2
SWA_HEAD_DIM = 64
SWA_WINDOW = 128
SWA_BLOCK = 128

MLA_HEADS = 8
MLA_Q_RANK = 384
MLA_KV_RANK = 256
MLA_NOPE = 64
MLA_ROPE = 32
MLA_V = 64

DIFF_HEADS = 4
DIFF_HEAD_DIM = 64

Q_BLOCK = 128

D_FF = 2816
N_EXPERTS = 8
TOP_K = 2
D_FF_EXPERT = 3584

N_EVEN = (DEPTH + 1) // 2
N_ODD = DEPTH // 2

GDN_QKV = GDN_HEADS * (2 * GDN_DK + GDN_DV)
GDN_Z = GDN_HEADS * GDN_DV
SWA_Q = SWA_Q_HEADS * SWA_HEAD_DIM
SWA_KV = SWA_KV_HEADS * SWA_HEAD_DIM
EVEN_COLS = (GDN_QKV, GDN_Z, 2 * GDN_HEADS, 2 * GDN_HEADS, SWA_Q, SWA_KV, SWA_KV)
EVEN_IN = sum(EVEN_COLS)
EVEN_MIX = GDN_Z + SWA_Q

DIFF_QK = DIFF_HEADS * 2 * DIFF_HEAD_DIM
DIFF_VW = DIFF_HEADS * 2 * DIFF_HEAD_DIM
ODD_COLS = (MLA_Q_RANK, MLA_KV_RANK, MLA_ROPE, DIFF_QK, DIFF_QK, DIFF_VW)
ODD_IN = sum(ODD_COLS)
ODD_MIX = MLA_HEADS * MLA_V + DIFF_VW

kernel_name = 'hybrid_diffusion_trunk'

def split_cols(a, sizes):
    return jnp.split(a, np.cumsum(sizes)[:-1].tolist(), axis=-1)

def rmsnorm(x, w):
    xf = x.astype(jnp.float32)
    y = xf * lax.rsqrt(jnp.mean(xf * xf, axis=-1, keepdims=True) + NORM_EPS)
    return (y * w.astype(jnp.float32)).astype(x.dtype)

def l2norm(x):
    xf = x.astype(jnp.float32)
    return xf * lax.rsqrt(jnp.sum(xf * xf, axis=-1, keepdims=True) + NORM_EPS)

def modulate(h, shift, scale):
    return h * (1 + scale) + shift

def axial_rope_tables(rows, rot_dim):
    row = jnp.repeat(jnp.arange(rows, dtype=jnp.float32), GRID_W)
    col = jnp.tile(jnp.arange(GRID_W, dtype=jnp.float32), rows)
    half = rot_dim // 2
    inv_freq = ROPE_THETA ** (-jnp.arange(0, half, 2, dtype=jnp.float32) / half)
    ang_r = row[:, None] * inv_freq[None, :]
    ang_c = col[:, None] * inv_freq[None, :]
    ang = jnp.concatenate([ang_r, ang_r, ang_c, ang_c], axis=-1)
    return jnp.cos(ang), jnp.sin(ang)

def rotate_half(x):
    x1, x2 = jnp.split(x, 2, axis=-1)
    return jnp.concatenate([-x2, x1], axis=-1)

def apply_axial_rope(x, cos, sin):
    half = x.shape[-1] // 2
    rot = jnp.concatenate([rotate_half(x[..., :half]), rotate_half(x[..., half:])], axis=-1)
    return x * cos[None, :, None, :].astype(x.dtype) + rot * sin[None, :, None, :].astype(x.dtype)

def centred_dwconv(x, w):
    pad = CONV_K // 2
    return lax.conv_general_dilated(x, w[:, None, :].astype(x.dtype), window_strides=(1,),
                                    padding=[(pad, pad)], dimension_numbers=('NWC', 'WIO', 'NWC'),
                                    feature_group_count=x.shape[-1])

def gated_delta_chunked(q, k, v, g, beta, state0):
    B, T, H, Dk = q.shape
    Dv = v.shape[-1]
    C = GDN_CHUNK
    N = T // C

    def to_chunks(a):
        a = a.reshape(B, N, C, H, *a.shape[3:])
        return jnp.moveaxis(a, (1, 3), (0, 2))

    qc, kc, vc = to_chunks(q), to_chunks(k), to_chunks(v)
    gc = jnp.cumsum(to_chunks(g), axis=-1)
    bc = to_chunks(beta)
    idx = jnp.arange(C)
    lower_incl = idx[:, None] >= idx[None, :]
    strict = idx[:, None] > idx[None, :]
    decay = jnp.exp(jnp.where(lower_incl, gc[..., :, None] - gc[..., None, :], -jnp.inf))
    kb = kc * bc[..., None]
    vb = vc * bc[..., None]
    L = jnp.where(strict, jnp.einsum('nbhid,nbhjd->nbhij', kb, kc) * decay, 0.0)
    eye = jnp.eye(C, dtype=jnp.float32)
    t_inv = lax.linalg.triangular_solve(eye + L, jnp.broadcast_to(eye, L.shape), left_side=True, lower=True)
    u = t_inv @ vb
    w = t_inv @ (kb * jnp.exp(gc)[..., None])
    attn_intra = jnp.where(lower_incl, jnp.einsum('nbhid,nbhjd->nbhij', qc, kc) * decay, 0.0)
    g_last = gc[..., -1]
    k_tail = kc * jnp.exp(g_last[..., None] - gc)[..., None]
    q_head = qc * jnp.exp(gc)[..., None]

    def step(S, inp):
        q_h, k_t, u_i, w_i, a_i, gl = inp
        v_new = u_i - w_i @ S
        o = q_h @ S + a_i @ v_new
        S = S * jnp.exp(gl)[..., None, None] + jnp.swapaxes(k_t, -1, -2) @ v_new
        return S, o

    s_final, o = lax.scan(step, state0, (q_head, k_tail, u, w, attn_intra, g_last))
    o = jnp.moveaxis(o, (0, 2), (1, 3)).reshape(B, T, H, Dv)
    return o, s_final

def window_gqa_latent(q, k, v, k_ctx, v_ctx, sink):
    B, T, Hq, D = q.shape
    Hk = k.shape[2]
    G = Hq // Hk
    W = SWA_BLOCK
    nb = T // W
    Tc = k_ctx.shape[1]
    scale = D ** -0.5
    qb = q.reshape(B, nb, W, Hk, G, D)

    def band(a):
        ap = jnp.pad(a, ((0, 0), (W, W), (0, 0), (0, 0))).reshape(B, nb + 2, W, Hk, D)
        return jnp.concatenate([ap[:, :-2], ap[:, 1:-1], ap[:, 2:]], axis=2)

    k_win, v_win = band(k), band(v)
    i_abs = jnp.arange(nb)[:, None] * W + jnp.arange(W)[None, :]
    j_abs = jnp.arange(nb)[:, None] * W - W + jnp.arange(3 * W)[None, :]
    valid = ((jnp.abs(i_abs[:, :, None] - j_abs[:, None, :]) <= SWA_WINDOW)
             & (j_abs >= 0)[:, None, :] & (j_abs < T)[:, None, :])
    s_win = jnp.einsum('bnqhgd,bnkhd->bnhgqk', qb, k_win).astype(jnp.float32) * scale
    s_win = jnp.where(valid[None, :, None, None], s_win, -jnp.inf)
    s_ctx = jnp.einsum('bnqhgd,bchd->bnhgqc', qb, k_ctx).astype(jnp.float32) * scale
    s_sink = jnp.broadcast_to(sink.astype(jnp.float32).reshape(1, 1, Hk, G, 1, 1), s_ctx.shape[:-1] + (1,))
    p = jax.nn.softmax(jnp.concatenate([s_sink, s_ctx, s_win], axis=-1), axis=-1).astype(v.dtype)
    o = (jnp.einsum('bnhgqc,bchd->bnqhgd', p[..., 1:1 + Tc], v_ctx)
         + jnp.einsum('bnhgqk,bnkhd->bnqhgd', p[..., 1 + Tc:], v_win))
    return o.reshape(B, T, Hq * D)

def gqa_sink_dense(q, k, v, sink):
    B, Tq, Hq, D = q.shape
    Hk = k.shape[2]
    G = Hq // Hk
    qg = q.reshape(B, Tq, Hk, G, D)
    s = jnp.einsum('bqhgd,bkhd->bhgqk', qg, k).astype(jnp.float32) * D ** -0.5
    s_sink = jnp.broadcast_to(sink.astype(jnp.float32).reshape(1, Hk, G, 1, 1), s.shape[:-1] + (1,))
    p = jax.nn.softmax(jnp.concatenate([s_sink, s], axis=-1), axis=-1)[..., 1:].astype(v.dtype)
    o = jnp.einsum('bhgqk,bkhd->bqhgd', p, v)
    return o.reshape(B, Tq, Hq * D)

def sweep_query_blocks(fn, *qs):
    B, T = qs[0].shape[:2]
    nb = T // Q_BLOCK
    blocks = tuple(jnp.moveaxis(a.reshape(B, nb, Q_BLOCK, *a.shape[2:]), 1, 0) for a in qs)
    out = lax.map(lambda xs: fn(*xs), blocks)
    return jnp.moveaxis(out, 0, 1).reshape(B, T, *out.shape[3:])

def mla_attend(q_nope, q_rope, k_nope, k_rope, v):
    scale = (MLA_NOPE + MLA_ROPE) ** -0.5
    s = (jnp.einsum('bqhd,bshd->bhqs', q_nope, k_nope)
         + jnp.einsum('bqhr,bsr->bhqs', q_rope, k_rope)).astype(jnp.float32) * scale
    p = jax.nn.softmax(s, axis=-1).astype(v.dtype)
    return jnp.einsum('bhqs,bshd->bqhd', p, v)

def diff_attend(q1, q2, k1, k2, v, lam):
    scale = DIFF_HEAD_DIM ** -0.5
    s1 = jnp.einsum('bqhd,bshd->bhqs', q1, k1).astype(jnp.float32) * scale
    s2 = jnp.einsum('bqhd,bshd->bhqs', q2, k2).astype(jnp.float32) * scale
    a = jax.nn.softmax(s1, axis=-1) - lam * jax.nn.softmax(s2, axis=-1)
    return jnp.einsum('bhqs,bshe->bqhe', a.astype(v.dtype), v)

def even_mixer(h_c, h_l, w_in, conv_w, a_log, dt_bias, gdn_norm, sink, w_out, cos, sin, need_ctx):
    B, Tc, _ = h_c.shape
    T = h_l.shape[1]
    n_all = Tc + T
    proj = jnp.concatenate([h_c, h_l], axis=1) @ w_in
    qkv, z, ga, gb, sq, sk, sv = split_cols(proj, EVEN_COLS)

    g = -jnp.exp(a_log.astype(jnp.float32)) * jax.nn.softplus(
        ga.astype(jnp.float32).reshape(B, n_all, 2, GDN_HEADS) + dt_bias.astype(jnp.float32))
    beta = jax.nn.sigmoid(gb.astype(jnp.float32).reshape(B, n_all, 2, GDN_HEADS))

    def qkv_heads(u):
        n = u.shape[1]
        u = jax.nn.silu(centred_dwconv(u, conv_w))
        q, k, v = split_cols(u, (GDN_HEADS * GDN_DK, GDN_HEADS * GDN_DK, GDN_HEADS * GDN_DV))
        q = l2norm(q.reshape(B, n, GDN_HEADS, GDN_DK)) * GDN_DK ** -0.5
        k = l2norm(k.reshape(B, n, GDN_HEADS, GDN_DK))
        v = v.reshape(B, n, GDN_HEADS, GDN_DV).astype(jnp.float32)
        return q, k, v

    qc, kc, vc = qkv_heads(qkv[:, :Tc])
    ql, kl, vl = qkv_heads(qkv[:, Tc:])
    g_c, g_l = g[:, :Tc], g[:, Tc:]
    b_c, b_l = beta[:, :Tc], beta[:, Tc:]
    s0 = jnp.zeros((B, GDN_HEADS, GDN_DK, GDN_DV), jnp.float32)
    rev = lambda t: jnp.flip(t, axis=1)
    oc_f, s_f = gated_delta_chunked(qc, kc, vc, g_c[:, :, 0], b_c[:, :, 0], s0)
    oc_b, s_b = gated_delta_chunked(rev(qc), rev(kc), rev(vc), rev(g_c[:, :, 1]), rev(b_c[:, :, 1]), s0)
    ol_f, _ = gated_delta_chunked(ql, kl, vl, g_l[:, :, 0], b_l[:, :, 0], s_f)
    ol_b, _ = gated_delta_chunked(rev(ql), rev(kl), rev(vl), rev(g_l[:, :, 1]), rev(b_l[:, :, 1]), s_b)

    def gdn_out(o, zz):
        n = o.shape[1]
        o = rmsnorm(o, gdn_norm).astype(zz.dtype).reshape(B, n, GDN_Z)
        return o * jax.nn.silu(zz)

    lat_gdn = gdn_out(ol_f + rev(ol_b), z[:, Tc:])

    sq_c = sq[:, :Tc].reshape(B, Tc, SWA_Q_HEADS, SWA_HEAD_DIM)
    sk_c = sk[:, :Tc].reshape(B, Tc, SWA_KV_HEADS, SWA_HEAD_DIM)
    sv_c = sv[:, :Tc].reshape(B, Tc, SWA_KV_HEADS, SWA_HEAD_DIM)
    sq_l = apply_axial_rope(sq[:, Tc:].reshape(B, T, SWA_Q_HEADS, SWA_HEAD_DIM), cos, sin)
    sk_l = apply_axial_rope(sk[:, Tc:].reshape(B, T, SWA_KV_HEADS, SWA_HEAD_DIM), cos, sin)
    sv_l = sv[:, Tc:].reshape(B, T, SWA_KV_HEADS, SWA_HEAD_DIM)
    lat_swa = window_gqa_latent(sq_l, sk_l, sv_l, sk_c, sv_c, sink)

    y_l = jnp.concatenate([lat_gdn, lat_swa], axis=-1) @ w_out
    y_c = None
    if need_ctx:
        ctx_gdn = gdn_out(oc_f + rev(oc_b), z[:, :Tc])
        ctx_swa = gqa_sink_dense(sq_c, sk_c, sv_c, sink)
        y_c = jnp.concatenate([ctx_gdn, ctx_swa], axis=-1) @ w_out
    return y_c, y_l

def odd_mixer(h_c, h_l, w_in, q_norm, kv_norm, w_uq, w_ukv, lam_p, lam_init, subln, w_out,
              cos_d, sin_d, cos_r, sin_r, need_ctx):
    B, Tc, _ = h_c.shape
    T = h_l.shape[1]
    n_all = Tc + T
    proj = jnp.concatenate([h_c, h_l], axis=1) @ w_in
    cq, ckv, kr, dq, dk, dv = split_cols(proj, ODD_COLS)

    q_m = (rmsnorm(cq, q_norm) @ w_uq).reshape(B, n_all, MLA_HEADS, MLA_NOPE + MLA_ROPE)
    kv_m = (rmsnorm(ckv, kv_norm) @ w_ukv).reshape(B, n_all, MLA_HEADS, MLA_NOPE + MLA_V)
    qn, qr = q_m[..., :MLA_NOPE], q_m[..., MLA_NOPE:]
    kn, vm = kv_m[..., :MLA_NOPE], kv_m[..., MLA_NOPE:]
    qr_l = apply_axial_rope(qr[:, Tc:], cos_r, sin_r)
    kr_l = apply_axial_rope(kr[:, Tc:, None, :], cos_r, sin_r)[:, :, 0]
    kr_all = jnp.concatenate([kr[:, :Tc], kr_l], axis=1)
    mla_l = sweep_query_blocks(lambda a, b: mla_attend(a, b, kn, kr_all, vm), qn[:, Tc:], qr_l)
    mla_l = mla_l.reshape(B, T, MLA_HEADS * MLA_V)

    dq = dq.reshape(B, n_all, 2 * DIFF_HEADS, DIFF_HEAD_DIM)
    dk = dk.reshape(B, n_all, 2 * DIFF_HEADS, DIFF_HEAD_DIM)
    dv = dv.reshape(B, n_all, DIFF_HEADS, 2 * DIFF_HEAD_DIM)
    dq_l = apply_axial_rope(dq[:, Tc:], cos_d, sin_d).reshape(B, T, DIFF_HEADS, 2, DIFF_HEAD_DIM)
    dk_l = apply_axial_rope(dk[:, Tc:], cos_d, sin_d)
    dk_all = jnp.concatenate([dk[:, :Tc], dk_l], axis=1).reshape(B, n_all, DIFF_HEADS, 2, DIFF_HEAD_DIM)
    k1, k2 = dk_all[..., 0, :], dk_all[..., 1, :]
    lp = lam_p.astype(jnp.float32)
    lam = jnp.exp(jnp.sum(lp[0] * lp[1])) - jnp.exp(jnp.sum(lp[2] * lp[3])) + lam_init

    def diff_post(o):
        n = o.shape[1]
        return (rmsnorm(o, subln) * (1.0 - lam_init)).reshape(B, n, DIFF_VW)

    diff_l = sweep_query_blocks(lambda a, b: diff_attend(a, b, k1, k2, dv, lam),
                                dq_l[..., 0, :], dq_l[..., 1, :])
    y_l = jnp.concatenate([mla_l, diff_post(diff_l)], axis=-1) @ w_out
    y_c = None
    if need_ctx:
        mla_c = mla_attend(qn[:, :Tc], qr[:, :Tc], kn[:, :Tc], kr[:, :Tc], vm[:, :Tc])
        dq_c = dq[:, :Tc].reshape(B, Tc, DIFF_HEADS, 2, DIFF_HEAD_DIM)
        diff_c = diff_attend(dq_c[..., 0, :], dq_c[..., 1, :], k1[:, :Tc], k2[:, :Tc], dv[:, :Tc], lam)
        y_c = jnp.concatenate([mla_c.reshape(B, Tc, MLA_HEADS * MLA_V), diff_post(diff_c)], axis=-1) @ w_out
    return y_c, y_l

def swiglu(h, w_gate, w_up, w_down):
    return (jax.nn.silu(h @ w_gate) * (h @ w_up)) @ w_down

def moe_swiglu(h, w_router, w_gate, w_up, w_down):
    logits = (h @ w_router).astype(jnp.float32)
    top_val, top_idx = lax.top_k(logits, TOP_K)
    top_w = jax.nn.softmax(top_val, axis=-1)
    gates = jnp.sum(jax.nn.one_hot(top_idx, N_EXPERTS, dtype=jnp.float32) * top_w[..., None], axis=-2)
    gates = gates.astype(h.dtype)
    out = jnp.zeros_like(h)
    for e in range(N_EXPERTS):
        out = out + gates[:, e:e + 1] * swiglu(h, w_gate[e], w_up[e], w_down[e])
    return out

def setup_inputs(seed: int = 0) -> dict:
    key = jax.random.key(seed)
    keys = list(jax.random.split(key, 40))
    D = D_MODEL

    def nrm(shape, scale):
        return jax.random.normal(keys.pop(), shape, jnp.float32) * scale

    def gain(shape):
        return 1.0 + nrm(shape, 0.02)

    inp = {}
    inp['x'] = nrm((BATCH, SEQ, D), 1.0)
    inp['c'] = nrm((BATCH, D), 1.0)
    inp['ctx'] = nrm((BATCH, CTX_LEN, D), 1.0)
    inp['c_ctx'] = nrm((D,), 1.0)
    inp['e_mod_w'] = nrm((N_EVEN, D, 6 * D), D ** -0.5)
    inp['e_mod_b'] = nrm((N_EVEN, 6 * D), 0.02)
    inp['e_norms'] = gain((N_EVEN, 4, D))
    inp['e_w_in'] = nrm((N_EVEN, D, EVEN_IN), D ** -0.5)
    inp['e_conv_w'] = nrm((N_EVEN, CONV_K, GDN_QKV), CONV_K ** -0.5)
    inp['e_a_log'] = jnp.log(jax.random.uniform(keys.pop(), (N_EVEN, 2, GDN_HEADS), jnp.float32, 1.0, 16.0))
    inp['e_dt_bias'] = 1.0 + nrm((N_EVEN, 2, GDN_HEADS), 0.1)
    inp['e_gdn_norm'] = gain((N_EVEN, GDN_DV))
    inp['e_sink'] = nrm((N_EVEN, SWA_Q_HEADS), 0.5)
    inp['e_w_out'] = nrm((N_EVEN, EVEN_MIX, D), EVEN_MIX ** -0.5)
    inp['e_ffn_gate'] = nrm((N_EVEN, D, D_FF), D ** -0.5)
    inp['e_ffn_up'] = nrm((N_EVEN, D, D_FF), D ** -0.5)
    inp['e_ffn_down'] = nrm((N_EVEN, D_FF, D), D_FF ** -0.5)
    inp['o_mod_w'] = nrm((N_ODD, D, 6 * D), D ** -0.5)
    inp['o_mod_b'] = nrm((N_ODD, 6 * D), 0.02)
    inp['o_norms'] = gain((N_ODD, 4, D))
    inp['o_w_in'] = nrm((N_ODD, D, ODD_IN), D ** -0.5)
    inp['o_q_norm'] = gain((N_ODD, MLA_Q_RANK))
    inp['o_kv_norm'] = gain((N_ODD, MLA_KV_RANK))
    inp['o_w_uq'] = nrm((N_ODD, MLA_Q_RANK, MLA_HEADS * (MLA_NOPE + MLA_ROPE)), MLA_Q_RANK ** -0.5)
    inp['o_w_ukv'] = nrm((N_ODD, MLA_KV_RANK, MLA_HEADS * (MLA_NOPE + MLA_V)), MLA_KV_RANK ** -0.5)
    inp['o_lambda'] = nrm((N_ODD, 4, DIFF_HEAD_DIM), 0.1)
    inp['o_subln'] = gain((N_ODD, 2 * DIFF_HEAD_DIM))
    inp['o_w_out'] = nrm((N_ODD, ODD_MIX, D), ODD_MIX ** -0.5)
    inp['o_router'] = nrm((N_ODD, D, N_EXPERTS), D ** -0.5)
    inp['o_exp_gate'] = nrm((N_ODD, N_EXPERTS, D, D_FF_EXPERT), D ** -0.5)
    inp['o_exp_up'] = nrm((N_ODD, N_EXPERTS, D, D_FF_EXPERT), D ** -0.5)
    inp['o_exp_down'] = nrm((N_ODD, N_EXPERTS, D_FF_EXPERT, D), D_FF_EXPERT ** -0.5)
    return inp

def reference(x, c, ctx, c_ctx,
              e_mod_w, e_mod_b, e_norms, e_w_in, e_conv_w, e_a_log, e_dt_bias, e_gdn_norm, e_sink, e_w_out,
              e_ffn_gate, e_ffn_up, e_ffn_down,
              o_mod_w, o_mod_b, o_norms, o_w_in, o_q_norm, o_kv_norm, o_w_uq, o_w_ukv, o_lambda, o_subln,
              o_w_out, o_router, o_exp_gate, o_exp_up, o_exp_down):
    B, T, D = x.shape
    Tc = ctx.shape[1]
    rows = T // GRID_W
    cos_s, sin_s = axial_rope_tables(rows, SWA_HEAD_DIM)
    cos_d, sin_d = axial_rope_tables(rows, DIFF_HEAD_DIM)
    cos_r, sin_r = axial_rope_tables(rows, MLA_ROPE)
    silu_c = jax.nn.silu(c)
    silu_cc = jax.nn.silu(c_ctx)
    h_ctx = ctx
    for i in range(DEPTH):
        last = i == DEPTH - 1
        j = i // 2
        even = i % 2 == 0
        mod_w, mod_b, norms = (e_mod_w[j], e_mod_b[j], e_norms[j]) if even else (o_mod_w[j], o_mod_b[j], o_norms[j])
        m_l = jnp.split((silu_c @ mod_w + mod_b)[:, None, :], 6, axis=-1)
        m_c = jnp.split((silu_cc @ mod_w + mod_b)[None, None, :], 6, axis=-1)

        a_c = modulate(rmsnorm(h_ctx, norms[0]), m_c[0], m_c[1])
        a_l = modulate(rmsnorm(x, norms[0]), m_l[0], m_l[1])
        if even:
            y_c, y_l = even_mixer(a_c, a_l, e_w_in[j], e_conv_w[j], e_a_log[j], e_dt_bias[j], e_gdn_norm[j],
                                  e_sink[j], e_w_out[j], cos_s, sin_s, not last)
        else:
            lam_init = 0.8 - 0.6 * math.exp(-0.3 * i)
            y_c, y_l = odd_mixer(a_c, a_l, o_w_in[j], o_q_norm[j], o_kv_norm[j], o_w_uq[j], o_w_ukv[j],
                                 o_lambda[j], lam_init, o_subln[j], o_w_out[j], cos_d, sin_d, cos_r, sin_r,
                                 not last)
        x = x + m_l[2] * rmsnorm(y_l, norms[1])
        if not last:
            h_ctx = h_ctx + m_c[2] * rmsnorm(y_c, norms[1])

        f_in = modulate(rmsnorm(x, norms[2]), m_l[3], m_l[4])
        if not last:
            f_in = jnp.concatenate([modulate(rmsnorm(h_ctx, norms[2]), m_c[3], m_c[4]), f_in], axis=1)
        if even:
            f_out = swiglu(f_in, e_ffn_gate[j], e_ffn_up[j], e_ffn_down[j])
        else:
            f_out = moe_swiglu(f_in.reshape(-1, D), o_router[j], o_exp_gate[j], o_exp_up[j],
                               o_exp_down[j]).reshape(f_in.shape)
        x = x + m_l[5] * rmsnorm(f_out[:, -T:], norms[3])
        if not last:
            h_ctx = h_ctx + m_c[5] * rmsnorm(f_out[:, :Tc], norms[3])
    return x


_drawn_inputs = setup_inputs


def setup_inputs(seed=0):
    import zlib

    import numpy as np

    out = dict(_drawn_inputs(seed))
    spreads = {}
    factors = {'e_dt_bias': 3.994, 'e_sink': 8.0, 'o_q_norm': 8.0, 'o_kv_norm': 3.892}
    for name, (base, spread) in spreads.items():
        noise = np.random.default_rng([zlib.crc32(name.encode()), seed]).standard_normal(out[name].shape)
        drawn = base * np.exp(spread * noise) if base else spread * noise
        out[name] = jnp.asarray(drawn.astype(out[name].dtype))
    for name, factor in factors.items():
        out[name] = (out[name] * factor).astype(out[name].dtype)
    return out
```

```python
from contextlib import ExitStack

import numpy as np
import concourse.bass as bass
from concourse import mybir

F32 = mybir.dt.float32
I32 = mybir.dt.int32
ALU = mybir.AluOpType
ACT = mybir.ActivationFunctionType
AXX = mybir.AxisListType.X

P = 128
D = 1024
KB = D // P
TILES = 4
LAT = 2
SEQ = 512
EPS = 1e-6
HEADS = 8
HD = 64
CH = 64
F_DENSE = 2816
F_EXP = 3584
EXPERTS = 8
EVEN_T = 1536
EVEN_R = 1312
ODD_IN = 2208
LAM_INIT = 0.8 - 0.6 * float(np.exp(-0.3))
NEG = -1e30

CONST_PARTS = [("ident", 128), ("ones", 128), ("le", 128), ("gt", 128), ("ge", 128), ("lt", 128),
               ("le_c", 64), ("gt_c", 64), ("ge_c", 64), ("lt_c", 64),
               ("levels", 2 * 6 * 64), ("chunk_of", 128), ("eye_c", 64), ("band", 512), ("cos64", 128), ("sin64", 128),
               ("cos32", 64), ("sin32", 64), ("iota", 128), ("before", 128), ("earlier", 64)]
CONST_AT = {}
N_CONST = 0
for _name, _n in CONST_PARTS:
    CONST_AT[_name] = (N_CONST, _n)
    N_CONST += _n


def rope_table(dim):
    tok = np.arange(256)
    half = dim // 2
    inv = (10000.0 ** (-np.arange(0, half, 2, dtype=np.float32) / half)).astype(np.float32)
    ar = (tok // 64).astype(np.float32)[:, None] * inv
    ac = (tok % 64).astype(np.float32)[:, None] * inv
    ang = np.concatenate([ar, ar, ac, ac], -1).astype(np.float32)
    sign = np.tile(np.repeat([-1.0, 1.0], half // 2), 2).astype(np.float32)
    return np.cos(ang).astype(np.float32), np.sin(ang).astype(np.float32) * sign


def shape_constants():
    c = {}
    t = np.arange(P)
    same = (t[:, None] // CH) == (t[None, :] // CH)
    c["ident"], c["ones"] = np.eye(P), np.ones((P, P))
    tests = {"le": lambda a, b: a <= b, "gt": lambda a, b: a > b, "ge": lambda a, b: a >= b, "lt": lambda a, b: a < b}
    for n, f in tests.items():
        c[n] = f(t[:, None], t[None, :]) & same
        c[n + "_c"] = f((t % CH)[:, None], np.arange(CH)[None, :])
    lev = np.zeros((P, 2, 6, CH))
    i, j = (t % CH)[:, None], np.arange(CH)[None, :]
    for n in range(6):
        b = 1 << n
        lev[:, 0, n] = (i // (2 * b) == j // (2 * b)) & ((i // b) % 2 == 1) & ((j // b) % 2 == 0)
        lev[:, 1, n] = (i // (2 * b) == j // (2 * b)) & ((i // b) % 2 == 0) & ((j // b) % 2 == 1)
    c["levels"] = lev
    c["eye_c"] = i == j
    c["chunk_of"] = np.repeat((t // CH)[:, None] == np.arange(2)[None, :], CH, 1)
    band = np.zeros((P, 2, 256))
    for q in range(2):
        band[:, q] = np.where(np.abs((q * P + t)[:, None] - np.arange(256)[None, :]) <= 128, 0.0, NEG)
    c["band"] = band
    for n in (64, 32):
        cos, sin = rope_table(n)
        c[f"cos{n}"] = cos.reshape(2, P, n).transpose(1, 0, 2)
        c[f"sin{n}"] = sin.reshape(2, P, n).transpose(1, 0, 2)
    c["iota"] = np.tile(np.arange(P), (P, 1))
    c["before"] = t[:, None] < t[None, :]
    e = np.arange(8)
    c["earlier"] = np.tile((e[None, :] < e[:, None]).reshape(1, 64), (P, 1))
    return np.concatenate([np.asarray(c[n], np.float32).reshape(P, -1) for n, _ in CONST_PARTS], 1)


def shared_semaphores():
    table = {}

    def kind(shared, *stages):
        at = 0
        for name, n in stages:
            table[name] = (shared, at)
            at += n

    turns = (("en0", 4), ("eoutc", 4), ("en2", 4), ("on0", 4), ("ooutc", 2), ("on2", 2))
    kind("turned", *((t + "_tr", 2 * n) for t, n in turns))
    for e in ("_evA", "_evD"):
        kind("turned" + e, *((t + e, n) for t, n in turns))
    for e in ("_ss", "_xn"):
        kind("norm" + e, *((t + e, n) for t, n in turns if not t.endswith("c")))
    for e in ("_s", "_m", "_exp", "_t", "_pt", "_pv", "_o"):
        kind("att" + e, ("sw" + e, 32), ("ml" + e, 16), ("df" + e, 8))
    gates = (("e1", 4), ("e3", 4), ("o1", 2), ("o3", 2))
    kind("gate_diag", *((t + "_diag", 1) for t, _ in gates))
    for e in ("_gr", "_gev"):
        kind("gate" + e, *((t + e, n) for t, n in gates))
    kind("row_squares", ("e1_sq", 8), ("e3_sq", 8), ("o1_sq", 4), ("o3_sq", 2))
    groups = (("erow", 12), ("swtr", 10), ("orow", 16), ("uq", 4), ("ukv", 8), ("mtr", 16), ("dtr", 16))
    kind("rows_made", *((t if t.endswith("tr") else t + "_made", n) for t, n in groups))
    for e in "AD":
        kind("rows_ev" + e, *((t + "_ev" + e, n // 2) for t, n in groups))
    kind("mod_cols", ("emod_cols", 12), ("omod_cols", 12))
    kind("out_made", ("eout_made", 8), ("oout_made", 4))
    return table


SHARED = shared_semaphores()


class Tally:

    def __init__(self, sem):
        self.sem, self.n = sem, 0

    def add(self, ins, k=1):
        ins.then_inc(self.sem, k)
        self.n += k


def hybrid_trunk(nc, a, out):
    ctx = ExitStack()
    with ctx:
        def sb(name, shape):
            return ctx.enter_context(nc.sbuf_tensor(name, shape, F32))

        sems = {}

        def S(name):
            name = SHARED.get(name, (name, 0))[0]
            if name not in sems:
                sems[name] = ctx.enter_context(nc.semaphore(name))
            return sems[name]

        def nth(name, n):
            return S(name), SHARED.get(name, (name, 0))[1] + n

        const = sb("const", [P, N_CONST])
        xr = sb("xr", [P, TILES, D])
        SLOT = 4096
        RING = 4
        A = RING * SLOT
        BZ = A + 11392
        mem = sb("mem", [P, BZ + 14592])
        ps = ctx.enter_context(nc.psum_tensor("ps", [P, 8, 512], F32))

        def M(at, *dims):
            n = int(np.prod(dims))
            v = mem[:, at:at + n]
            if len(dims) == 1:
                return v
            names = "abcd"[:len(dims)]
            return v.rearrange("p (%s) -> p %s" % (" ".join(names), " ".join(names)),
                               **{names[i]: dims[i] for i in range(len(dims))})

        def C(name):
            at, n = CONST_AT[name]
            return const[:, at:at + n]

        ident, ones = C("ident"), C("ones")
        levels = C("levels").rearrange("p (d l j) -> p d l j", d=2, l=6)
        band = C("band").rearrange("p (q k) -> p q k", q=2)
        cos64, sin64, cos32, sin32 = (C(n).rearrange("p (t d) -> p t d", t=2) for n in ("cos64", "sin64", "cos32", "sin32"))

        slot = [M(i * SLOT, SLOT) for i in range(7)]
        rows1 = sb("rows1", [P, P])
        rows2 = sb("rows2", [P, P])
        rows3 = sb("rows3", [5, P])
        cols1, cols2, cols3 = sb("cols1", [P, P]), sb("cols2", [P, 124]), sb("cols3", [P, 5])
        bc = sb("bc", [P, 488])
        scol = sb("scol", [P, 2, KB])
        modc = sb("modc", [P, 48, 2])
        scaleA = sb("scaleA", [P, KB, 2])
        gatec = sb("gatec", [P, KB, 2])
        st = sb("st", [P, 64])
        alog, dtb, gdnw, sink, subln, lamv = (bc[:, 0:16], bc[:, 16:32], bc[:, 32:96], bc[:, 96:104], bc[:, 104:232], bc[:, 232:488])

        qkvrow = M(A, TILES, EVEN_T)
        rowbuf = M(A + 6144, TILES, EVEN_R)
        aT = M(BZ, KB, SEQ)
        Gb = M(BZ + 4096, 2, D)
        tmp = M(BZ + 6144, 2, D)
        qkvT = M(BZ + 8192, 12, 2, 260)

        stream = []

        def take(parts, freed_by, count, borrowed=None):
            stream.append((parts, freed_by, count, borrowed))
            return len(stream) - 1

        def kview(w, c0, c1):
            return w.rearrange("(k p) n -> p k n", p=P)[:, :, c0:c1]

        def sv(i, k, n, at=0):
            return slot[i % RING][:, at:at + k * n].rearrange("p (k n) -> p k n", k=k)

        def simple(w, c0, c1, sem, count, borrowed=None):
            i = len(stream)
            k = w.shape[0] // P
            return take([(sv(i, k, c1 - c0), kview(w, c0, c1))], sem, count, borrowed)

        e_mod = [simple(a["e_mod_w"][0], 512 * n, 512 * n + 512, "emod_cols", n + 1) for n in range(12)]
        w_in = a["e_w_in"][0]
        e_qkv = [simple(w_in, 512 * n, 512 * n + 512, "qkvT_made", 4 * n + 4) for n in range(3)]
        R_CH = [(0, 512), (512, 1024), (1024, 1312)]
        e_row = [simple(w_in, EVEN_T + c0, EVEN_T + c1, "erow_made", 4 * n + 4) for n, (c0, c1) in enumerate(R_CH)]
        e_out = [simple(a["e_w_out"][0], 512 * n, 512 * n + 512, "eout_made", 4 * n + 4) for n in range(2)]
        e_gu = []
        for n in range(11):
            i = len(stream)
            e_gu.append(take([(sv(i, 8, 256), kview(a["e_ffn_gate"][0], 256 * n, 256 * n + 256)),
                              (sv(i, 8, 256, 2048), kview(a["e_ffn_up"][0], 256 * n, 256 * n + 256))],
                             "gu_made", 2 * n + 2, "gdn" if n < 2 else None))
        DOWN = [(0, 8), (8, 16), (16, 22)]
        e_down = []
        for half in range(2):
            for n, (k0, k1) in enumerate(DOWN):
                i = len(stream)
                e_down.append(take([(sv(i, k1 - k0, 512), a["e_ffn_down"][0][k0 * P:k1 * P, :].rearrange(
                    "(k p) n -> p k n", p=P)[:, :, 512 * half:512 * half + 512])], "down_step", 3 * half + n + 1))
        o_mod = [simple(a["o_mod_w"][0], 512 * n, 512 * n + 512, "omod_cols", n + 1) for n in range(12)]
        ow = a["o_w_in"][0]
        O_CH = [(0, 384), (384, 672), (672, 1184), (1184, 1696), (1696, 2208)]
        O_LAT = [True, False, True, False, False]
        o_in, made = [], 0
        for n, (c0, c1) in enumerate(O_CH):
            made += 2 if O_LAT[n] else 4
            o_in.append(simple(ow, c0, c1, "orow_made", made))
        o_uq = simple(a["o_w_uq"][0], 0, 768, "uq_made", 4)
        o_ukv = simple(a["o_w_ukv"][0], 0, 1024, "ukv_made", 8)
        o_out = [simple(a["o_w_out"][0], 512 * n, 512 * n + 512, "oout_made", 2 * n + 2) for n in range(2)]
        N_STREAM = len(stream)

        landed_at, per_slot = [], [0] * RING
        for i, (parts, *_r) in enumerate(stream):
            per_slot[i % RING] += 16 * len(parts)
            landed_at.append(per_slot[i % RING])

        def arrived(pe, i):
            pe.wait_ge(*nth(f"landed{i % RING}", landed_at[i]))

        block = ctx.enter_context(nc.Block())

        PHASES = ["emod", "eproj", "gprep", "seg0", "seg1", "gdn", "swprep", "sw", "ecat", "eout", "egu", "edown", "omod", "oproj",
                  "lowr", "up", "mprep", "ml", "dprep", "df", "ocat", "omix", "route"]

        def phase_ended(eng, name):
            eng.wait_ge(*nth("phase_over", 3 * (PHASES.index(name) + 1)))

        def phase_over(eng, name):
            eng.drain().then_inc(S("phase_over"), 1)
            phase_ended(eng, name)

        FCH = 512
        NCHUNK = F_EXP // FCH
        MO = BZ + 1024
        xn_l = M(MO, 2, D)
        fT = M(MO + 2048, KB, 256)
        xsT = M(MO + 4096, KB, P)
        hrow = M(MO + 5120, 2, FCH)
        hT = M(MO + 6144, 2, 4, P)
        ysb = M(MO + 7168, D)
        moe = M(MO + 8192, 2, D)
        pick = M(MO + 10240, 2, P)
        pickw = M(MO + 10496, 2, P)
        pickT = M(MO + 10752, 2, P)
        mtmp = M(MO + 11008, D)
        moe_slots = 3 * NCHUNK
        MRING = 7
        logit, rank = (sb(n, [P, 2, EXPERTS]) for n in ("logit", "rank"))
        sel16, gate16, posn16 = (sb(n, [P, 2, 2 * EXPERTS]) for n in ("sel", "gate", "posn"))
        sel, gate, posn = (b[:, :, 0:EXPERTS] for b in (sel16, gate16, posn16))
        pair = sb("pair", [P, 2, 64])
        router = sb("router", [P, KB, EXPERTS])

        ORDER = [("g", 0), ("u", 0)]
        for c in range(1, NCHUNK):
            ORDER += [("g", c), ("u", c), ("d", c - 1)]
        ORDER += [("d", NCHUNK - 1)]
        SLOT_OF = {k: n for n, k in enumerate(ORDER)}

        MAX_PASSES = EXPERTS + 2 * SEQ // (P + 1)
        plan = sb("plan", [1, 32])
        plan_i = ctx.enter_context(nc.sbuf_tensor("plan_i", [1, 32], I32))

        def passes(eng):
            eng.wait_ge(*nth("plan_ready", 1))
            return eng.value_load(plan_i[0:1, 15:16], min_val=EXPERTS, max_val=MAX_PASSES)

        def moe_sync(sp):
            wg, wu, wd = (a[n][0] for n in ("o_exp_gate", "o_exp_up", "o_exp_down"))
            wg, wu, wd = (w.rearrange("e d f -> (e d) f") for w in (wg, wu, wd))

            def weights(it, e):
                for n, (kind, c) in enumerate(ORDER):
                    sp.wait_ge(*nth("moe_read", it * len(ORDER) + (n + 1)))
                    dst = slot[n % MRING]
                    if kind == "d":
                        src = wd[bass.ds(e * F_EXP + c * FCH, FCH), :].rearrange("(k p) n -> p k n", p=P)
                        dst = dst.rearrange("p (k n) -> p k n", k=4)
                    else:
                        w = wg if kind == "g" else wu
                        src = w[bass.ds(e * D, D), c * FCH:c * FCH + FCH].rearrange("(k p) n -> p k n", p=P)
                        dst = dst.rearrange("p (k n) -> p k n", k=8)
                    sp.dma_start(dst, src).then_inc(S(f"mlanded{n % MRING}"), 16)

            weights(0, 0)
            n_passes = passes(sp)
            with sp.Fori(1, n_passes) as it:
                weights(it, sp.value_load(plan_i[0:1, bass.ds(it, 1)], min_val=0, max_val=EXPERTS - 1))

        @block.sync
        def _(sp):
            sp.dma_start(const[:], a["consts"]).then_inc(S("const_in"), 16)
            sp.dma_start(rows1[0:8, :], a["c"].rearrange("a (k p) -> (a k) p", p=P)).then_inc(S("small_in"), 16)
            sp.dma_start(rows1[8:16, :], a["c_ctx"].rearrange("(k p) -> k p", p=P)).then_inc(S("small_in"), 16)
            sp.dma_start(rows1[16:64, :], a["e_mod_b"].rearrange("a (k p) -> (a k) p", p=P)).then_inc(S("small_in"), 16)
            sp.dma_start(rows1[64:112, :], a["o_mod_b"].rearrange("a (k p) -> (a k) p", p=P)).then_inc(S("small_in"), 16)
            sp.dma_start(rows2[0:32, :], a["e_norms"].rearrange("a m (k p) -> (a m k) p", p=P)).then_inc(S("small_in"), 16)
            sp.dma_start(rows2[32:64, :], a["o_norms"].rearrange("a m (k p) -> (a m k) p", p=P)).then_inc(S("small_in"), 16)
            sp.dma_start(rows2[64:124, :], a["e_conv_w"].rearrange("a m (k p) -> (a m k) p", p=P)).then_inc(S("small_in"), 16)
            sp.dma_start(rows3[0:3, :], a["o_q_norm"].rearrange("a (k p) -> (a k) p", p=P)).then_inc(S("small_in"), 16)
            sp.dma_start(rows3[3:5, :], a["o_kv_norm"].rearrange("a (k p) -> (a k) p", p=P)).then_inc(S("small_in"), 16)
            at = 0
            for name, n in (("e_a_log", 16), ("e_dt_bias", 16), ("e_gdn_norm", 64), ("e_sink", 8), ("o_subln", 128), ("o_lambda", 256)):
                src = a[name].rearrange("a b c -> (a b c)") if len(a[name].shape) == 3 else a[name].rearrange("a b -> (a b)")
                sp.dma_start(bc[:, at:at + n], src.partition_broadcast(P)).then_inc(S("small_in"), 16)
                at += n
            sp.dma_start(router[:], a["o_router"][0].rearrange("(k p) e -> p k e", p=P)).then_inc(S("small_in"), 16)
            sp.dma_start(xr[:, 0:2, :], a["ctx"][0].rearrange("(t p) d -> p t d", p=P)).then_inc(S("x_in"), 16)
            sp.dma_start(xr[:, 2:4, :], a["x"][0].rearrange("(t p) d -> p t d", p=P)).then_inc(S("x_in"), 16)
            for i, (parts, _f, _c, borrowed) in enumerate(stream):
                if i >= RING:
                    _p, sem_name, count, _b = stream[i - RING]
                    sp.wait_ge(*nth(sem_name, count))
                if borrowed:
                    phase_ended(sp, borrowed)
                for dst, src in parts:
                    sp.dma_start(dst, src).then_inc(S(f"landed{i % RING}"), 16)
            phase_ended(sp, "omix")
            moe_sync(sp)
            sp.wait_ge(*nth("result", 2))
            sp.dma_start(out[0].rearrange("(t p) d -> p t d", p=P), xr[:, 2:4, :]).then_inc(S("stored"), 16)
            sp.wait_ge(*nth("stored", 16))

        def bch(x, n):
            return x.unsqueeze(2).to_broadcast([x.shape[0], x.shape[1], n])

        def bcm(x, m):
            return x.unsqueeze(1).to_broadcast([x.shape[0], m, x.shape[1]])

        def hv(x, m=HEADS):
            return x.rearrange("p (h d) -> p h d", h=m)

        cond_of = lambda t: 0 if t >= LAT else 1
        ALL, LATS = list(range(TILES)), [2, 3]
        SQRT_D = float(np.sqrt(D))
        gx, gg, gbeta, gl_, ge_ = (sb(n, [P, TILES, 16]) for n in ("gx", "gg", "gbeta", "gl_", "ge_"))
        ea = sb("ea", [P, 16])
        gst = sb("gst", [P, TILES, 16])
        eall = sb("eall", [P, 96])
        bg = sb("bg", [P, 2, 16])
        Lb, Xb, Yb, Cb = (M(n * 1024, 2, 512) for n in range(4))
        kTt, qTt = M(4096, HEADS, P), M(5120, HEADS, P)
        AT = M(6144, 2, 2, 512)
        kbgT, qgT = M(BZ, 2, HEADS, P), M(BZ + 2048, 2, HEADS, P)
        kt = M(BZ + 4096, 2, 2, 512)
        vbst = M(BZ + 6144, 4, 512)
        XT = M(BZ + 8192, 2, 2, 512)
        ostep = M(BZ + 10240, 4, 512)
        kbgrow, qgrow = M(BZ + 10240, HEADS, 2, HD), M(BZ + 11264, HEADS, 2, HD)
        Sst, rr, vn, ox = (M(BZ + 12288 + 512 * n, 512) for n in range(4))
        rhsb = [Cb[:, 0], Cb[:, 1], Yb[:, 0], Yb[:, 1]]
        swq, swk = M(BZ, HEADS, SEQ), M(BZ + 4096, 2, SEQ)
        prob, probT = M(BZ + 5120, 2, 512), M(BZ + 6144, 2, 512)
        rt1, rt2 = M(BZ + 7168, 640), M(BZ + 7808, 640)
        rt3, rt4 = M(BZ + 4096, 512), M(BZ + 4608, 512)
        hTd = M(A, 22, SEQ)
        sil = M(BZ + 8192, 2, 512)
        cq, ckvkr = M(A, 2, 384), M(A + 768, TILES, 288)
        dq, dk, dv = M(A + 1920, 2, 512), M(A + 2944, TILES, 512), M(A + 4992, TILES, 512)
        cqT, ckvT, rowq = M(A + 7040, 3, 256), M(A + 7808, 2, SEQ), M(A + 8832, 2, 768)
        cat1 = M(A + 7040, 2, D)
        rowkv = M(BZ + 8192, TILES, D)
        k96, kT1, qT1 = M(BZ + 4096, TILES, HEADS, 96), M(BZ, HEADS, SEQ), M(BZ + 12288, HEADS, 256)
        prob1, probT1 = M(BZ + 4096, 4, 512), M(BZ + 6144, 2, 512)
        lam = sb("lam", [P, 4])

        erow_dst = [rowbuf[:, t, c0:c1] for c0, c1 in R_CH for t in ALL]
        sw_dst = [swq[0:HD, h, :] for h in range(8)] + [swk[0:HD, h, :] for h in range(2)]
        orow_dst = ([cq[:, t, :] for t in range(2)] + [ckvkr[:, t, :] for t in ALL] + [dq[:, t, :] for t in range(2)]
                    + [dk[:, t, :] for t in ALL] + [dv[:, t, :] for t in ALL])
        uq_dst = [rowq[:, t, 384 * c:384 * c + 384] for t in range(2) for c in range(2)]
        ukv_dst = [rowkv[:, t, 512 * c:512 * c + 512] for t in ALL for c in range(2)]
        mtr_dst = [kT1[0:96, h, :] for h in range(8)] + [qT1[0:96, h, :] for h in range(8)]
        dtr_dst = [kT1[0:HD, h, :] for h in range(8)] + [qT1[0:HD, h, :] for h in range(8)]
        msil = M(MO + 12032, 2, FCH)
        plan_w = sb("plan_w", [1, 24])
        by_pair = sb("by_pair", [1, 64])[:].rearrange("p (e j) -> p e j", e=8)
        nsink = sb("nsink", [P, HEADS])
        sw_jobs = []
        for t in ALL:
            for h in range(HEADS):
                nk = 256 if t < LAT else 512
                g = h // 4
                sw_jobs.append(dict(q=swq[0:HD, h, t * P:t * P + P], k=swk[0:HD, g, 0:nk], nk=nk, vw=HD,
                                    v=[rowbuf[:, b, 1184 + g * HD:1184 + g * HD + HD] for b in range(nk // P)],
                                    scale=HD ** -0.5, mask=band[:, t - LAT, :] if t >= LAT else None,
                                    sink=sink[:, h:h + 1], nsink=nsink[:, h:h + 1], out=qkvrow[:, t, 512 + h * HD:512 + h * HD + HD]))
        ml_jobs = []
        for t in range(2):
            for h in range(HEADS):
                ml_jobs.append(dict(q=qT1[0:96, h, t * P:t * P + P], k=kT1[0:96, h, :], nk=512, vw=HD,
                                    v=[rowkv[:, b, h * P + HD:h * P + P] for b in range(4)],
                                    scale=96 ** -0.5, mask=None, sink=None, out=cat1[:, t, h * HD:h * HD + HD]))

        rs = sb("rs", [P, 3, 64])

        @block.tensor
        def _(pe):
            def turn(bank, j, src, dst_p=P, cols=P):
                k = src.shape[0]
                return pe.transpose(ps[0:dst_p, bank, j * P:j * P + cols], src, ident[0:k, 0:k])

            def norm_T(tag, tiles, buf=tmp):
                for n in range(len(tiles)):
                    pe.wait_ge(*nth(tag + "_xn", n + 1))
                    for half in range(2):
                        if n >= 2:
                            pe.wait_ge(*nth(tag + ("_evA", "_evD")[half], n - 1))
                        for j in range(4):
                            ins = turn(2 * (n % 2) + half, j, buf[:, n % 2, (4 * half + j) * P:(4 * half + j + 1) * P])
                        ins.then_inc(S(tag + "_tr"), 1)

            def cat_T(tag, src, tiles):
                for n, t in enumerate(tiles):
                    for half in range(2):
                        if n >= 2:
                            pe.wait_ge(*nth(tag + ("_evA", "_evD")[half], n - 1))
                        for j in range(4):
                            ins = turn(2 * (n % 2) + half, j, src(t)[:, (4 * half + j) * P:(4 * half + j + 1) * P])
                        ins.then_inc(S(tag + "_tr"), 1)

            def mod_cols(tag, slots):
                for n, i in enumerate(slots):
                    arrived(pe, i)
                    w = sv(i, 8, 512)
                    for b in range(4):
                        for k in range(KB):
                            ins = pe.matmul(ps[:, 0, (4 * n + b) * 2:(4 * n + b) * 2 + 2], w[:, k, b * P:b * P + P],
                                            scol[:, :, k], start=(k == 0), stop=(k == KB - 1))
                    ins.then_inc(S(tag + "_cols"), 1)

            def gate_rows(tag, conds):
                pe.wait_ge(*nth(tag + "_diag", 1))
                for n in range(2 * conds):
                    pe.matmul(ps[:, n, :], ones, tmp.rearrange("p a d -> p (a d)")[:, 512 * n:512 * n + 512],
                              start=True, stop=True).then_inc(S(tag + "_gr"), 1)

            def rows(made, ev, jobs, banks=4):
                for g, (i, lhs, rhs, width) in enumerate(jobs):
                    if i is not None:
                        arrived(pe, i)
                    if g >= banks:
                        pe.wait_ge(*nth(ev + "AD"[g % 2], (g - banks) // 2 + 1))
                    for k, (l, r) in enumerate(zip(lhs, rhs)):
                        ins = pe.matmul(ps[:, g % banks, 0:width], l, r, start=(k == 0), stop=(k == len(lhs) - 1))
                    ins.then_inc(S(made), 1)

            pe.wait_ge(*nth("const_in", 16))
            pe.wait_ge(*nth("small_in", 16 * 16))
            turn(0, 0, rows1[0:112, :], P, 112)
            turn(0, 1, rows2[0:124, :], P, 124)
            turn(0, 2, rows3[0:5, :], P, 5).then_inc(S("cols_tr"), 1)
            pe.wait_ge(*nth("silu_c", 1))
            mod_cols("emod", e_mod)
            phase_over(pe, "emod")
            norm_T("en0", ALL)
            pe.wait_ge(*nth("en0_evA", 4))
            pe.wait_ge(*nth("en0_evD", 4))

            def conv_turn(b):
                pe.wait_ge(*nth("conv_silu", b + 1))
                if b >= 2:
                    pe.wait_ge(*nth("conv_ev", b - 1))
                for t in ALL:
                    ins = turn(4 + b % 2, t, sil_c[:, b % 2, t * P:t * P + P])
                ins.then_inc(S("conv_tr"), 1)

            sil_c = tmp[:, :, 0:512]
            for b in range(12):
                arrived(pe, e_qkv[b // 4])
                w = sv(e_qkv[b // 4], 8, 512)
                if b >= 4:
                    pe.wait_ge(*nth("qkvT_ev", b - 3))
                for k in range(KB):
                    ins = pe.matmul(ps[:, b % 4, :], w[:, k, (b % 4) * P:(b % 4 + 1) * P], aT[:, k, :],
                                    start=(k == 0), stop=(k == KB - 1))
                ins.then_inc(S("qkvT_made"), 1)
                if b >= 2:
                    conv_turn(b - 2)
            conv_turn(10)
            conv_turn(11)
            pe.wait_ge(*nth("qkvT_ev", 12))
            jobs = []
            for n, (c0, c1) in enumerate(R_CH):
                w = sv(e_row[n], 8, c1 - c0)
                jobs += [(e_row[n], [aT[:, k, t * P:t * P + P] for k in range(KB)], [w[:, k, :] for k in range(KB)], c1 - c0)
                         for t in ALL]
            rows("erow_made", "erow_ev", jobs)
            phase_over(pe, "eproj")

            phase_over(pe, "gprep")
            lhs_cum = (C("le"), C("ge"))
            lhs_tail = (C("gt"), C("lt"))
            chunk_of = C("chunk_of").rearrange("p (c j) -> p c j", c=2)
            eye_c = C("eye_c")
            for seg in range(2):
                for tl in range(2):
                    t = 2 * seg + tl
                    for d in range(2):
                        g = gg[:, t, d * 8:d * 8 + 8]
                        pe.matmul(ps[:, 7, tl * 32 + d * 8:tl * 32 + d * 8 + 8], lhs_cum[d], g, start=True, stop=True)
                        pe.matmul(ps[:, 7, tl * 32 + 16 + d * 8:tl * 32 + 24 + d * 8], lhs_tail[d], g, start=True, stop=True)
                        for c in range(2):
                            s = 2 * tl + c if d == 0 else 3 - (2 * tl + c)
                            ins = pe.matmul(ps[d * 64:d * 64 + 64, 7, 64 + 8 * s:72 + 8 * s], chunk_of[:, c, :], g,
                                            start=True, stop=True)
                ins.then_inc(S("gh_mm"), 1)
                for tl in range(2):
                    t = 2 * seg + tl
                    q_ = qkvrow[:, t, 0:512]
                    k_ = qkvrow[:, t, 512:1024]
                    if tl == 1:
                        pe.wait_ge(*nth("inv_x", 12 * t))
                    for b in range(8):
                        if b == 4:
                            pe.wait_ge(*nth("row_ready", 2 * t + 1))
                        if b == 6:
                            pe.wait_ge(*nth("row_ready", 2 * t + 2))
                        for j in range(4):
                            h = 4 * (b % 2) + j
                            if b < 4:
                                src = (k_, q_)[b // 2][:, h * HD:h * HD + HD]
                                ins = turn(b, j, src, HD)
                            else:
                                src = (kbgrow, qgrow)[(b - 4) // 2][:, h].rearrange("p d k -> p (d k)")
                                ins = turn(b, j, src)
                        ins.then_inc(S("tr_done"), 1)
                    pe.wait_ge(*nth("tr_evA", 4 * t + 2))
                    pe.wait_ge(*nth("tr_evD", 4 * t + 2))
                    for kind in range(2):
                        for h in range(HEADS):
                            for c in range(2):
                                cs = slice(c * CH, c * CH + CH)
                                ins = pe.matmul(ps[cs, kind, h * CH:h * CH + CH], kTt[0:64, h, cs],
                                                (kTt, qTt)[kind][0:64, h, cs], start=True, stop=True)
                        ins.then_inc(S("gram_done"), 1)
                    pe.wait_ge(*nth("tr_evA", 4 * t + 4))
                    pe.wait_ge(*nth("tr_evD", 4 * t + 4))
                    for n in range(4):
                        d = n % 2
                        pe.wait_ge(*nth("rhs_ready", 4 * t + n + 1))
                        pe.matmul(ps[:, 2 + n, :], (lhs_cum[d], lhs_tail[d])[n // 2], rhsb[n], start=True, stop=True)\
                          .then_inc(S("dec_done"), 1)
                    for lv in range(6):
                        for d in range(2):
                            pe.wait_ge(*nth("inv_c", 12 * t + 2 * lv + d + 1))
                            if lv > 0:
                                pe.wait_ge(*nth("inv_x", 12 * t + 2 * (lv - 1) + d + 1))
                            for h in range(HEADS):
                                for c in range(2):
                                    cs, hs = slice(c * CH, c * CH + CH), slice(h * CH, h * CH + CH)
                                    rhs = eye_c[cs, :] if lv == 0 else XT[cs, tl, d, hs]
                                    ins = pe.matmul(ps[cs, d, hs], Cb[cs, d, hs], rhs, start=True, stop=True)
                            ins.then_inc(S("inv_y"), 1)
                        if lv == 0:
                            continue
                        for d in range(2):
                            pe.wait_ge(*nth("inv_ye", 10 * t + 2 * (lv - 1) + d + 1))
                            for which in range(2):
                                if which == 0 and lv == 5:
                                    continue
                                for h in range(HEADS):
                                    for c in range(2):
                                        cs, hs = slice(c * CH, c * CH + CH), slice(h * CH, h * CH + CH)
                                        if which == 0:
                                            ins = pe.matmul(ps[cs, 2 + d, hs], Yb[cs, d, hs], Xb[cs, d, hs], start=True, stop=True)
                                        else:
                                            ins = pe.matmul(ps[cs, 4 + d, hs], Xb[cs, d, hs], Yb[cs, d, hs], start=True, stop=True)
                            ins.then_inc(S("inv_z"), 1)
                pe.wait_ge(*nth("inv_x", 12 * (2 * seg + 2)))
                for n in range(4):
                    N = 4 * seg + n
                    where = []
                    for d in range(2):
                        s = n if d == 0 else 3 - n
                        where.append((s // 2, slice((s % 2) * CH, (s % 2) * CH + CH), slice(d * 64, d * 64 + 64)))

                    def each(bank, lhs, rhs, by_chunk_out):
                        for d in range(2):
                            tl, cs, ds_ = where[d]
                            for h in range(HEADS):
                                hs = slice(h * CH, h * CH + CH)
                                o = ps[cs if by_chunk_out else ds_, bank, hs]
                                ins = pe.matmul(o, lhs(d, tl, cs, ds_, h, hs), rhs(d, cs, ds_, hs), start=True, stop=True)
                        return ins

                    pe.wait_ge(*nth("sc_s", N + 1))
                    each(0, lambda d, tl, cs, ds_, h, hs: kbgT[ds_, tl, h, cs], lambda d, cs, ds_, hs: Sst[ds_, hs], True)\
                        .then_inc(S("sc_p"), 1)
                    pe.wait_ge(*nth("sc_ox", N)) if N else None
                    each(1, lambda d, tl, cs, ds_, h, hs: qgT[ds_, tl, h, cs], lambda d, cs, ds_, hs: Sst[ds_, hs], True)\
                        .then_inc(S("sc_o1"), 1)
                    pe.wait_ge(*nth("sc_r", N + 1))
                    each(2, lambda d, tl, cs, ds_, h, hs: XT[cs, tl, d, hs], lambda d, cs, ds_, hs: rr[cs, hs], True)\
                        .then_inc(S("sc_v"), 1)
                    pe.wait_ge(*nth("sc_vn", N + 1))
                    each(4, lambda d, tl, cs, ds_, h, hs: kt[cs, tl, d, hs], lambda d, cs, ds_, hs: vn[cs, hs], False)\
                        .then_inc(S("sc_u"), 1)
                    pe.wait_ge(*nth("sc_ost", N)) if N else None
                    each(3, lambda d, tl, cs, ds_, h, hs: AT[cs, tl, d, hs], lambda d, cs, ds_, hs: vn[cs, hs], True)\
                        .then_inc(S("sc_o2"), 1)
                phase_over(pe, f"seg{seg}")
            phase_over(pe, "gdn")

            def attention(tag, jobs):
                J = len(jobs)

                def scores(n):
                    if n >= 2:
                        pe.wait_ge(*nth(tag + "_exp", n - 1))
                    j = jobs[n]
                    pe.matmul(ps[:, n % 2, 0:j["nk"]], j["q"], j["k"], start=True, stop=True).then_inc(S(tag + "_s"), 1)

                scores(0)
                for n in range(J):
                    if n + 1 < J:
                        scores(n + 1)
                    j = jobs[n]
                    nb = j["nk"] // P
                    pe.wait_ge(*nth(tag + "_exp", n + 1))
                    if n >= 2:
                        pe.wait_ge(*nth(tag + "_pt", n - 1))
                    for b in range(nb):
                        ins = turn(2 + n % 2, b, prob[:, n % 2, b * P:b * P + P])
                    ins.then_inc(S(tag + "_t"), 1)
                    pe.wait_ge(*nth(tag + "_pt", n + 1))
                    if n >= 2:
                        pe.wait_ge(*nth(tag + "_o", n - 1))
                    for b in range(nb):
                        ins = pe.matmul(ps[:, 4 + n % 2, 0:j["vw"]], probT[:, n % 2, b * P:b * P + P], j["v"][b],
                                        start=(b == 0), stop=(b == nb - 1))
                    ins.then_inc(S(tag + "_pv"), 1)

            pe.wait_ge(*nth("swrope", 1))
            for h in range(10):
                if h >= 4:
                    pe.wait_ge(*nth("swtr_ev" + "AD"[h % 2], (h - 4) // 2 + 1))
                for t in ALL:
                    ins = turn(h % 4, t, rowbuf[:, t, 544 + h * HD:544 + h * HD + HD], HD)
                ins.then_inc(S("swtr"), 1)
            phase_over(pe, "swprep")
            attention("sw", sw_jobs)
            phase_over(pe, "sw")

            def out_proj(tag, slots, tiles, nt):
                pe.wait_ge(*nth(tag + "c_evA", nt))
                pe.wait_ge(*nth(tag + "c_evD", nt))
                for n, i in enumerate(slots):
                    arrived(pe, i)
                    w = sv(i, 8, 512)
                    for t in range(nt):
                        for k in range(KB):
                            ins = pe.matmul(ps[:, 4 * n + t, :], aT[:, k, tiles[t] * P:tiles[t] * P + P], w[:, k, :],
                                            start=(k == 0), stop=(k == KB - 1))
                        ins.then_inc(S(tag + "_made"), 1)

            cat_T("eoutc", lambda t: qkvrow[:, t, 0:1024], ALL)
            pe.wait_ge(*nth("eoutc_evA", 4))
            pe.wait_ge(*nth("eoutc_evD", 4))
            gate_rows("e1", 2)
            phase_over(pe, "ecat")
            out_proj("eout", e_out, ALL, 4)
            phase_over(pe, "eout")
            norm_T("en2", ALL)
            pe.wait_ge(*nth("en2_evA", 4))
            pe.wait_ge(*nth("en2_evD", 4))
            for b in range(22):
                i = e_gu[b // 2]
                arrived(pe, i)
                if b >= 2:
                    pe.wait_ge(*nth("gu_h", b - 1))
                for w in range(2):
                    wv = sv(i, 8, 256, 2048 * w)
                    for k in range(KB):
                        ins = pe.matmul(ps[:, 4 * w + b % 2, :], wv[:, k, (b % 2) * P:(b % 2 + 1) * P], aT[:, k, :],
                                        start=(k == 0), stop=(k == KB - 1))
                ins.then_inc(S("gu_made"), 1)
            gate_rows("e3", 2)
            phase_over(pe, "egu")
            for half in range(2):
                for n, (k0, k1) in enumerate(DOWN):
                    i = e_down[3 * half + n]
                    arrived(pe, i)
                    w = sv(i, k1 - k0, 512)
                    for k in range(k0, k1):
                        for t in ALL:
                            ins = pe.matmul(ps[:, 4 * half + t, :], hTd[:, k, t * P:t * P + P], w[:, k - k0, :],
                                            start=(k == 0), stop=(k == 21))
                    ins.then_inc(S("down_step"), 1)
            phase_over(pe, "edown")
            mod_cols("omod", o_mod)
            phase_over(pe, "omod")
            norm_T("on0", ALL)
            pe.wait_ge(*nth("on0_evA", 4))
            pe.wait_ge(*nth("on0_evD", 4))
            jobs = []
            for n, (c0, c1) in enumerate(O_CH):
                w = sv(o_in[n], 8, c1 - c0)
                jobs += [(o_in[n], [aT[:, k, t * P:t * P + P] for k in range(KB)], [w[:, k, :] for k in range(KB)], c1 - c0)
                         for t in (LATS if O_LAT[n] else ALL)]
            rows("orow_made", "orow_ev", jobs)
            phase_over(pe, "oproj")
            pe.wait_ge(*nth("lowrank", 1))
            for j in range(3):
                for t in range(2):
                    ins = turn(j, t, cq[:, t, j * P:j * P + P])
            ins.then_inc(S("lr_tr"), 1)
            for j in range(2):
                for t in ALL:
                    ins = turn(3 + j, t, ckvkr[:, t, j * P:j * P + P])
            ins.then_inc(S("lr_tr"), 1)
            phase_over(pe, "lowr")
            w = sv(o_uq, 3, 768)
            rows("uq_made", "uq_ev", [(o_uq, [cqT[:, k, t * P:t * P + P] for k in range(3)],
                                       [w[:, k, 384 * c:384 * c + 384] for k in range(3)], 384) for t in range(2) for c in range(2)])
            pe.wait_ge(*nth("uq_evA", 2))
            pe.wait_ge(*nth("uq_evD", 2))
            w = sv(o_ukv, 2, 1024)
            rows("ukv_made", "ukv_ev", [(o_ukv, [ckvT[:, k, t * P:t * P + P] for k in range(2)],
                                         [w[:, k, 512 * c:512 * c + 512] for k in range(2)], 512) for t in ALL for c in range(2)])
            phase_over(pe, "up")
            pe.wait_ge(*nth("k96_ready", 1))
            for h in range(16):
                if h >= 4:
                    pe.wait_ge(*nth("mtr_ev" + "AD"[h % 2], (h - 4) // 2 + 1))
                for t in (ALL if h < 8 else (0, 1)):
                    src = k96[:, t, h, :] if h < 8 else rowq[:, t, (h - 8) * 96:(h - 8) * 96 + 96]
                    ins = turn(h % 4, t, src, 96)
                ins.then_inc(S("mtr"), 1)
            phase_over(pe, "mprep")
            attention("ml", ml_jobs)
            phase_over(pe, "ml")
            for h in range(16):
                if h >= 4:
                    pe.wait_ge(*nth("dtr_ev" + "AD"[h % 2], (h - 4) // 2 + 1))
                for t in (ALL if h < 8 else (0, 1)):
                    src = (dk[:, t] if h < 8 else dq[:, t])[:, (h % 8) * HD:(h % 8) * HD + HD]
                    ins = turn(h % 4, t, src, HD)
                ins.then_inc(S("dtr"), 1)
            phase_over(pe, "dprep")

            def dscores(n):
                h, t = n // 2, n % 2
                if n >= 2:
                    pe.wait_ge(*nth("df_exp", n - 1))
                for w in range(2):
                    ins = pe.matmul(ps[:, 2 * (n % 2) + w, :], qT1[0:HD, 2 * h + w, t * P:t * P + P], kT1[0:HD, 2 * h + w, :],
                                    start=True, stop=True)
                ins.then_inc(S("df_s"), 1)

            dscores(0)
            for n in range(8):
                h = n // 2
                if n + 1 < 8:
                    dscores(n + 1)
                pe.wait_ge(*nth("df_a", n + 1))
                if n >= 2:
                    pe.wait_ge(*nth("df_pt", n - 1))
                for b in range(4):
                    ins = turn(4 + n % 2, b, prob1[:, 2 * (n % 2), b * P:b * P + P])
                ins.then_inc(S("df_t"), 1)
                pe.wait_ge(*nth("df_pt", n + 1))
                if n >= 2:
                    pe.wait_ge(*nth("df_o", n - 1))
                for b in range(4):
                    ins = pe.matmul(ps[:, 6 + n % 2, 0:P], probT1[:, n % 2, b * P:b * P + P], dv[:, b, h * P:h * P + P],
                                    start=(b == 0), stop=(b == 3))
                ins.then_inc(S("df_pv"), 1)
            phase_over(pe, "df")
            pe.wait_ge(*nth("subln", 1))
            cat_T("ooutc", lambda t: cat1[:, t - 2, :], LATS)
            pe.wait_ge(*nth("ooutc_evA", 2))
            pe.wait_ge(*nth("ooutc_evD", 2))
            gate_rows("o1", 1)
            phase_over(pe, "ocat")
            out_proj("oout", o_out, LATS, 2)
            pe.drain().then_inc(S("moe_read"), MRING)
            phase_over(pe, "omix")
            norm_T("on2", LATS, xn_l)
            pe.wait_ge(*nth("on2_evA", 2))
            pe.wait_ge(*nth("on2_evD", 2))
            for t in range(2):
                for k in range(KB):
                    ins = pe.matmul(ps[:, 4, t * 8:t * 8 + 8], fT[:, k, t * P:t * P + P], router[:, k, :],
                                    start=(k == 0), stop=(k == KB - 1))
            ins.then_inc(S("logits"), 1)
            pe.wait_ge(*nth("selected", 1))
            pe.matmul(ps[:, 5, 0:8], C("before"), sel[:, 0, :], start=True, stop=True)
            pe.matmul(ps[:, 5, 8:16], ones, sel[:, 0, :], start=True, stop=False)
            pe.matmul(ps[:, 5, 8:16], C("before"), sel[:, 1, :], start=False, stop=True)
            pe.matmul(ps[:, 5, 16:24], ones, sel[:, 0, :], start=True, stop=False)
            pe.matmul(ps[:, 5, 16:24], ones, sel[:, 1, :], start=False, stop=True).then_inc(S("positions"), 1)
            phase_over(pe, "route")
            n_passes = passes(pe)
            with pe.Fori(0, n_passes) as it:
                pe.wait_ge(*nth("m_pick", it + 1))
                for k in range(KB):
                    for t in range(2):
                        ins = pe.matmul(ps[:, k // 4, (k % 4) * P:(k % 4 + 1) * P], xn_l[:, t, k * P:k * P + P], pick[:, t, :],
                                        start=(t == 0), stop=(t == 1))
                ins.then_inc(S("m_gath"), 1)
                for t in range(2):
                    ins = turn(6, t, pickw[:, t, :])
                ins.then_inc(S("m_pt"), 1)
                pe.wait_ge(*nth("m_xsA", it + 1))
                pe.wait_ge(*nth("m_xsD", it + 1))
                for c in range(NCHUNK + 1):
                    if c < NCHUNK:
                        for w in range(2):
                            n = SLOT_OF[("gu"[w], c)]
                            pe.wait_ge(*nth(f"mlanded{n % MRING}", it * 48 + (16 * (n // MRING) + 16)))
                            wv = slot[n % MRING].rearrange("p (k n) -> p k n", k=8)
                            if c >= 2:
                                pe.wait_ge(*nth("m_h", it * NCHUNK + (c - 1)))
                            for k in range(KB):
                                ins = pe.matmul(ps[:, 2 * (c % 2) + w, :], xsT[:, k, :], wv[:, k, :],
                                                start=(k == 0), stop=(k == KB - 1))
                            ins.then_inc(S("moe_read"), 1)
                    if c >= 1:
                        b = (c - 1) % 2
                        pe.wait_ge(*nth("m_h", it * NCHUNK + c))
                        if c >= 2:
                            pe.wait_ge(*nth("m_ht", it * NCHUNK + (c - 1)))
                        for j in range(4):
                            ins = turn(6, j, hrow[:, b, j * P:j * P + P])
                        ins.then_inc(S("m_tr"), 1)
                        n = SLOT_OF[("d", c - 1)]
                        pe.wait_ge(*nth("m_ht", it * NCHUNK + c))
                        pe.wait_ge(*nth(f"mlanded{n % MRING}", it * 48 + (16 * (n // MRING) + 16)))
                        wv = slot[n % MRING].rearrange("p (k n) -> p k n", k=4)
                        for f in range(4):
                            for o in range(2):
                                ins = pe.matmul(ps[:, 4 + o, :], hT[:, b, f, :], wv[:, f, 512 * o:512 * o + 512],
                                                start=(c == 1 and f == 0), stop=(c == NCHUNK and f == 3))
                        ins.then_inc(S("moe_read"), 1)
                pe.wait_ge(*nth("m_y", it + 1))
                for t in range(2):
                    for o in range(2):
                        ins = pe.matmul(ps[:, 2 * t + o, :], pickT[:, t, :], ysb[:, 512 * o:512 * o + 512], start=True, stop=True)
                ins.then_inc(S("m_sc"), 1)
                pe.wait_ge(*nth("m_acc", it + 1))
            gate_rows("o3", 1)

        @block.scalar
        def _(act):
            def copy(dst, src):
                return act.activation(dst, src, ACT.Copy)

            def norm_T(tag, tiles, shift, dst):
                def square(n):
                    if n:
                        act.wait_ge(*nth(tag + "_ss", n))
                    act.activation(ps[:, 6:8, :], xr[:, tiles[n], :].rearrange("p (a b) -> p a b", a=2), ACT.Square,
                                   accum_out=st[:, n:n + 1]).then_inc(S(tag + "_ss"), 1)
                square(0)
                for n, t in enumerate(tiles):
                    if n + 1 < len(tiles):
                        square(n + 1)
                    act.wait_ge(*nth(tag + "_tr", 2 * n + 1))
                    for k in range(4):
                        ins = act.activation(dst(t)[:, k, :], ps[:, 2 * (n % 2), k * P:k * P + P], ACT.Identity,
                                             bias=modc[:, shift + k, cond_of(t):cond_of(t) + 1],
                                             scale=scaleA[:, k, cond_of(t):cond_of(t) + 1])
                    ins.then_inc(S(tag + "_evA"), 1)

            def cat_T(tag, tiles):
                for n, t in enumerate(tiles):
                    act.wait_ge(*nth(tag + "_tr", 2 * n + 1))
                    copy(aT[:, 0:4, t * P:t * P + P], ps[:, 2 * (n % 2), :].rearrange("p (k n) -> p k n", k=4))\
                        .then_inc(S(tag + "_evA"), 1)

            def gate_rows(tag, conds):
                for n in range(2 * conds):
                    act.wait_ge(*nth(tag + "_gr", n + 1))
                    copy(Gb[:, n // 2, 512 * (n % 2):512 * (n % 2) + 512], ps[:, n, :]).then_inc(S(tag + "_gev"), 1)

            def rows(made, ev, dsts, banks=4):
                for g, d in enumerate(dsts):
                    if g % 2 == 0:
                        act.wait_ge(*nth(made, g + 1))
                        copy(d, ps[:, g % banks, 0:d.shape[-1]]).then_inc(S(ev + "A"), 1)

            def squares(tag, ready, nt):
                for half in range(2):
                    for t in range(nt):
                        act.wait_ge(*nth(tag[0], ready(half, t)))
                        if half or t:
                            act.wait_ge(*nth(tag[1], half * nt + t))
                        act.activation(sqj[:, t % 2, :], ps[:, 4 * half + t, :], ACT.Square,
                                       accum_out=st[:, 4 * half + t:4 * half + t + 1]).then_inc(S(tag[1]), 1)

            sqj = tmp[:, :, 512:1024]
            act.wait_ge(*nth("cols_ready", 1))
            act.activation(scol[:], cols1[:, 0:16].rearrange("p (c k) -> p c k", c=2), ACT.Silu).then_inc(S("silu_c"), 1)
            act.activation(ea[:], alog, ACT.Exp).then_inc(S("ea"), 1)
            phase_over(act, "emod")
            act.wait_ge(*nth("x_in", 32))
            norm_T("en0", ALL, 0, lambda t: aT[:, :, t * P:t * P + P])
            sil_c = tmp[:, :, 0:512]
            for b in range(12 + 2):
                if b < 12:
                    act.wait_ge(*nth("qkvT_made", b + 1))
                    copy(qkvT[:, b, :, 2:258], ps[:, b % 4, :].rearrange("p (s n) -> p s n", s=2)).then_inc(S("qkvT_ev"), 1)
                if 1 <= b < 13:
                    act.wait_ge(*nth("conv", b))
                    if b >= 3:
                        act.wait_ge(*nth("conv_tr", b - 2))
                    act.activation(sil_c[:, (b - 1) % 2, :], tmp[:, (b - 1) % 2, 512:1024], ACT.Silu).then_inc(S("conv_silu"), 1)
                if b >= 2:
                    act.wait_ge(*nth("conv_tr", b - 1))
                    copy(qkvrow[:, :, (b - 2) * P:(b - 2) * P + P], ps[:, 4 + b % 2, :].rearrange("p (t n) -> p t n", t=4))\
                        .then_inc(S("conv_ev"), 1)
            rows("erow_made", "erow_ev", erow_dst)
            phase_over(act, "eproj")
            for t in ALL:
                if t >= 2:
                    act.wait_ge(*nth("qk_red", t - 1))
                act.activation(tmp[:, t % 2, :], qkvrow[:, t, 0:1024], ACT.Square).then_inc(S("qk_sq"), 1)
            act.wait_ge(*nth("g_abs", 1))
            act.activation(ge_[:], ge_[:], ACT.Exp).then_inc(S("g_e"), 1)
            act.wait_ge(*nth("g_e", 1))
            act.activation(gl_[:], ge_[:], ACT.Ln, bias=1.0).then_inc(S("g_ln"), 1)
            act.activation(gbeta[:], rowbuf[:, :, 528:544], ACT.Exp, scale=-1.0).then_inc(S("b_e"), 1)
            phase_over(act, "gprep")
            for seg in range(2):
                act.wait_ge(*nth("gh_mm", seg + 1))
                act.activation(eall[:], ps[:, 7, 0:96], ACT.Exp).then_inc(S("gh_exp"), 1)
                for tl in range(2):
                    t = 2 * seg + tl
                    dsts = [kTt[0:HD, 0:4, :], qTt[0:HD, 0:4, :], kbgT[:, tl, 0:4, :], qgT[:, tl, 0:4, :]]
                    for n, d in enumerate(dsts):
                        act.wait_ge(*nth("tr_done", 8 * t + 2 * n + 1))
                        copy(d, ps[0:d.shape[0], 2 * n, :].rearrange("p (h n) -> p h n", h=4)).then_inc(S("tr_evA"), 1)
                    for n in range(4):
                        act.wait_ge(*nth("dec_done", 4 * t + n + 1))
                        dst = Lb[:, n % 2] if n < 2 else AT[:, tl, n % 2]
                        act.activation(dst, ps[:, 2 + n, :], ACT.Exp).then_inc(S("dec_exp"), 1)
                    for lv in range(1, 6):
                        for d in range(2):
                            act.wait_ge(*nth("inv_y", 12 * t + 2 * lv + d + 1))
                            if lv > 1:
                                act.wait_ge(*nth("inv_z", 10 * t + 2 * (lv - 2) + d + 1))
                            copy(Yb[:, d], ps[:, d, :]).then_inc(S("inv_ye"), 1)
                for n in range(4):
                    N = 4 * seg + n
                    if N:
                        act.wait_ge(*nth("sc_ost", N))
                    act.wait_ge(*nth("sc_o1", N + 1))
                    copy(ox, ps[:, 1, :]).then_inc(S("sc_ox"), 1)
                    act.wait_ge(*nth("sc_v", N + 1))
                    if N:
                        act.wait_ge(*nth("sc_o2", N))
                    copy(vn, ps[:, 2, :]).then_inc(S("sc_vn"), 1)
                phase_over(act, f"seg{seg}")
            for t in ALL:
                act.wait_ge(*nth("o_comb", 8))
                if t >= 1:
                    act.wait_ge(*nth("o_done", t))
                act.activation(tmp[:, 0, 0:512], qkvrow[:, t, 0:512], ACT.Square).then_inc(S("o_sq"), 1)
                act.activation(tmp[:, 1, 0:512], rowbuf[:, t, 0:512], ACT.Silu).then_inc(S("z_silu"), 1)
            phase_over(act, "gdn")

            def attention(tag, jobs):
                def exp(n):
                    j = jobs[n]
                    act.wait_ge(*nth(tag + "_m", n + 1))
                    if n >= 2:
                        act.wait_ge(*nth(tag + "_t", n - 1))
                    nm = st[:, 8 + n % 4:9 + n % 4]
                    if j["sink"] is not None:
                        act.activation(st[:, 16 + n % 4:17 + n % 4], j["sink"], ACT.Exp, bias=nm)
                    act.activation(prob[:, n % 2, 0:j["nk"]], ps[:, n % 2, 0:j["nk"]], ACT.Exp, bias=nm, scale=j["scale"],
                                   accum_out=st[:, 12 + n % 4:13 + n % 4]).then_inc(S(tag + "_exp"), 1)
                exp(0)
                for n, j in enumerate(jobs):
                    if n + 1 < len(jobs):
                        exp(n + 1)
                    act.wait_ge(*nth(tag + "_t", n + 1))
                    if n >= 2:
                        act.wait_ge(*nth(tag + "_pv", n - 1))
                    copy(probT[:, n % 2, 0:j["nk"]], ps[:, 2 + n % 2, 0:j["nk"]]).then_inc(S(tag + "_pt"), 1)

            def turned(tr, ev, dsts):
                for h, d in enumerate(dsts):
                    if h % 2 == 0:
                        act.wait_ge(*nth(tr, h + 1))
                        copy(d, ps[0:d.shape[0], h % 4, 0:d.shape[-1]]).then_inc(S(ev + "A"), 1)

            turned("swtr", "swtr_ev", sw_dst)
            phase_over(act, "swprep")
            attention("sw", sw_jobs)
            phase_over(act, "sw")
            cat_T("eoutc", ALL)
            gate_rows("e1", 2)
            phase_over(act, "ecat")
            squares(("eout_made", "e1_sq"), lambda half, t: 4 * half + t + 1, 4)
            phase_over(act, "eout")
            norm_T("en2", ALL, 24, lambda t: aT[:, :, t * P:t * P + P])
            for b in range(22):
                act.wait_ge(*nth("gu_made", b + 1))
                if b >= 2:
                    act.wait_ge(*nth("gu_h", b - 1))
                act.activation(sil[:, b % 2, :], ps[:, b % 2, :], ACT.Silu).then_inc(S("gu_silu"), 1)
            gate_rows("e3", 2)
            phase_over(act, "egu")
            squares(("down_step", "e3_sq"), lambda half, t: 3 * half + 3, 4)
            phase_over(act, "edown")
            phase_over(act, "omod")
            norm_T("on0", ALL, 0, lambda t: aT[:, :, t * P:t * P + P])
            rows("orow_made", "orow_ev", orow_dst)
            phase_over(act, "oproj")
            for t in range(2):
                act.activation(tmp[:, t, 0:384], cq[:, t, :], ACT.Square, accum_out=st[:, t:t + 1])
            for t in ALL:
                ins = act.activation(tmp[:, t % 2, 384 + 256 * (t // 2):640 + 256 * (t // 2)], ckvkr[:, t, 0:256], ACT.Square, accum_out=st[:, 2 + t:3 + t])
            ins.then_inc(S("lr_sq"), 1)
            phase_over(act, "lowr")
            rows("uq_made", "uq_ev", uq_dst)
            rows("ukv_made", "ukv_ev", ukv_dst)
            phase_over(act, "up")
            turned("mtr", "mtr_ev", mtr_dst)
            phase_over(act, "mprep")
            attention("ml", ml_jobs)
            phase_over(act, "ml")
            act.wait_ge(*nth("lam_s", 1))
            act.activation(lam[:, 0:2], lam[:, 0:2], ACT.Exp).then_inc(S("lam_e"), 1)
            turned("dtr", "dtr_ev", dtr_dst)
            phase_over(act, "dprep")

            def dexp(n):
                act.wait_ge(*nth("df_m", n + 1))
                if n >= 2:
                    act.wait_ge(*nth("df_t", n - 1))
                for w in range(2):
                    ins = act.activation(prob1[:, 2 * (n % 2) + w, :], ps[:, 2 * (n % 2) + w, :], ACT.Exp,
                                         bias=st[:, 8 + 2 * (n % 2) + w:9 + 2 * (n % 2) + w], scale=HD ** -0.5,
                                         accum_out=st[:, 12 + 2 * (n % 2) + w:13 + 2 * (n % 2) + w])
                ins.then_inc(S("df_exp"), 1)
            dexp(0)
            for n in range(8):
                if n + 1 < 8:
                    dexp(n + 1)
                act.wait_ge(*nth("df_t", n + 1))
                if n >= 2:
                    act.wait_ge(*nth("df_pv", n - 1))
                copy(probT1[:, n % 2, :], ps[:, 4 + n % 2, :]).then_inc(S("df_pt"), 1)
            phase_over(act, "df")
            for t in range(2):
                ins = act.activation(tmp[:, t, 0:512], cat1[:, t, 512:1024], ACT.Square)
            ins.then_inc(S("sub_sq"), 1)
            cat_T("ooutc", LATS)
            gate_rows("o1", 1)
            phase_over(act, "ocat")
            squares(("oout_made", "o1_sq"), lambda half, t: 2 * half + t + 1, 2)
            phase_over(act, "omix")
            norm_T("on2", LATS, 24, lambda t: fT[:, :, (t - 2) * P:(t - 1) * P])
            act.wait_ge(*nth("lg_sub", 1))
            act.activation(gate, gate, ACT.Exp).then_inc(S("lg_exp"), 1)
            phase_over(act, "route")
            n_passes = passes(act)
            with act.Fori(0, n_passes) as it:
                act.wait_ge(*nth("m_pt", it + 1))
                copy(pickT, ps[:, 6, 0:256].rearrange("p (a b) -> p a b", a=2)).then_inc(S("m_pte"), 1)
                for k in range(4):
                    ins = act.activation(xsT[:, k, :], ps[:, 0, k * P:k * P + P], ACT.Identity,
                                         bias=modc[:, 24 + k, 0:1], scale=scaleA[:, k, 0:1])
                ins.then_inc(S("m_xsA"), 1)
                for c in range(NCHUNK):
                    act.wait_ge(*nth("moe_read", it * len(ORDER) + (MRING + SLOT_OF[("g", c)] + 1)))
                    if c >= 2:
                        act.wait_ge(*nth("m_h", it * NCHUNK + (c - 1)))
                    act.activation(msil[:, c % 2, :], ps[:, 2 * (c % 2), :], ACT.Silu).then_inc(S("m_silu"), 1)
                    act.wait_ge(*nth("m_tr", it * NCHUNK + (c + 1)))
                    if c >= 2:
                        act.wait_ge(*nth("moe_read", it * len(ORDER) + (MRING + SLOT_OF[("d", c - 2)] + 1)))
                    copy(hT[:, c % 2, :, :], ps[:, 6, :].rearrange("p (a b) -> p a b", a=4)).then_inc(S("m_ht"), 1)
                act.wait_ge(*nth("moe_read", it * len(ORDER) + (MRING + len(ORDER))))
                for o in range(2):
                    ins = copy(ysb[:, 512 * o:512 * o + 512], ps[:, 4 + o, :])
                ins.then_inc(S("m_y"), 1)
            act.wait_ge(*nth("moe_done", 1))
            for t in range(2):
                act.activation(ps[:, 4 + 2 * t:6 + 2 * t, :], moe[:, t, :].rearrange("p (a b) -> p a b", a=2), ACT.Square,
                               accum_out=st[:, t:t + 1]).then_inc(S("o3_sq"), 1)
            gate_rows("o3", 1)

        @block.vector
        def _(v):
            tallies = {}

            def tally(name):
                if name not in tallies:
                    tallies[name] = Tally(S(name))
                return tallies[name]

            def link(ins, name="dve_order"):
                tally(name).add(ins)
                v.wait_ge(*nth(name, tally(name).n))

            def signal(ins, name):
                tally(name).add(ins)

            def power(dst, src, eps):
                n = src.shape[1] * (src.shape[2] if len(src.shape) == 3 else 1)
                x, y, w = rs[:, 0, 0:n], rs[:, 1, 0:n], rs[:, 2, 0:n]
                like = lambda b: b.rearrange("p (t h) -> p t h", h=src.shape[2]) if len(src.shape) == 3 else b
                link(v.tensor_scalar(like(x), src, eps, None, ALU.add))
                link(v.tensor_scalar(w.bitcast(I32), x.bitcast(I32), 1, None, ALU.logical_shift_right))
                link(v.tensor_scalar(y.bitcast(I32), w.bitcast(I32), -1.0, float(0x5f3759df), ALU.mult, ALU.add))
                for step in range(3):
                    if n == 1:
                        link(v.tensor_scalar(w, y, y, x, ALU.mult, ALU.mult))
                    else:
                        link(v.tensor_tensor(w, y, y, ALU.mult))
                        link(v.tensor_tensor(w, w, x, ALU.mult))
                    link(v.tensor_scalar(w, w, -0.5, 1.5, ALU.mult, ALU.add))
                    link(v.tensor_tensor(dst if step == 2 else like(y), like(y), like(w), ALU.mult))

            def norm_T(tag, tiles, shift, dst, buf=tmp):
                def normed(n):
                    v.wait_ge(*nth(tag + "_ss", n + 1))
                    power(st[:, 16 + n:17 + n], st[:, n:n + 1], D * EPS)
                    if n >= 2:
                        v.wait_ge(*nth(tag + "_tr", 2 * n - 2))
                    signal(v.tensor_scalar(buf[:, n % 2, :], xr[:, tiles[n], :], st[:, 16 + n:17 + n], SQRT_D, ALU.mult, ALU.mult),
                           tag + "_xn")
                normed(0)
                for n, t in enumerate(tiles):
                    if n + 1 < len(tiles):
                        normed(n + 1)
                    v.wait_ge(*nth(tag + "_tr", 2 * n + 2))
                    c = cond_of(t)
                    for k in range(4, 8):
                        ins = v.tensor_scalar(dst(t)[:, k, :], ps[:, 2 * (n % 2) + 1, (k - 4) * P:(k - 3) * P],
                                              scaleA[:, k, c:c + 1], modc[:, shift + k, c:c + 1], ALU.mult, ALU.add)
                    signal(ins, tag + "_evD")

            def cat_T(tag, tiles):
                for n, t in enumerate(tiles):
                    v.wait_ge(*nth(tag + "_tr", 2 * n + 2))
                    signal(v.tensor_copy(aT[:, 4:8, t * P:t * P + P], ps[:, 2 * (n % 2) + 1, :].rearrange("p (k n) -> p k n", k=4)),
                           tag + "_evD")

            def mod_columns(tag, bias):
                v.wait_ge(*nth(tag + "_cols", 12))
                link(v.tensor_tensor(modc[:], ps[:, 0, 0:96].rearrange("p (k c) -> p k c", c=2), bch(bias, 2), ALU.add))

            def scale_columns(at, norms):
                link(v.scalar_tensor_tensor(scaleA[:], modc[:, at:at + 8, :], 1.0, bch(norms, 2), ALU.add, ALU.mult))

            def gate_diag(tag, at, norms, conds):
                link(v.scalar_tensor_tensor(gatec[:], modc[:, at:at + 8, :], SQRT_D, bch(norms, 2), ALU.mult, ALU.mult))
                for c in range(conds):
                    ins = v.tensor_tensor(tmp[:, c, :].rearrange("p (k j) -> p k j", k=KB), bcm(ident, KB),
                                          bch(gatec[:, :, c], P), ALU.mult)
                    (signal if c == conds - 1 else lambda i, _n: link(i))(ins, tag + "_diag")

            def rows(made, ev, dsts, banks=4):
                for g, d in enumerate(dsts):
                    if g % 2 == 1:
                        v.wait_ge(*nth(made, g + 1))
                        signal(v.tensor_copy(d, ps[:, g % banks, 0:d.shape[-1]]), ev + "D")

            def turned(tr, ev, dsts):
                for h, d in enumerate(dsts):
                    if h % 2 == 1:
                        v.wait_ge(*nth(tr, h + 1))
                        signal(v.tensor_copy(d, ps[0:d.shape[0], h % 4, 0:d.shape[-1]]), ev + "D")

            def residual(tag, rows_tag, tiles, gate_tag, gates):
                nt = len(tiles)
                v.wait_ge(*nth(gate_tag + "_gev", gates))
                for t in range(nt):
                    v.wait_ge(*nth(tag, nt + t + 1))
                    link(v.tensor_tensor(st[:, 24 + t:25 + t], st[:, t:t + 1], st[:, 4 + t:5 + t], ALU.add))
                    power(st[:, 28 + t:29 + t], st[:, 24 + t:25 + t], D * EPS)
                    c = cond_of(tiles[t])
                    for half in range(2):
                        hs = slice(512 * half, 512 * half + 512)
                        link(v.scalar_tensor_tensor(tmp[:, half, 0:512], ps[:, 4 * half + t, :], st[:, 28 + t:29 + t],
                                                    Gb[:, c, hs], ALU.mult, ALU.mult))
                        link(v.tensor_tensor(xr[:, tiles[t], hs], xr[:, tiles[t], hs], tmp[:, half, 0:512], ALU.add))

            def rope(x, cos, sin, heads, n, t, b1, b2):
                q = n // 4
                b1v = b1[:, 0:heads * n].rearrange("p (h d) -> p h d", h=heads)
                b2v = b2[:, 0:heads * n].rearrange("p (h a b q) -> p h a b q", h=heads, a=2, b=2)
                xs = x.rearrange("p h (a b q) -> p h a b q", a=2, b=2)
                ss = sin[:, t, :].rearrange("p (a b q) -> p a b q", a=2, b=2)
                link(v.tensor_tensor(b1v, x, bcm(cos[:, t, :], heads), ALU.mult))
                for b in range(2):
                    link(v.tensor_tensor(b2v[:, :, :, b, :], xs[:, :, :, 1 - b, :],
                                         ss[:, :, b, :].unsqueeze(1).to_broadcast([P, heads, 2, q]), ALU.mult))
                link(v.tensor_tensor(x, b1v, b2[:, 0:heads * n].rearrange("p (h d) -> p h d", h=heads), ALU.add))

            v.wait_ge(*nth("cols_tr", 1))
            v.tensor_copy(cols1[:, 0:112], ps[:, 0, 0:112])
            v.tensor_copy(cols2[:, 0:124], ps[:, 0, P:P + 124])
            link(v.tensor_copy(cols3[:, 0:5], ps[:, 0, 256:261]), "cols_ready")
            link(v.tensor_scalar(nsink[:], sink, -1.0, None, ALU.mult))
            link(v.tensor_scalar(gdnw, gdnw, float(np.sqrt(HD)), None, ALU.mult))
            link(v.tensor_scalar(subln, subln, float(np.sqrt(2 * HD)) * (1.0 - LAM_INIT), None, ALU.mult))
            mod_columns("emod", cols1[:, 16:64])
            scale_columns(8, cols2[:, 0:8])
            phase_over(v, "emod")
            v.memset(qkvT[:, :, :, 0:2], 0.0)
            link(v.memset(qkvT[:, :, :, 258:260], 0.0))
            v.wait_ge(*nth("x_in", 32))
            norm_T("en0", ALL, 0, lambda t: aT[:, :, t * P:t * P + P])
            for b in range(12):
                v.wait_ge(*nth("qkvT_ev", b + 1))
                if b >= 2:
                    v.wait_ge(*nth("conv_silu", b - 1))
                else:
                    v.wait_ge(*nth("en0_tr", 8))
                acc = tmp[:, b % 2, 512:1024].rearrange("p (s n) -> p s n", s=2)
                link(v.tensor_scalar(acc, qkvT[:, b, :, 0:256], cols2[:, 64 + b:65 + b], None, ALU.mult))
                for j in range(1, 5):
                    ins = v.scalar_tensor_tensor(acc, qkvT[:, b, :, j:j + 256], cols2[:, 64 + 12 * j + b:65 + 12 * j + b], acc,
                                                 ALU.mult, ALU.add)
                    if j < 4:
                        link(ins)
                signal(ins, "conv")
            rows("erow_made", "erow_ev", erow_dst)
            phase_over(v, "eproj")
            link(v.tensor_tensor(gx[:], rowbuf[:, :, 512:528], bcm(dtb, TILES), ALU.add))
            signal(v.scalar_tensor_tensor(ge_[:], gx[:], -1.0, gx[:], ALU.mult, ALU.min), "g_abs")
            for t in ALL:
                v.wait_ge(*nth("qk_sq", t + 1))
                link(v.tensor_reduce(gst[:, t, :], tmp[:, t % 2, :].rearrange("p (h d) -> p h d", h=16), AXX, ALU.add), "qk_red")
            power(gst[:], gst[:], EPS)
            link(v.tensor_scalar(gst[:, :, 0:8], gst[:, :, 0:8], HD ** -0.5, None, ALU.mult))
            for t in ALL:
                x = qkvrow[:, t, 0:1024].rearrange("p (h d) -> p h d", h=16)
                link(v.tensor_tensor(x, x, bch(gst[:, t, :], HD), ALU.mult))
            v.wait_ge(*nth("g_ln", 1))
            v.wait_ge(*nth("ea", 1))
            link(v.scalar_tensor_tensor(gg[:], gx[:], 0.0, gl_[:], ALU.max, ALU.add))
            link(v.scalar_tensor_tensor(gg[:], gg[:], -1.0, bcm(ea[:], TILES), ALU.mult, ALU.mult))
            v.wait_ge(*nth("b_e", 1))
            link(v.tensor_scalar(gbeta[:], gbeta[:], 1.0, None, ALU.add))
            link(v.reciprocal(gbeta[:], gbeta[:]))
            phase_over(v, "gprep")
            link(v.memset(Sst, 0.0), "sc_s")
            mask_l, mask_a = (C("gt_c"), C("lt_c")), (C("le_c"), C("ge_c"))
            eye_c = C("eye_c")
            for seg in range(2):
                v.wait_ge(*nth("gh_exp", seg + 1))
                for tl in range(2):
                    t = 2 * seg + tl
                    if tl:
                        v.wait_ge(*nth("tr_done", 8 * t))
                    q_, k_, v_ = (qkvrow[:, t, 512 * n:512 * n + 512].rearrange("p (h d) -> p h d", h=HEADS) for n in range(3))
                    link(v.tensor_tensor(bg[:, tl, :], gbeta[:, t, :], eall[:, 32 * tl:32 * tl + 16], ALU.mult))
                    for dst, x, f in ((kbgrow, k_, bg[:, tl, :]), (qgrow, q_, eall[:, 32 * tl:32 * tl + 16])):
                        for d in range(2):
                            ins = v.tensor_tensor(dst[:, :, d, :], x, bch(f[:, 8 * d:8 * d + 8], HD), ALU.mult)
                        signal(ins, "row_ready")
                    for b in range(2):
                        v.wait_ge(*nth("tr_done", 8 * t + 2 * b + 2))
                        signal(v.tensor_copy((kTt, qTt)[b][0:HD, 4:8, :], ps[0:HD, 2 * b + 1, :].rearrange("p (h n) -> p h n", h=4)),
                               "tr_evD")
                    for b in range(2):
                        v.wait_ge(*nth("tr_done", 8 * t + 4 + 2 * b + 2))
                        signal(v.tensor_copy((kbgT, qgT)[b][:, tl, 4:8, :], ps[:, 5 + 2 * b, :].rearrange("p (h n) -> p h n", h=4)),
                               "tr_evD")
                    for n in range(4):
                        d = n % 2
                        signal(v.tensor_tensor(hv(rhsb[n]), bch(gg[:, t, 8 * d:8 * d + 8], CH),
                                               bcm((mask_l, mask_a)[n // 2][d], HEADS), ALU.mult), "rhs_ready")
                    for d in range(2):
                        link(v.tensor_tensor(hv(kt[:, tl, d]), k_, bch(eall[:, 32 * tl + 16 + 8 * d:32 * tl + 24 + 8 * d], HD), ALU.mult))
                        for c in range(2):
                            cs = slice(c * CH, c * CH + CH)
                            s = 2 * tl + c if d == 0 else 3 - (2 * tl + c)
                            link(v.tensor_tensor(hv(vbst[cs, s, :]), v_[cs], bch(gbeta[cs, t, 8 * d:8 * d + 8], HD), ALU.mult))
                    v.wait_ge(*nth("gram_done", 2 * t + 1))
                    for d in range(2):
                        v.wait_ge(*nth("dec_exp", 4 * t + 1 + d))
                        link(v.tensor_tensor(Lb[:, d], Lb[:, d], ps[:, 0, :], ALU.mult))
                        link(v.tensor_tensor(hv(Lb[:, d]), hv(Lb[:, d]), bcm(mask_l[d], HEADS), ALU.mult))
                        link(v.tensor_tensor(hv(Lb[:, d]), hv(Lb[:, d]), bch(gbeta[:, t, 8 * d:8 * d + 8], CH), ALU.mult))
                    v.wait_ge(*nth("gram_done", 2 * t + 2))
                    for d in range(2):
                        v.wait_ge(*nth("dec_exp", 4 * t + 3 + d))
                        link(v.tensor_tensor(AT[:, tl, d], AT[:, tl, d], ps[:, 1, :], ALU.mult))
                        link(v.tensor_tensor(hv(AT[:, tl, d]), hv(AT[:, tl, d]), bcm(mask_a[d], HEADS), ALU.mult))
                    for lv in range(6):
                        for d in range(2):
                            link(v.tensor_tensor(hv(Cb[:, d]), hv(Lb[:, d]), bcm(levels[:, d, lv, :], HEADS), ALU.mult), "inv_c")
                        for d in range(2):
                            X, Xt = Xb[:, d], XT[:, tl, d]
                            if lv == 0:
                                v.wait_ge(*nth("inv_y", 12 * t + d + 1))
                                link(v.tensor_tensor(hv(X), bcm(eye_c, HEADS), hv(Cb[:, d]), ALU.subtract))
                                link(v.tensor_tensor(hv(Xt), bcm(eye_c, HEADS), hv(ps[:, d, :]), ALU.subtract), "inv_x")
                            else:
                                v.wait_ge(*nth("inv_z", 10 * t + 2 * (lv - 1) + d + 1))
                                if lv < 5:
                                    link(v.tensor_tensor(X, X, ps[:, 2 + d, :], ALU.subtract))
                                link(v.tensor_tensor(Xt, Xt, ps[:, 4 + d, :], ALU.subtract), "inv_x")
                for n in range(4):
                    N = 4 * seg + n
                    v.wait_ge(*nth("sc_p", N + 1))
                    signal(v.tensor_tensor(rr, vbst[:, n, :], ps[:, 0, :], ALU.subtract), "sc_r")
                    v.wait_ge(*nth("sc_o1", N + 1))
                    link(v.tensor_tensor(hv(Sst), hv(Sst), bch(eall[:, 64 + 8 * n:72 + 8 * n], HD), ALU.mult))
                    v.wait_ge(*nth("sc_u", N + 1))
                    link(v.tensor_tensor(Sst, Sst, ps[:, 4, :], ALU.add), "sc_s")
                    v.wait_ge(*nth("sc_ox", N + 1))
                    v.wait_ge(*nth("sc_o2", N + 1))
                    link(v.tensor_tensor(ostep[:, n, :], ox, ps[:, 3, :], ALU.add), "sc_ost")
                for s in range(4):
                    cs = slice((s % 2) * CH, (s % 2) * CH + CH)
                    link(v.tensor_tensor(qkvrow[cs, 2 * seg + s // 2, 0:512], ostep[cs, s, :], ostep[cs, 3 - s, :], ALU.add), "o_comb")
                phase_over(v, f"seg{seg}")
            for t in ALL:
                v.wait_ge(*nth("o_sq", t + 1))
                link(v.tensor_reduce(st[:, 32:40], tmp[:, 0, 0:512].rearrange("p (h d) -> p h d", h=HEADS), AXX, ALU.add))
                power(st[:, 40:48], st[:, 32:40], HD * EPS)
                o = qkvrow[:, t, 0:512]
                link(v.tensor_tensor(hv(o), hv(o), bch(st[:, 40:48], HD), ALU.mult))
                link(v.tensor_tensor(hv(o), hv(o), bcm(gdnw, HEADS), ALU.mult))
                v.wait_ge(*nth("z_silu", t + 1))
                link(v.tensor_tensor(o, o, tmp[:, 1, 0:512], ALU.mult), "o_done")
            phase_over(v, "gdn")

            def attention(tag, jobs):
                def maxes(n):
                    j = jobs[n]
                    v.wait_ge(*nth(tag + "_s", n + 1))
                    if j["mask"] is not None:
                        link(v.tensor_tensor(ps[:, n % 2, 256:512], ps[:, n % 2, 256:512], j["mask"], ALU.add))
                    link(v.tensor_reduce(st[:, 24 + n % 4:25 + n % 4], ps[:, n % 2, 0:j["nk"]], AXX, ALU.max))
                    nm, mx = st[:, 8 + n % 4:9 + n % 4], st[:, 24 + n % 4:25 + n % 4]
                    if j["sink"] is not None:
                        signal(v.tensor_scalar(nm, mx, -j["scale"], j["nsink"], ALU.mult, ALU.min), tag + "_m")
                    else:
                        signal(v.tensor_scalar(nm, mx, -j["scale"], None, ALU.mult), tag + "_m")
                maxes(0)
                for n, j in enumerate(jobs):
                    if n + 1 < len(jobs):
                        maxes(n + 1)
                    v.wait_ge(*nth(tag + "_exp", n + 1))
                    den = st[:, 12 + n % 4:13 + n % 4]
                    if j["sink"] is not None:
                        link(v.tensor_tensor(st[:, 28 + n % 4:29 + n % 4], den, st[:, 16 + n % 4:17 + n % 4], ALU.add))
                        den = st[:, 28 + n % 4:29 + n % 4]
                    link(v.reciprocal(st[:, 20 + n % 4:21 + n % 4], den))
                    v.wait_ge(*nth(tag + "_pv", n + 1))
                    signal(v.tensor_scalar(j["out"], ps[:, 4 + n % 2, 0:j["vw"]], st[:, 20 + n % 4:21 + n % 4], None, ALU.mult),
                           tag + "_o")

            for t in LATS:
                rope(rowbuf[:, t, 544:1184].rearrange("p (h d) -> p h d", h=10), cos64, sin64, 10, HD, t - 2, rt1, rt2)
            v.drain().then_inc(S("swrope"), 1)
            turned("swtr", "swtr_ev", sw_dst)
            phase_over(v, "swprep")
            attention("sw", sw_jobs)
            phase_over(v, "sw")
            cat_T("eoutc", ALL)
            gate_diag("e1", 16, cols2[:, 8:16], 2)
            phase_over(v, "ecat")
            residual("e1_sq", None, ALL, "e1", 4)
            scale_columns(32, cols2[:, 16:24])
            phase_over(v, "eout")
            norm_T("en2", ALL, 24, lambda t: aT[:, :, t * P:t * P + P])
            for b in range(22):
                v.wait_ge(*nth("gu_silu", b + 1))
                signal(v.tensor_tensor(hTd[:, b, :], sil[:, b % 2, :], ps[:, 4 + b % 2, :], ALU.mult), "gu_h")
            gate_diag("e3", 40, cols2[:, 24:32], 2)
            phase_over(v, "egu")
            residual("e3_sq", None, ALL, "e3", 4)
            phase_over(v, "edown")
            mod_columns("omod", cols1[:, 64:112])
            scale_columns(8, cols2[:, 32:40])
            phase_over(v, "omod")
            norm_T("on0", ALL, 0, lambda t: aT[:, :, t * P:t * P + P])
            rows("orow_made", "orow_ev", orow_dst)
            phase_over(v, "oproj")
            v.wait_ge(*nth("lr_sq", 1))
            power(st[:, 16:18], st[:, 0:2], 384 * EPS)
            power(st[:, 18:22], st[:, 2:6], 256 * EPS)
            for t in range(2):
                link(v.tensor_scalar(cq[:, t, :], cq[:, t, :], st[:, 16 + t:17 + t], float(np.sqrt(384)), ALU.mult, ALU.mult))
            for t in ALL:
                ins = v.tensor_scalar(ckvkr[:, t, 0:256], ckvkr[:, t, 0:256], st[:, 18 + t:19 + t], 16.0, ALU.mult, ALU.mult)
                (signal if t == 3 else lambda i, _n: link(i))(ins, "lowrank")
            v.wait_ge(*nth("lr_tr", 1))
            for j in range(3):
                link(v.tensor_scalar(cqT[:, j, :], ps[:, j, 0:256], cols3[:, j:j + 1], None, ALU.mult))
            v.wait_ge(*nth("lr_tr", 2))
            for j in range(2):
                link(v.tensor_scalar(ckvT[:, j, :], ps[:, 3 + j, :], cols3[:, 3 + j:4 + j], None, ALU.mult))
            phase_over(v, "lowr")
            rows("uq_made", "uq_ev", uq_dst)
            rows("ukv_made", "ukv_ev", ukv_dst)
            phase_over(v, "up")
            for t in range(2):
                rope(rowq[:, t, :].rearrange("p (h d) -> p h d", h=HEADS)[:, :, 64:96], cos32, sin32, HEADS, 32, t, rt3, rt4)
                rope(ckvkr[:, 2 + t, 256:288].rearrange("p (h d) -> p h d", h=1), cos32, sin32, 1, 32, t, rt3, rt4)
                rope(hv(dq[:, t, :]), cos64, sin64, HEADS, HD, t, rt3, rt4)
                rope(hv(dk[:, 2 + t, :]), cos64, sin64, HEADS, HD, t, rt3, rt4)
            for t in ALL:
                link(v.tensor_copy(k96[:, t, :, 0:64], hv(rowkv[:, t, :])[:, :, 0:64]))
                ins = v.tensor_copy(k96[:, t, :, 64:96], bcm(ckvkr[:, t, 256:288], HEADS))
                (signal if t == 3 else lambda i, _n: link(i))(ins, "k96_ready")
            turned("mtr", "mtr_ev", mtr_dst)
            phase_over(v, "mprep")
            attention("ml", ml_jobs)
            phase_over(v, "ml")
            lp = lamv.rearrange("p (a b d) -> p a b d", a=2, b=2)
            lbuf = M(BZ + 7168, 2, HD)
            link(v.tensor_tensor(lbuf, lp[:, :, 0, :], lp[:, :, 1, :], ALU.mult))
            signal(v.tensor_reduce(lam[:, 0:2], lbuf, AXX, ALU.add), "lam_s")
            v.wait_ge(*nth("lam_e", 1))
            link(v.tensor_tensor(lam[:, 2:3], lam[:, 1:2], lam[:, 0:1], ALU.subtract))
            link(v.tensor_scalar(lam[:, 3:4], lam[:, 2:3], -LAM_INIT, None, ALU.add))
            turned("dtr", "dtr_ev", dtr_dst)
            phase_over(v, "dprep")

            def dmax(n):
                v.wait_ge(*nth("df_s", n + 1))
                b = 2 * (n % 2)
                link(v.tensor_reduce(st[:, 24 + b:26 + b], ps[:, b:b + 2, :], AXX, ALU.max))
                signal(v.tensor_scalar(st[:, 8 + b:10 + b], st[:, 24 + b:26 + b], -HD ** -0.5, None, ALU.mult), "df_m")
            dmax(0)
            for n in range(8):
                h, t, b = n // 2, n % 2, 2 * (n % 2)
                v.wait_ge(*nth("df_exp", n + 1))
                link(v.reciprocal(st[:, 16:18], st[:, 12 + b:14 + b]))
                link(v.tensor_tensor(st[:, 18:19], st[:, 17:18], lam[:, 3:4], ALU.mult))
                link(v.tensor_scalar(prob1[:, b, :], prob1[:, b, :], st[:, 16:17], None, ALU.mult))
                link(v.scalar_tensor_tensor(prob1[:, b, :], prob1[:, b + 1, :], st[:, 18:19], prob1[:, b, :], ALU.mult, ALU.add), "df_a")
                if n + 1 < 8:
                    dmax(n + 1)
                v.wait_ge(*nth("df_pv", n + 1))
                signal(v.tensor_copy(cat1[:, t, 512 + h * P:512 + h * P + P], ps[:, 6 + n % 2, 0:P]), "df_o")
            phase_over(v, "df")
            v.wait_ge(*nth("sub_sq", 1))
            for t in range(2):
                link(v.tensor_reduce(st[:, 32 + 4 * t:36 + 4 * t], tmp[:, t, 0:512].rearrange("p (h d) -> p h d", h=4), AXX, ALU.add))
            power(st[:, 40:48], st[:, 32:40], 2 * HD * EPS)
            for t in range(2):
                o = cat1[:, t, 512:1024].rearrange("p (h d) -> p h d", h=4)
                link(v.tensor_tensor(o, o, bch(st[:, 40 + 4 * t:44 + 4 * t], P), ALU.mult))
                ins = v.tensor_tensor(o, o, bcm(subln, 4), ALU.mult)
                (signal if t == 1 else lambda i, _n: link(i))(ins, "subln")
            cat_T("ooutc", LATS)
            gate_diag("o1", 16, cols2[:, 40:48], 1)
            phase_over(v, "ocat")
            residual("o1_sq", None, LATS, "o1", 2)
            scale_columns(32, cols2[:, 48:56])
            phase_over(v, "omix")
            norm_T("on2", LATS, 24, lambda t: fT[:, :, (t - 2) * P:(t - 1) * P], xn_l)
            v.wait_ge(*nth("logits", 1))
            link(v.tensor_copy(logit[:], ps[:, 4, 0:16].rearrange("p (t e) -> p t e", t=2)))
            for t in range(2):
                l = logit[:, t, :]
                p0, p1 = (pair[:, n, :].rearrange("p (e j) -> p e j", e=8) for n in range(2))
                link(v.tensor_tensor(p0, bcm(l, 8), bch(l, 8), ALU.is_gt))
                link(v.tensor_tensor(p1, bcm(l, 8), bch(l, 8), ALU.is_equal))
                link(v.tensor_tensor(pair[:, 1, :], pair[:, 1, :], C("earlier"), ALU.mult))
                link(v.tensor_tensor(pair[:, 0, :], pair[:, 0, :], pair[:, 1, :], ALU.add))
                link(v.tensor_reduce(rank[:, t, :], p0, AXX, ALU.add))
                link(v.tensor_reduce(st[:, 50 + t:51 + t], l, AXX, ALU.max))
                link(v.tensor_scalar(gate[:, t, :], l, st[:, 50 + t:51 + t], None, ALU.subtract))
            signal(v.tensor_scalar(sel, rank[:], 1.5, None, ALU.is_lt), "selected")
            v.wait_ge(*nth("selected", 1))
            v.drain().then_inc(S("lg_sub"), 1)
            v.wait_ge(*nth("lg_exp", 1))
            link(v.tensor_tensor(gate, gate, sel, ALU.mult))
            link(v.tensor_reduce(st[:, 52:54], gate, AXX, ALU.add))
            link(v.reciprocal(st[:, 54:56], st[:, 52:54]))
            link(v.tensor_tensor(gate, gate, bch(st[:, 54:56], 8), ALU.mult))
            v.wait_ge(*nth("positions", 1))
            link(v.tensor_copy(posn, ps[:, 5, 0:16].rearrange("p (t e) -> p t e", t=2)))
            link(v.memset(moe[:], 0.0))
            big, nth_big, weighed = plan_w[:, 0:8], plan_w[:, 8:16], plan_w[:, 16:24]
            count_to = C("iota")[0:1, 0:EXPERTS]
            link(v.tensor_scalar(big, ps[0:1, 5, 16:24], float(P), None, ALU.is_gt))
            link(v.tensor_tensor(by_pair, bcm(big, 8), C("earlier")[0:1].rearrange("p (e j) -> p e j", e=8), ALU.mult))
            link(v.tensor_reduce(nth_big, by_pair, AXX, ALU.add))
            link(v.tensor_tensor(weighed, big, count_to, ALU.mult))
            again = MAX_PASSES - EXPERTS
            link(v.tensor_tensor(by_pair[:, 0:again], bcm(nth_big, again), bch(C("iota")[0:1, 0:again], 8), ALU.is_equal))
            link(v.tensor_tensor(by_pair[:, 0:again], by_pair[:, 0:again], bcm(weighed, again), ALU.mult))
            link(v.memset(plan[:], 0.0))
            link(v.tensor_copy(plan[:, 0:8], count_to))
            link(v.tensor_copy(plan[:, 16:24], count_to))
            link(v.tensor_reduce(plan[:, 8:8 + again], by_pair[:, 0:again], AXX, ALU.add))
            link(v.tensor_scalar(plan[:, 24:24 + again], plan[:, 8:8 + again], float(EXPERTS), None, ALU.add))
            link(v.tensor_reduce(st[0:1, 56:57], big, AXX, ALU.add))
            link(v.tensor_scalar(plan[:, 15:16], st[0:1, 56:57], float(EXPERTS), None, ALU.add))
            link(v.tensor_copy(plan_i[:], plan[:]), "plan_ready")
            v.tensor_copy(sel16[:, :, 8:16], sel)
            v.tensor_copy(gate16[:, :, 8:16], gate)
            link(v.tensor_scalar(posn16[:, :, 8:16], posn, float(-P), None, ALU.add))
            phase_over(v, "route")
            n_passes = passes(v)
            with v.Fori(0, n_passes) as it:
                e = v.value_load(plan_i[0:1, bass.ds(it + 16, 1)], min_val=0, max_val=2 * EXPERTS - 1)
                for t in range(2):
                    v.tensor_scalar(pick[:, t, :], C("iota"), posn16[:, t, bass.ds(e, 1)], sel16[:, t, bass.ds(e, 1)],
                                    ALU.is_equal, ALU.mult).then_inc(S("m_p1"), 1)
                v.wait_ge(*nth("m_p1", it * 2 + 2))
                for t in range(2):
                    ins = v.tensor_scalar(pickw[:, t, :], pick[:, t, :], gate16[:, t, bass.ds(e, 1)], None, ALU.mult)
                ins.then_inc(S("m_pick"), 1)
                v.wait_ge(*nth("m_gath", it + 1))
                for k in range(4, 8):
                    ins = v.tensor_scalar(xsT[:, k, :], ps[:, 1, (k - 4) * P:(k - 3) * P], scaleA[:, k, 0:1],
                                          modc[:, 24 + k, 0:1], ALU.mult, ALU.add)
                ins.then_inc(S("m_xsD"), 1)
                for c in range(NCHUNK):
                    v.wait_ge(*nth("m_silu", it * NCHUNK + (c + 1)))
                    v.wait_ge(*nth("moe_read", it * len(ORDER) + (MRING + SLOT_OF[("u", c)] + 1)))
                    if c >= 2:
                        v.wait_ge(*nth("m_tr", it * NCHUNK + (c - 1)))
                    v.tensor_tensor(hrow[:, c % 2, :], msil[:, c % 2, :], ps[:, 2 * (c % 2) + 1, :], ALU.mult)\
                        .then_inc(S("m_h"), 1)
                v.wait_ge(*nth("m_sc", it + 1))
                for t in range(2):
                    m2 = moe[:, t, :].rearrange("p (a b) -> p a b", a=2)
                    ins = v.tensor_tensor(m2, m2, ps[:, 2 * t:2 * t + 2, :], ALU.add)
                ins.then_inc(S("m_acc"), 1)
            link(v.drain(), "moe_done")
            gate_diag("o3", 40, cols2[:, 56:64], 1)
            v.wait_ge(*nth("o3_gev", 2))
            v.wait_ge(*nth("o3_sq", 2))
            power(st[:, 16:18], st[:, 0:2], D * EPS)
            for t in range(2):
                link(v.scalar_tensor_tensor(mtmp, moe[:, t, :], st[:, 16 + t:17 + t], Gb[:, 0, :], ALU.mult, ALU.mult))
                link(v.tensor_tensor(xr[:, 2 + t, :], xr[:, 2 + t, :], mtmp, ALU.add), "result")


_INS = ['x', 'c', 'ctx', 'c_ctx', 'e_mod_w', 'e_mod_b', 'e_norms', 'e_w_in', 'e_conv_w', 'e_a_log', 'e_dt_bias',
        'e_gdn_norm', 'e_sink', 'e_w_out', 'e_ffn_gate', 'e_ffn_up', 'e_ffn_down', 'o_mod_w', 'o_mod_b', 'o_norms',
        'o_w_in', 'o_q_norm', 'o_kv_norm', 'o_w_uq', 'o_w_ukv', 'o_lambda', 'o_subln', 'o_w_out', 'o_router',
        'o_exp_gate', 'o_exp_up', 'o_exp_down']


def kernel(**inputs):
    import numpy as _np
    import concourse.bacc as _bacc
    from concourse import mybir as _mybir
    from concourse.bass_utils import run_bass_kernel_spmd as _run

    nc = _bacc.Bacc("TRN2", target_bir_lowering=False, num_devices=1)
    arrays, aps = {}, {}
    for name in _INS:
        arr = _np.ascontiguousarray(inputs[name])
        arrays[f"in_{name}"] = arr
        aps[name] = nc.dram_tensor(f"in_{name}", arr.shape, _mybir.dt.from_np(arr.dtype), kind="ExternalInput").ap()
    arrays["shape_consts"] = shape_constants()
    aps["consts"] = nc.dram_tensor("shape_consts", (P, N_CONST), F32, kind="ExternalInput").ap()
    out = nc.dram_tensor("out", (1, 256, D), F32, kind="ExternalOutput").ap()
    hybrid_trunk(nc, aps, out)
    r = _run(nc, [arrays], core_ids=[0])
    return r.results[0]["out"]
```

```python
from contextlib import ExitStack

import numpy as np
import concourse.bass as bass
from concourse import mybir

F32 = mybir.dt.float32
F32R = mybir.dt.float32r
I32 = mybir.dt.int32
ALU = mybir.AluOpType
ACT = mybir.ActivationFunctionType
AXX = mybir.AxisListType.X

P = 128
D = 1024
KB = D // P
TILES = 4
LAT = 2
SEQ = 512
EPS = 1e-6
HEADS = 8
HD = 64
CH = 64
F_DENSE = 2816
F_EXP = 3584
EXPERTS = 8
EVEN_T = 1536
EVEN_R = 1312
ODD_IN = 2208
LAM_INIT = 0.8 - 0.6 * float(np.exp(-0.3))
NEG = -1e30

CONST_PARTS = [("ident", 128), ("ones", 128), ("le", 128), ("gt", 128), ("ge", 128), ("lt", 128),
               ("le_c", 64), ("gt_c", 64), ("ge_c", 64), ("lt_c", 64),
               ("levels", 2 * 6 * 64), ("chunk_of", 128), ("eye_c", 64), ("band", 512), ("cos64", 128), ("sin64", 128),
               ("cos32", 64), ("sin32", 64), ("iota", 128), ("before", 128), ("earlier", 64)]
CONST_AT = {}
N_CONST = 0
for _name, _n in CONST_PARTS:
    CONST_AT[_name] = (N_CONST, _n)
    N_CONST += _n


def rope_table(dim):
    tok = np.arange(256)
    half = dim // 2
    inv = (10000.0 ** (-np.arange(0, half, 2, dtype=np.float32) / half)).astype(np.float32)
    ar = (tok // 64).astype(np.float32)[:, None] * inv
    ac = (tok % 64).astype(np.float32)[:, None] * inv
    ang = np.concatenate([ar, ar, ac, ac], -1).astype(np.float32)
    sign = np.tile(np.repeat([-1.0, 1.0], half // 2), 2).astype(np.float32)
    return np.cos(ang).astype(np.float32), np.sin(ang).astype(np.float32) * sign


def shape_constants():
    c = {}
    t = np.arange(P)
    same = (t[:, None] // CH) == (t[None, :] // CH)
    c["ident"], c["ones"] = np.eye(P), np.ones((P, P))
    tests = {"le": lambda a, b: a <= b, "gt": lambda a, b: a > b, "ge": lambda a, b: a >= b, "lt": lambda a, b: a < b}
    for n, f in tests.items():
        c[n] = f(t[:, None], t[None, :]) & same
        c[n + "_c"] = f((t % CH)[:, None], np.arange(CH)[None, :])
    lev = np.zeros((P, 2, 6, CH))
    i, j = (t % CH)[:, None], np.arange(CH)[None, :]
    for n in range(6):
        b = 1 << n
        lev[:, 0, n] = (i // (2 * b) == j // (2 * b)) & ((i // b) % 2 == 1) & ((j // b) % 2 == 0)
        lev[:, 1, n] = (i // (2 * b) == j // (2 * b)) & ((i // b) % 2 == 0) & ((j // b) % 2 == 1)
    c["levels"] = lev
    c["eye_c"] = i == j
    c["chunk_of"] = np.repeat((t // CH)[:, None] == np.arange(2)[None, :], CH, 1)
    band = np.zeros((P, 2, 256))
    for q in range(2):
        band[:, q] = np.where(np.abs((q * P + t)[:, None] - np.arange(256)[None, :]) <= 128, 0.0, NEG)
    c["band"] = band
    for n in (64, 32):
        cos, sin = rope_table(n)
        c[f"cos{n}"] = cos.reshape(2, P, n).transpose(1, 0, 2)
        c[f"sin{n}"] = sin.reshape(2, P, n).transpose(1, 0, 2)
    c["iota"] = np.tile(np.arange(P), (P, 1))
    c["before"] = t[:, None] < t[None, :]
    e = np.arange(8)
    c["earlier"] = np.tile((e[None, :] < e[:, None]).reshape(1, 64), (P, 1))
    return np.concatenate([np.asarray(c[n], np.float32).reshape(P, -1) for n, _ in CONST_PARTS], 1)


def shared_semaphores():
    table = {}

    def kind(shared, *stages):
        at = 0
        for name, n in stages:
            table[name] = (shared, at)
            at += n

    turns = (("en0", 4), ("eoutc", 4), ("en2", 4), ("on0", 4), ("ooutc", 2), ("on2", 2))
    kind("turned", *((t + "_tr", 2 * n) for t, n in turns))
    for e in ("_evA", "_evD"):
        kind("turned" + e, *((t + e, n) for t, n in turns))
    for e in ("_ss", "_xn"):
        kind("norm" + e, *((t + e, n) for t, n in turns if not t.endswith("c")))
    for e in ("_s", "_m", "_exp", "_t", "_pt", "_pv", "_o"):
        kind("att" + e, ("sw" + e, 32), ("ml" + e, 16), ("df" + e, 8))
    gates = (("e1", 4), ("e3", 4), ("o1", 2), ("o3", 2))
    kind("gate_diag", *((t + "_diag", 1) for t, _ in gates))
    for e in ("_gr", "_gev"):
        kind("gate" + e, *((t + e, n) for t, n in gates))
    kind("new_rows", ("e1_new", 4), ("e3_new", 4), ("o1_new", 2))
    kind("row_squares", ("e1_sq", 8), ("e3_sq", 8), ("o1_sq", 4), ("o3_sq", 2))
    groups = (("erow", 12), ("swtr", 10), ("orow", 16), ("uq", 4), ("ukv", 8), ("mtr", 16), ("dtr", 16))
    kind("rows_made", *((t if t.endswith("tr") else t + "_made", n) for t, n in groups))
    for e in "AD":
        kind("rows_ev" + e, *((t + "_ev" + e, n // 2) for t, n in groups))
    for e in ("_prod", "_row", "_turned", "_cols"):
        kind("mod" + e, ("emod" + e, 12), ("omod" + e, 12))
    kind("out_made", ("eout_made", 8), ("oout_made", 4))
    return table


SHARED = shared_semaphores()


class Tally:

    def __init__(self, sem):
        self.sem, self.n = sem, 0

    def add(self, ins, k=1):
        ins.then_inc(self.sem, k)
        self.n += k


def hybrid_trunk(nc, a, out):
    ctx = ExitStack()
    with ctx:
        def sb(name, shape):
            return ctx.enter_context(nc.sbuf_tensor(name, shape, F32))

        sems = {}

        def S(name):
            name = SHARED.get(name, (name, 0))[0]
            if name not in sems:
                sems[name] = ctx.enter_context(nc.semaphore(name))
            return sems[name]

        def nth(name, n):
            return S(name), SHARED.get(name, (name, 0))[1] + n

        const = sb("const", [P, N_CONST])
        xr = sb("xr", [P, TILES, D])
        SLOT = 4096
        RING = 4
        A = RING * SLOT
        BZ = A + 11392
        mem_at = (nc.sbuf_base + 31) // 32 * 32
        mem = sb("mem", [P, BZ + 14592])
        ps = ctx.enter_context(nc.psum_tensor("ps", [P, 8, 512], F32))

        def M(at, *dims, of=None):
            n = int(np.prod(dims))
            v = mem[:, at:at + n] if of is None else of[:]
            if len(dims) == 1:
                return v
            names = "abcd"[:len(dims)]
            return v.rearrange("p (%s) -> p %s" % (" ".join(names), " ".join(names)),
                               **{names[i]: dims[i] for i in range(len(dims))})

        def R(at, *dims):
            n = int(np.prod(dims))
            return M(at, *dims, of=nc.alloc_sbuf_tensor_at(f"r{at}_{n}", [P, n], F32R, offset=mem_at + 4 * at))

        def C(name):
            at, n = CONST_AT[name]
            return const[:, at:at + n]

        ident, ones = C("ident"), C("ones")
        levels = C("levels").rearrange("p (d l j) -> p d l j", d=2, l=6)
        band = C("band").rearrange("p (q k) -> p q k", q=2)
        cos64, sin64, cos32, sin32 = (C(n).rearrange("p (t d) -> p t d", t=2) for n in ("cos64", "sin64", "cos32", "sin32"))

        slot = [M(i * SLOT, SLOT) for i in range(7)]
        rows1 = M(BZ, P)
        rows2 = M(BZ + P, P)
        rows3 = M(BZ + 2 * P, P)
        cols1, cols2, cols3 = sb("cols1", [P, P]), sb("cols2", [P, 124]), sb("cols3", [P, 5])
        bc = sb("bc", [P, 488])
        scol = sb("scol", [P, 2, KB])
        modc = sb("modc", [P, 48, 2])
        modn = sb("modn", [P, 48, 2])
        mrow = sb("mrow", [2, 2, 512])
        scaleA = sb("scaleA", [P, KB, 2])
        gatec = sb("gatec", [P, KB, 2])
        st = sb("st", [P, 64])
        alog, dtb, gdnw, sink, subln, lamv = (bc[:, 0:16], bc[:, 16:32], bc[:, 32:96], bc[:, 96:104], bc[:, 104:232], bc[:, 232:488])

        qkvrow = M(A, TILES, EVEN_T)
        rowbuf = M(A + 6144, TILES, EVEN_R)
        aT = M(BZ, KB, SEQ)
        Gb = M(BZ + 4096, 2, D)
        tmp = M(BZ + 6144, 2, D)
        qkvT = M(BZ + 8192, 12, 2, 260)

        slot_r = [R(i * SLOT, SLOT) for i in range(4)]
        aH_r, aL_r = R(BZ + 9216, KB, SEQ), R(BZ, KB, SEQ)
        aH = aH_r.bitcast(F32)
        DOWN_SPLIT, HIDDEN_SPLIT = {0: 3, 1: 2, 3: 3, 4: 2}, 16
        hidL_r = R(A, HIDDEN_SPLIT, SEQ)
        hidden_high = lambda k: (aL_r, aH_r)[k // KB][:, k % KB, :]

        stream, slot_of = [], []

        def place(slots=range(RING)):
            last = {n: -1 for n in slots}
            for i, n in enumerate(slot_of):
                if n in last:
                    last[n] = i
            slot_of.append(min(slots, key=lambda n: last[n]))

        def take(parts, freed_by, count, borrowed=None):
            stream.append((parts, freed_by, count, borrowed))
            return len(stream) - 1

        def kview(w, c0, c1):
            return w.rearrange("(k p) n -> p k n", p=P)[:, :, c0:c1]

        def sv(i, k, n, at=0):
            return slot[slot_of[i]][:, at:at + k * n].rearrange("p (k n) -> p k n", k=k)

        def simple(w, c0, c1, sem, count, borrowed=None, slots=range(RING)):
            i = len(stream)
            place(slots)
            k = w.shape[0] // P
            return take([(sv(i, k, c1 - c0), kview(w, c0, c1))], sem, count, borrowed)

        e_mod = [simple(a["e_mod_w"][0], 512 * n, 512 * n + 512, "emod_prod", n + 1) for n in range(12)]
        w_in = a["e_w_in"][0]
        e_qkv = [simple(w_in, 512 * n, 512 * n + 512, "qkvT_made", 4 * n + 4) for n in range(3)]
        R_CH = [(0, 512), (512, 1024), (1024, 1312)]
        e_row = [simple(w_in, EVEN_T + c0, EVEN_T + c1, "erow_made", 4 * n + 4) for n, (c0, c1) in enumerate(R_CH)]
        o_mod = [simple(a["o_mod_w"][0], 512 * n, 512 * n + 512, "omod_prod", n + 1, slots=(2, 3)) for n in range(12)]
        e_out = [simple(a["e_w_out"][0], 512 * n, 512 * n + 512, "eout_made", 4 * n + 4, slots=(2, 3)) for n in range(2)]
        e_gu = []
        for n in range(11):
            i = len(stream)
            place((0, 1))
            e_gu.append(take([(sv(i, 8, 256), kview(a["e_ffn_gate"][0], 256 * n, 256 * n + 256)),
                              (sv(i, 8, 256, 2048), kview(a["e_ffn_up"][0], 256 * n, 256 * n + 256))],
                             "gu_made", 2 * n + 2, "gdn" if n < 2 else None))
        DOWN = [(0, 8), (8, 16), (16, 22)]
        e_down = []
        for half in range(2):
            for n, (k0, k1) in enumerate(DOWN):
                i = len(stream)
                at = 3 * half + n
                place((0, 1))
                e_down.append(take([(sv(i, k1 - k0, 512), a["e_ffn_down"][0][k0 * P:k1 * P, :].rearrange(
                    "(k p) n -> p k n", p=P)[:, :, 512 * half:512 * half + 512])], "down_step", at + 1))
        ow = a["o_w_in"][0]
        O_CH = [(0, 384), (384, 672), (672, 1184), (1184, 1696), (1696, 2208)]
        O_LAT = [True, False, True, False, False]
        o_in, made = [], 0
        for n, (c0, c1) in enumerate(O_CH):
            made += 2 if O_LAT[n] else 4
            o_in.append(simple(ow, c0, c1, "orow_made", made, ("down_step", 5 - n) if n < 2 else None, slots=(2, 3)))
        o_made = np.cumsum([2 if lat else 4 for lat in O_LAT]).tolist()
        OIN_AT = {o_made[n - 2]: n for n in range(2, 5)}
        o_uq = simple(a["o_w_uq"][0], 0, 768, "uq_made", 4, ("orow_made", made), slots=(0, 1))
        o_ukv = simple(a["o_w_ukv"][0], 0, 1024, "ukv_made", 8, ("orow_made", made), slots=(0, 1))
        o_out = [simple(a["o_w_out"][0], 512 * n, 512 * n + 512, "oout_made", 2 * n + 2) for n in range(2)]
        N_STREAM = len(stream)

        landed_at, per_slot = [], [0] * RING
        for i, (parts, *_r) in enumerate(stream):
            per_slot[slot_of[i]] += 16 * len(parts)
            landed_at.append(per_slot[slot_of[i]])

        def arrived(pe, i):
            pe.wait_ge(*nth(f"landed{slot_of[i]}", landed_at[i]))

        block = ctx.enter_context(nc.Block())

        PHASES = ["emod", "eproj", "gprep", "seg0", "seg1", "gdn", "swprep", "sw", "ecat", "eout", "egu", "edown", "oproj",
                  "lowr", "up", "mprep", "ml", "dprep", "df", "ocat", "omix", "route"]

        def phase_ended(eng, name):
            eng.wait_ge(*nth("phase_over", 3 * (PHASES.index(name) + 1)))

        def phase_over(eng, name):
            eng.drain().then_inc(S("phase_over"), 1)
            phase_ended(eng, name)

        FCH = 512
        NCHUNK = F_EXP // FCH
        MO = BZ + 1024
        xn_l = M(MO, 2, D)
        fT = M(MO + 2048, KB, 256)
        xsT, xsH_r, xsL_r = M(MO + 4096, KB, P), R(MO + 2048, KB, P), R(MO + 4096, KB, P)
        xsH = xsH_r.bitcast(F32)
        hrow = M(MO + 5120, 2, FCH)
        hTH_r, hTL_r = R(MO + 6144, 2, 4, P), R(MO + 3072, 2, 4, P)
        hTH = hTH_r.bitcast(F32)
        ysb = M(MO + 7168, D)
        moe = M(MO + 8192, 2, D)
        pick = M(MO + 10240, 2, P)
        pickw = M(MO + 10496, 2, P)
        pickT = M(MO + 10752, 2, P)
        mtmp = M(MO + 11008, D)
        MRING, HRING, HALF = 7, 6, 2048
        wslot, wslot_r = ([at_(n * HALF, HALF) for n in range(MRING)] for at_ in (M, R))
        hslot_r = [R((MRING + n) * HALF, HALF) for n in range(HRING)]
        hslot = [h.bitcast(F32) for h in hslot_r]

        def parts_of(n, kind):
            k = 2 if kind == "d" else 4
            return tuple(b.rearrange("p (k n) -> p k n", k=k) for b in (hslot_r[n % HRING], wslot_r[n % MRING]))
        logit, rank = (sb(n, [P, 2, EXPERTS]) for n in ("logit", "rank"))
        sel16, gate16, posn16 = (sb(n, [P, 2, 2 * EXPERTS]) for n in ("sel", "gate", "posn"))
        sel, gate, posn = (b[:, :, 0:EXPERTS] for b in (sel16, gate16, posn16))
        pair = sb("pair", [P, 2, 64])
        router = sb("router", [P, KB, EXPERTS])

        ORDER = [(kind, 0, h) for kind in "gu" for h in range(2)]
        for c in range(1, NCHUNK):
            ORDER += [(kind, c, h) for kind in "gu" for h in range(2)] + [("d", c - 1, h) for h in range(2)]
        ORDER += [("d", NCHUNK - 1, h) for h in range(2)]
        UNITS = len(ORDER)
        UNIT_OF = {k: n for n, k in enumerate(ORDER)}
        LEAD = 3
        BESIDE = {n: [] for n in range(UNITS)}
        SCATTER_BANKS = (slice(2, 4), slice(6, 8))
        for c in range(NCHUNK):
            BESIDE[min(UNIT_OF["u", c, 1] + LEAD, UNITS - 2)].append((c, "gated"))
            BESIDE[UNIT_OF["g", c + 1, 1] + LEAD if c + 1 < NCHUNK else UNITS - 1].append((c, "turned"))
        BESIDE[1].append((0, "sum"))
        BESIDE[UNIT_OF["u", 0, 1] + LEAD].append((0, "weights"))
        BESIDE[UNITS // 2].append((0, "pick"))
        BESIDE[UNITS - 2].append((0, "gathered"))

        MAX_PASSES = EXPERTS + 2 * SEQ // (P + 1)
        plan = sb("plan", [1, 32])
        plan_i = ctx.enter_context(nc.sbuf_tensor("plan_i", [1, 32], I32))

        def passes(eng):
            eng.wait_ge(*nth("plan_ready", 1))
            return eng.value_load(plan_i[0:1, 15:16], min_val=EXPERTS, max_val=MAX_PASSES)

        def moe_sync(sp):
            wg, wu, wd = (a[n][0] for n in ("o_exp_gate", "o_exp_up", "o_exp_down"))
            wg, wu, wd = (w.rearrange("e d f -> (e d) f") for w in (wg, wu, wd))

            def weights(it, e):
                for n, (kind, c, h) in enumerate(ORDER):
                    sp.wait_ge(*nth("moe_read", it * UNITS + (n + 1)))
                    dst = wslot[n % MRING]
                    if kind == "d":
                        src = wd[bass.ds(e * F_EXP + (c * FCH + h * 2 * P), 2 * P), :].rearrange("(k p) n -> p k n", p=P)
                        dst = dst.rearrange("p (k n) -> p k n", k=2)
                    else:
                        w = wg if kind == "g" else wu
                        src = w[bass.ds(e * D + h * 4 * P, 4 * P), c * FCH:c * FCH + FCH].rearrange("(k p) n -> p k n", p=P)
                        dst = dst.rearrange("p (k n) -> p k n", k=4)
                    sp.dma_start(dst, src).then_inc(S(f"mlanded{n % MRING}"), 16)

            weights(0, 0)
            n_passes = passes(sp)
            with sp.Fori(1, n_passes) as it:
                weights(it, sp.value_load(plan_i[0:1, bass.ds(it, 1)], min_val=0, max_val=EXPERTS - 1))

        @block.sync
        def _(sp):
            sp.dma_start(const[:], a["consts"]).then_inc(S("const_in"), 16)
            sp.dma_start(rows1[0:8, :], a["c"].rearrange("a (k p) -> (a k) p", p=P)).then_inc(S("small_in"), 16)
            sp.dma_start(rows1[8:16, :], a["c_ctx"].rearrange("(k p) -> k p", p=P)).then_inc(S("small_in"), 16)
            sp.dma_start(rows1[16:64, :], a["e_mod_b"].rearrange("a (k p) -> (a k) p", p=P)).then_inc(S("small_in"), 16)
            sp.dma_start(rows1[64:112, :], a["o_mod_b"].rearrange("a (k p) -> (a k) p", p=P)).then_inc(S("small_in"), 16)
            sp.dma_start(rows2[0:32, :], a["e_norms"].rearrange("a m (k p) -> (a m k) p", p=P)).then_inc(S("small_in"), 16)
            sp.dma_start(rows2[32:64, :], a["o_norms"].rearrange("a m (k p) -> (a m k) p", p=P)).then_inc(S("small_in"), 16)
            sp.dma_start(rows2[64:124, :], a["e_conv_w"].rearrange("a m (k p) -> (a m k) p", p=P)).then_inc(S("small_in"), 16)
            sp.dma_start(rows3[0:3, :], a["o_q_norm"].rearrange("a (k p) -> (a k) p", p=P)).then_inc(S("small_in"), 16)
            sp.dma_start(rows3[3:5, :], a["o_kv_norm"].rearrange("a (k p) -> (a k) p", p=P)).then_inc(S("small_in"), 16)
            at = 0
            for name, n in (("e_a_log", 16), ("e_dt_bias", 16), ("e_gdn_norm", 64), ("e_sink", 8), ("o_subln", 128), ("o_lambda", 256)):
                src = a[name].rearrange("a b c -> (a b c)") if len(a[name].shape) == 3 else a[name].rearrange("a b -> (a b)")
                sp.dma_start(bc[:, at:at + n], src.partition_broadcast(P)).then_inc(S("small_in"), 16)
                at += n
            sp.dma_start(router[:], a["o_router"][0].rearrange("(k p) e -> p k e", p=P)).then_inc(S("small_in"), 16)
            def load(i):
                for dst, src in stream[i][0]:
                    sp.dma_start(dst, src).then_inc(S(f"landed{slot_of[i]}"), 16)

            for i in range(RING):
                load(i)
            sp.dma_start(xr[:, 0:2, :], a["ctx"][0].rearrange("(t p) d -> p t d", p=P)).then_inc(S("x_in"), 16)
            sp.dma_start(xr[:, 2:4, :], a["x"][0].rearrange("(t p) d -> p t d", p=P)).then_inc(S("x_in"), 16)
            filled = {}
            for i, (_p, _f, _c, borrowed) in enumerate(stream):
                if slot_of[i] in filled:
                    _p, sem_name, count, _b = stream[filled[slot_of[i]]]
                    sp.wait_ge(*nth(sem_name, count))
                filled[slot_of[i]] = i
                if borrowed == "gdn":
                    phase_ended(sp, borrowed)
                elif borrowed:
                    sp.wait_ge(*nth(*borrowed))
                if i >= RING:
                    load(i)
            phase_ended(sp, "omix")
            moe_sync(sp)
            sp.wait_ge(*nth("result", 2))
            sp.dma_start(out[0].rearrange("(t p) d -> p t d", p=P), xr[:, 2:4, :]).then_inc(S("stored"), 16)
            sp.wait_ge(*nth("stored", 16))

        def bch(x, n):
            return x.unsqueeze(2).to_broadcast([x.shape[0], x.shape[1], n])

        def bcm(x, m):
            return x.unsqueeze(1).to_broadcast([x.shape[0], m, x.shape[1]])

        def hv(x, m=HEADS):
            return x.rearrange("p (h d) -> p h d", h=m)

        cond_of = lambda t: 0 if t >= LAT else 1
        ALL, LATS = list(range(TILES)), [2, 3]
        SQRT_D = float(np.sqrt(D))
        gx, gg, gbeta, gl_, ge_ = (sb(n, [P, TILES, 16]) for n in ("gx", "gg", "gbeta", "gl_", "ge_"))
        ea = sb("ea", [P, 16])
        gst = sb("gst", [P, TILES, 16])
        eall = sb("eall", [P, 96])
        bg = sb("bg", [P, 2, 16])
        Lb, Xb, Yb, Cb = (M(n * 1024, 2, 512) for n in range(4))
        kTt, qTt = M(4096, HEADS, P), M(5120, HEADS, P)
        AT = M(6144, 2, 2, 512)
        kbgT, qgT = M(BZ, 2, HEADS, P), M(BZ + 2048, 2, HEADS, P)
        kt = M(BZ + 4096, 2, 2, 512)
        vbst = M(BZ + 6144, 4, 512)
        XT = M(BZ + 8192, 2, 2, 512)
        ostep = M(BZ + 10240, 4, 512)
        kbgrow, qgrow = M(BZ + 10240, HEADS, 2, HD), M(BZ + 11264, HEADS, 2, HD)
        Sst, rr, vn, ox = (M(BZ + 12288 + 512 * n, 512) for n in range(4))
        o_square, z_gate = M(BZ + 8192, TILES, 512), M(BZ + 10240, TILES, 512)
        rhsb = [Cb[:, 0], Cb[:, 1], Yb[:, 0], Yb[:, 1]]
        swq, swk = M(BZ, HEADS, SEQ), M(BZ + 4096, 2, SEQ)
        prob, probT = M(BZ + 5120, 2, 512), M(BZ + 6144, 2, 512)
        rt1, rt2 = M(BZ + 7168, 640), M(BZ + 7808, 640)
        rt3, rt4 = M(BZ + 4096, 512), M(BZ + 4608, 512)
        hTd = M(A, 22, SEQ)
        sil = M(BZ + 8192, 2, 512)
        cq, ckvkr = M(A, 2, 384), M(A + 768, TILES, 288)
        dq, dk, dv = M(A + 1920, 2, 512), M(A + 2944, TILES, 512), M(A + 4992, TILES, 512)
        cqT, ckvT, rowq = M(A + 7040, 3, 256), M(A + 7808, 2, SEQ), M(A + 8832, 2, 768)
        cat1 = M(A + 7040, 2, D)
        rowkv = M(BZ + 8192, TILES, D)
        k96, kT1, qT1 = M(BZ + 4096, TILES, HEADS, 96), M(BZ, HEADS, SEQ), M(BZ + 12288, HEADS, 256)
        prob1, probT1 = M(BZ + 4096, 4, 512), M(BZ + 6144, 2, 512)
        lam = sb("lam", [P, 4])

        erow_dst = [rowbuf[:, t, c0:c1] for c0, c1 in R_CH for t in ALL]
        sw_dst = [swq[0:HD, h, :] for h in range(8)] + [swk[0:HD, h, :] for h in range(2)]
        orow_dst = ([cq[:, t, :] for t in range(2)] + [ckvkr[:, t, :] for t in ALL] + [dq[:, t, :] for t in range(2)]
                    + [dk[:, t, :] for t in ALL] + [dv[:, t, :] for t in ALL])
        uq_dst = [rowq[:, t, 384 * c:384 * c + 384] for t in range(2) for c in range(2)]
        ukv_dst = [rowkv[:, t, 512 * c:512 * c + 512] for t in ALL for c in range(2)]
        mtr_dst = [kT1[0:96, h, :] for h in range(8)] + [qT1[0:96, h, :] for h in range(8)]
        dtr_dst = [kT1[0:HD, h, :] for h in range(8)] + [qT1[0:HD, h, :] for h in range(8)]
        msil = M(MO + 12032, 2, FCH)
        plan_w = sb("plan_w", [1, 24])
        by_pair = sb("by_pair", [1, 64])[:].rearrange("p (e j) -> p e j", e=8)
        nsink = sb("nsink", [P, HEADS])
        sw_jobs = []
        for t in ALL:
            for h in range(HEADS):
                nk = 256 if t < LAT else 512
                g = h // 4
                sw_jobs.append(dict(q=swq[0:HD, h, t * P:t * P + P], k=swk[0:HD, g, 0:nk], nk=nk, vw=HD,
                                    v=[rowbuf[:, b, 1184 + g * HD:1184 + g * HD + HD] for b in range(nk // P)],
                                    scale=HD ** -0.5, mask=band[:, t - LAT, :] if t >= LAT else None,
                                    sink=sink[:, h:h + 1], nsink=nsink[:, h:h + 1], out=qkvrow[:, t, 512 + h * HD:512 + h * HD + HD]))
        ml_jobs = []
        for t in range(2):
            for h in range(HEADS):
                ml_jobs.append(dict(q=qT1[0:96, h, t * P:t * P + P], k=kT1[0:96, h, :], nk=512, vw=HD,
                                    v=[rowkv[:, b, h * P + HD:h * P + P] for b in range(4)],
                                    scale=96 ** -0.5, mask=None, sink=None, out=cat1[:, t, h * HD:h * HD + HD]))

        rs = sb("rs", [P, 3, 64])

        @block.tensor
        def _(pe):
            def turn(bank, j, src, dst_p=P, cols=P):
                k = src.shape[0]
                return pe.transpose(ps[0:dst_p, bank, j * P:j * P + cols], src, ident[0:k, 0:k])

            def norm_T(tag, tiles, buf=tmp):
                for n in range(len(tiles)):
                    pe.wait_ge(*nth(tag + "_xn", n + 1))
                    for half in range(2):
                        if n >= 2:
                            pe.wait_ge(*nth(tag + ("_evA", "_evD")[half], n - 1))
                        for j in range(4):
                            ins = turn(2 * (n % 2) + half, j, buf[:, n % 2, (4 * half + j) * P:(4 * half + j + 1) * P])
                        ins.then_inc(S(tag + "_tr"), 1)

            def cat_T(tag, src, tiles):
                for n, t in enumerate(tiles):
                    for half in range(2):
                        if n >= 2:
                            pe.wait_ge(*nth(tag + ("_evA", "_evD")[half], n - 1))
                        for j in range(4):
                            ins = turn(2 * (n % 2) + half, j, src(t)[:, (4 * half + j) * P:(4 * half + j + 1) * P])
                        ins.then_inc(S(tag + "_tr"), 1)

            def mod_products(tag, i, ks, bank):
                if ks[0] == 0:
                    arrived(pe, i)
                for k in ks:
                    ins = pe.matmul(ps[0:2, bank, :], scol[:, :, k], sv(i, 8, 512)[:, k, :], start=(k == 0), stop=(k == KB - 1))
                if ks[-1] == KB - 1:
                    ins.then_inc(S(tag + "_prod"), 1)

            def mod_turn(tag, u, bank):
                pe.wait_ge(*nth(tag + "_row", u + 1))
                for b in range(4):
                    ins = pe.transpose(ps[:, bank, 2 * b:2 * b + 2], mrow[0:2, u % 2, b * P:b * P + P], ident[0:2, 0:2])
                ins.then_inc(S(tag + "_turned"), 1)

            def gate_rows(tag, conds):
                pe.wait_ge(*nth(tag + "_diag", 1))
                for n in range(2 * conds):
                    pe.matmul(ps[:, n, :], ones, tmp.rearrange("p a d -> p (a d)")[:, 512 * n:512 * n + 512],
                              start=True, stop=True).then_inc(S(tag + "_gr"), 1)

            def rows(made, ev, jobs, banks=4, ready=lambda i: arrived(pe, i)):
                for g, (i, lhs, rhs, width) in enumerate(jobs):
                    if i is not None:
                        ready(i)
                    if g >= banks:
                        pe.wait_ge(*nth(ev + "AD"[g % 2], (g - banks) // 2 + 1))
                    for k, (l, r) in enumerate(zip(lhs, rhs)):
                        ins = pe.matmul(ps[:, g % banks, 0:width], l, r, start=(k == 0), stop=(k == len(lhs) - 1))
                    ins.then_inc(S(made), 1)

            pe.wait_ge(*nth("const_in", 16))
            pe.wait_ge(*nth("small_in", 16 * 16))
            turn(0, 0, rows1[0:112, :], P, 112)
            turn(0, 1, rows2[0:124, :], P, 124)
            turn(0, 2, rows3[0:5, :], P, 5).then_inc(S("cols_tr"), 1)
            pe.wait_ge(*nth("silu_c", 1))
            for u in range(12):
                if u >= 4:
                    pe.wait_ge(*nth("emod_cols", u - 3))
                mod_products("emod", e_mod[u], range(KB), u % 4)
                if u:
                    mod_turn("emod", u - 1, (u - 1) % 4)
            mod_turn("emod", 11, 3)
            phase_over(pe, "emod")
            norm_T("en0", ALL)
            pe.wait_ge(*nth("en0_evA", 4))
            pe.wait_ge(*nth("en0_evD", 4))

            def conv_turn(b):
                pe.wait_ge(*nth("conv_silu", b + 1))
                if b >= 2:
                    pe.wait_ge(*nth("conv_ev", b - 1))
                for t in ALL:
                    ins = turn(4 + b % 2, t, sil_c[:, b % 2, t * P:t * P + P])
                ins.then_inc(S("conv_tr"), 1)

            sil_c = tmp[:, :, 0:512]
            for b in range(12):
                arrived(pe, e_qkv[b // 4])
                w = sv(e_qkv[b // 4], 8, 512)
                if b >= 4:
                    pe.wait_ge(*nth("qkvT_ev", b - 3))
                for k in range(KB):
                    ins = pe.matmul(ps[:, b % 4, :], w[:, k, (b % 4) * P:(b % 4 + 1) * P], aT[:, k, :],
                                    start=(k == 0), stop=(k == KB - 1))
                ins.then_inc(S("qkvT_made"), 1)
                if b >= 2:
                    conv_turn(b - 2)
            conv_turn(10)
            conv_turn(11)
            pe.wait_ge(*nth("qkvT_ev", 12))
            jobs = []
            for n, (c0, c1) in enumerate(R_CH):
                w = sv(e_row[n], 8, c1 - c0)
                jobs += [(e_row[n], [aT[:, k, t * P:t * P + P] for k in range(KB)], [w[:, k, :] for k in range(KB)], c1 - c0)
                         for t in ALL]
            rows("erow_made", "erow_ev", jobs)
            phase_over(pe, "eproj")

            phase_over(pe, "gprep")
            lhs_cum = (C("le"), C("ge"))
            lhs_tail = (C("gt"), C("lt"))
            chunk_of = C("chunk_of").rearrange("p (c j) -> p c j", c=2)
            eye_c = C("eye_c")

            def omod_piece(t, n):
                u, piece = 3 * t + n // 7, n % 7
                if n >= 21:
                    return
                if piece == 0 and n:
                    pe.wait_ge(*nth("omod_cols", u))
                if piece < 4:
                    mod_products("omod", o_mod[u], (2 * piece, 2 * piece + 1), 6)
                if piece == 5:
                    mod_turn("omod", u, 6)

            for seg in range(2):
                for tl in range(2):
                    t = 2 * seg + tl
                    for d in range(2):
                        g = gg[:, t, d * 8:d * 8 + 8]
                        pe.matmul(ps[:, 7, tl * 32 + d * 8:tl * 32 + d * 8 + 8], lhs_cum[d], g, start=True, stop=True)
                        pe.matmul(ps[:, 7, tl * 32 + 16 + d * 8:tl * 32 + 24 + d * 8], lhs_tail[d], g, start=True, stop=True)
                        for c in range(2):
                            s = 2 * tl + c if d == 0 else 3 - (2 * tl + c)
                            ins = pe.matmul(ps[d * 64:d * 64 + 64, 7, 64 + 8 * s:72 + 8 * s], chunk_of[:, c, :], g,
                                            start=True, stop=True)
                ins.then_inc(S("gh_mm"), 1)
                for tl in range(2):
                    t = 2 * seg + tl
                    q_ = qkvrow[:, t, 0:512]
                    k_ = qkvrow[:, t, 512:1024]
                    if tl == 1:
                        pe.wait_ge(*nth("inv_x", 12 * t))
                    for b in range(8):
                        if b == 6 and t:
                            pe.wait_ge(*nth("omod_cols", 3 * t))
                        if b == 4:
                            pe.wait_ge(*nth("row_ready", 2 * t + 1))
                        if b == 6:
                            pe.wait_ge(*nth("row_ready", 2 * t + 2))
                        for j in range(4):
                            h = 4 * (b % 2) + j
                            if b < 4:
                                src = (k_, q_)[b // 2][:, h * HD:h * HD + HD]
                                ins = turn(b, j, src, HD)
                            else:
                                src = (kbgrow, qgrow)[(b - 4) // 2][:, h].rearrange("p d k -> p (d k)")
                                ins = turn(b, j, src)
                        ins.then_inc(S("tr_done"), 1)
                    pe.wait_ge(*nth("tr_evA", 4 * t + 2))
                    pe.wait_ge(*nth("tr_evD", 4 * t + 2))
                    for kind in range(2):
                        if kind == 1:
                            pe.wait_ge(*nth("tr_evA", 4 * t + 4))
                            pe.wait_ge(*nth("tr_evD", 4 * t + 4))
                        for h in range(HEADS):
                            for c in range(2):
                                cs = slice(c * CH, c * CH + CH)
                                ins = pe.matmul(ps[cs, (0, 7)[kind], h * CH:h * CH + CH], kTt[0:64, h, cs],
                                                (kTt, qTt)[kind][0:64, h, cs], start=True, stop=True)
                        ins.then_inc(S("gram_done"), 1)
                    for n in range(4):
                        d = n % 2
                        pe.wait_ge(*nth("rhs_ready", 4 * t + n + 1))
                        pe.matmul(ps[:, 2 + n, :], (lhs_cum[d], lhs_tail[d])[n // 2], rhsb[n], start=True, stop=True)\
                          .then_inc(S("dec_done"), 1)
                    beside = 0
                    for lv in range(6):
                        for d in range(2):
                            omod_piece(t, beside)
                            beside += 1
                            pe.wait_ge(*nth("inv_c", 12 * t + 2 * lv + d + 1))
                            if lv > 0:
                                pe.wait_ge(*nth("inv_x", 12 * t + 2 * (lv - 1) + d + 1))
                            for h in range(HEADS):
                                for c in range(2):
                                    cs, hs = slice(c * CH, c * CH + CH), slice(h * CH, h * CH + CH)
                                    rhs = eye_c[cs, :] if lv == 0 else XT[cs, tl, d, hs]
                                    ins = pe.matmul(ps[cs, d, hs], Cb[cs, d, hs], rhs, start=True, stop=True)
                            ins.then_inc(S("inv_y"), 1)
                        if lv == 0:
                            continue
                        for d in range(2):
                            omod_piece(t, beside)
                            beside += 1
                            pe.wait_ge(*nth("inv_ye", 10 * t + 2 * (lv - 1) + d + 1))
                            pe.wait_ge(*nth("inv_x0", 10 * t + 2 * (lv - 1) + d + 1))
                            for h in range(HEADS):
                                for c in range(2):
                                    cs, hs = slice(c * CH, c * CH + CH), slice(h * CH, h * CH + CH)
                                    ins = pe.matmul(ps[cs, 4 + d, hs], Xb[cs, d, hs], Yb[cs, d, hs], start=True, stop=True)
                            ins.then_inc(S("inv_z"), 1)
                            if lv == 5:
                                continue
                            for h in range(HEADS):
                                for c in range(2):
                                    cs, hs = slice(c * CH, c * CH + CH), slice(h * CH, h * CH + CH)
                                    ins = pe.matmul(ps[cs, 2 + d, hs], Yb[cs, d, hs], Xb[cs, d, hs], start=True, stop=True)
                            ins.then_inc(S("inv_z0"), 1)
                pe.wait_ge(*nth("inv_x", 12 * (2 * seg + 2)))
                for n in range(4):
                    N = 4 * seg + n
                    where = []
                    for d in range(2):
                        s = n if d == 0 else 3 - n
                        where.append((s // 2, slice((s % 2) * CH, (s % 2) * CH + CH), slice(d * 64, d * 64 + 64)))

                    def each(bank, lhs, rhs, by_chunk_out):
                        for d in range(2):
                            tl, cs, ds_ = where[d]
                            for h in range(HEADS):
                                hs = slice(h * CH, h * CH + CH)
                                o = ps[cs if by_chunk_out else ds_, bank, hs]
                                ins = pe.matmul(o, lhs(d, tl, cs, ds_, h, hs), rhs(d, cs, ds_, hs), start=True, stop=True)
                        return ins

                    pe.wait_ge(*nth("sc_s", N + 1))
                    each(0, lambda d, tl, cs, ds_, h, hs: kbgT[ds_, tl, h, cs], lambda d, cs, ds_, hs: Sst[ds_, hs], True)\
                        .then_inc(S("sc_p"), 1)
                    pe.wait_ge(*nth("sc_ox", N)) if N else None
                    each(1, lambda d, tl, cs, ds_, h, hs: qgT[ds_, tl, h, cs], lambda d, cs, ds_, hs: Sst[ds_, hs], True)\
                        .then_inc(S("sc_o1"), 1)
                    pe.wait_ge(*nth("sc_r", N + 1))
                    each(2, lambda d, tl, cs, ds_, h, hs: XT[cs, tl, d, hs], lambda d, cs, ds_, hs: rr[cs, hs], True)\
                        .then_inc(S("sc_v"), 1)
                    pe.wait_ge(*nth("sc_vn", N + 1))
                    each(4, lambda d, tl, cs, ds_, h, hs: kt[cs, tl, d, hs], lambda d, cs, ds_, hs: vn[cs, hs], False)\
                        .then_inc(S("sc_u"), 1)
                    pe.wait_ge(*nth("sc_ost", N)) if N else None
                    each(3, lambda d, tl, cs, ds_, h, hs: AT[cs, tl, d, hs], lambda d, cs, ds_, hs: vn[cs, hs], True)\
                        .then_inc(S("sc_o2"), 1)
                phase_over(pe, f"seg{seg}")
            pe.wait_ge(*nth("omod_cols", 12))
            phase_over(pe, "gdn")

            def attention(tag, jobs):
                J = len(jobs)

                def scores(n):
                    if n >= 2:
                        pe.wait_ge(*nth(tag + "_exp", n - 1))
                    j = jobs[n]
                    pe.matmul(ps[:, n % 2, 0:j["nk"]], j["q"], j["k"], start=True, stop=True).then_inc(S(tag + "_s"), 1)

                def turn_probs(n):
                    pe.wait_ge(*nth(tag + "_exp", n + 1))
                    if n >= 2:
                        pe.wait_ge(*nth(tag + "_pt", n - 1))
                    for b in range(jobs[n]["nk"] // P):
                        ins = turn(2 + n % 2, b, prob[:, n % 2, b * P:b * P + P])
                    ins.then_inc(S(tag + "_t"), 1)

                scores(0)
                scores(1)
                turn_probs(0)
                for n in range(J):
                    if n + 2 < J:
                        scores(n + 2)
                    if n + 1 < J:
                        turn_probs(n + 1)
                    j = jobs[n]
                    nb = j["nk"] // P
                    pe.wait_ge(*nth(tag + "_pt", n + 1))
                    if n >= 2:
                        pe.wait_ge(*nth(tag + "_o", n - 1))
                    for b in range(nb):
                        ins = pe.matmul(ps[:, 4 + n % 2, 0:j["vw"]], probT[:, n % 2, b * P:b * P + P], j["v"][b],
                                        start=(b == 0), stop=(b == nb - 1))
                    ins.then_inc(S(tag + "_pv"), 1)

            pe.wait_ge(*nth("swrope", 1))
            for h in range(10):
                if h >= 4:
                    pe.wait_ge(*nth("swtr_ev" + "AD"[h % 2], (h - 4) // 2 + 1))
                for t in ALL:
                    ins = turn(h % 4, t, rowbuf[:, t, 544 + h * HD:544 + h * HD + HD], HD)
                ins.then_inc(S("swtr"), 1)
            phase_over(pe, "swprep")
            attention("sw", sw_jobs)
            phase_over(pe, "sw")

            def out_proj(tag, slots, tiles, nt):
                pe.wait_ge(*nth(tag + "c_evA", nt))
                pe.wait_ge(*nth(tag + "c_evD", nt))
                for n, i in enumerate(slots):
                    arrived(pe, i)
                    w = sv(i, 8, 512)
                    for t in range(nt):
                        for k in range(KB):
                            ins = pe.matmul(ps[:, 4 * n + t, :], aT[:, k, tiles[t] * P:tiles[t] * P + P], w[:, k, :],
                                            start=(k == 0), stop=(k == KB - 1))
                        ins.then_inc(S(tag + "_made"), 1)

            cat_T("eoutc", lambda t: qkvrow[:, t, 0:1024], ALL)
            pe.wait_ge(*nth("eoutc_evA", 4))
            pe.wait_ge(*nth("eoutc_evD", 4))
            gate_rows("e1", 2)
            phase_over(pe, "ecat")
            out_proj("eout", e_out, ALL, 4)
            phase_over(pe, "eout")
            norm_T("en2", ALL)
            pe.wait_ge(*nth("en2_lo", 4))
            for b in range(22):
                i = b // 2
                pe.wait_ge(*nth("gu_lo", i + 1))
                if b >= 2:
                    pe.wait_ge(*nth("gu_h", b - 1))
                for w in range(2):
                    wh, wl = (slot_r[s][:, 2048 * w:2048 * w + 2048].rearrange("p (k n) -> p k n", k=KB)
                              for s in (2 + i % 2, slot_of[e_gu[i]]))
                    for k in range(KB):
                        for n, (x, y) in enumerate(((wh, aH_r), (wh, aL_r), (wl, aH_r))):
                            ins = pe.matmul(ps[:, 4 * w + b % 2, :], x[:, k, (b % 2) * P:(b % 2 + 1) * P], y[:, k, :],
                                            start=(k == 0 and n == 0), stop=(k == KB - 1 and n == 2))
                ins.then_inc(S("gu_made"), 1)
            gate_rows("e3", 2)
            phase_over(pe, "egu")
            for half in range(2):
                for n, (k0, k1) in enumerate(DOWN):
                    at = 3 * half + n
                    i = e_down[at]
                    if at in DOWN_SPLIT:
                        pe.wait_ge(*nth("down_lo", list(DOWN_SPLIT).index(at) + 1))
                        wh, wl = (slot_r[s][:].rearrange("p (k n) -> p k n", k=KB) for s in (DOWN_SPLIT[at], slot_of[i]))
                        for k in range(k0, k1):
                            if half == 0:
                                pe.wait_ge(*nth("hidden_lo", k + 1))
                            for t in ALL:
                                xh, xl = hidden_high(k)[:, t * P:t * P + P], hidL_r[:, k, t * P:t * P + P]
                                for m, (x, y) in enumerate(((xh, wh), (xh, wl), (xl, wh))):
                                    ins = pe.matmul(ps[:, 4 * half + t, :], x, y[:, k - k0, :], start=(k == 0 and m == 0), stop=False)
                        ins.then_inc(S("down_step"), 1)
                        continue
                    arrived(pe, i)
                    w = sv(i, k1 - k0, 512)
                    for k in range(k0, k1):
                        for t in ALL:
                            ins = pe.matmul(ps[:, 4 * half + t, :], hTd[:, k, t * P:t * P + P], w[:, k - k0, :],
                                            start=(k == 0), stop=(k == 21))
                    ins.then_inc(S("down_step"), 1)
            phase_over(pe, "edown")
            norm_T("on0", ALL)
            pe.wait_ge(*nth("on0_lo", 4))
            jobs = []
            for n, (c0, c1) in enumerate(O_CH):
                wh, wl = (slot_r[s][:, 0:KB * (c1 - c0)].rearrange("p (k n) -> p k n", k=KB) for s in (n % 2, slot_of[o_in[n]]))
                for t in (LATS if O_LAT[n] else ALL):
                    ts = slice(t * P, t * P + P)
                    jobs.append((n, [x[:, k, ts] for k in range(KB) for x in (aH_r, aH_r, aL_r)],
                                 [w[:, k, :] for k in range(KB) for w in (wh, wl, wh)], c1 - c0))
            rows("orow_made", "orow_ev", jobs, ready=lambda n: pe.wait_ge(*nth("oin_lo", n + 1)))
            phase_over(pe, "oproj")
            pe.wait_ge(*nth("lowrank", 1))
            for j in range(3):
                for t in range(2):
                    ins = turn(j, t, cq[:, t, j * P:j * P + P])
            ins.then_inc(S("lr_tr"), 1)
            for j in range(2):
                for t in ALL:
                    ins = turn(3 + j, t, ckvkr[:, t, j * P:j * P + P])
            ins.then_inc(S("lr_tr"), 1)
            phase_over(pe, "lowr")
            w = sv(o_uq, 3, 768)
            rows("uq_made", "uq_ev", [(o_uq, [cqT[:, k, t * P:t * P + P] for k in range(3)],
                                       [w[:, k, 384 * c:384 * c + 384] for k in range(3)], 384) for t in range(2) for c in range(2)])
            pe.wait_ge(*nth("uq_evA", 2))
            pe.wait_ge(*nth("uq_evD", 2))
            w = sv(o_ukv, 2, 1024)
            rows("ukv_made", "ukv_ev", [(o_ukv, [ckvT[:, k, t * P:t * P + P] for k in range(2)],
                                         [w[:, k, 512 * c:512 * c + 512] for k in range(2)], 512) for t in ALL for c in range(2)])
            phase_over(pe, "up")
            pe.wait_ge(*nth("k96_ready", 1))
            for h in range(16):
                if h >= 4:
                    pe.wait_ge(*nth("mtr_ev" + "AD"[h % 2], (h - 4) // 2 + 1))
                for t in (ALL if h < 8 else (0, 1)):
                    src = k96[:, t, h, :] if h < 8 else rowq[:, t, (h - 8) * 96:(h - 8) * 96 + 96]
                    ins = turn(h % 4, t, src, 96)
                ins.then_inc(S("mtr"), 1)
            phase_over(pe, "mprep")
            attention("ml", ml_jobs)
            phase_over(pe, "ml")
            for h in range(16):
                if h >= 4:
                    pe.wait_ge(*nth("dtr_ev" + "AD"[h % 2], (h - 4) // 2 + 1))
                for t in (ALL if h < 8 else (0, 1)):
                    src = (dk[:, t] if h < 8 else dq[:, t])[:, (h % 8) * HD:(h % 8) * HD + HD]
                    ins = turn(h % 4, t, src, HD)
                ins.then_inc(S("dtr"), 1)
            phase_over(pe, "dprep")

            def dscores(n):
                h, t = n // 2, n % 2
                if n >= 2:
                    pe.wait_ge(*nth("df_exp", n - 1))
                for w in range(2):
                    ins = pe.matmul(ps[:, 2 * (n % 2) + w, :], qT1[0:HD, 2 * h + w, t * P:t * P + P], kT1[0:HD, 2 * h + w, :],
                                    start=True, stop=True)
                ins.then_inc(S("df_s"), 1)

            def dturn(n):
                pe.wait_ge(*nth("df_a", n + 1))
                if n >= 2:
                    pe.wait_ge(*nth("df_pt", n - 1))
                for b in range(4):
                    ins = turn(4 + n % 2, b, prob1[:, 2 * (n % 2), b * P:b * P + P])
                ins.then_inc(S("df_t"), 1)

            dscores(0)
            dscores(1)
            dturn(0)
            for n in range(8):
                h = n // 2
                if n + 2 < 8:
                    dscores(n + 2)
                if n + 1 < 8:
                    dturn(n + 1)
                pe.wait_ge(*nth("df_pt", n + 1))
                if n >= 2:
                    pe.wait_ge(*nth("df_o", n - 1))
                for b in range(4):
                    ins = pe.matmul(ps[:, 6 + n % 2, 0:P], probT1[:, n % 2, b * P:b * P + P], dv[:, b, h * P:h * P + P],
                                    start=(b == 0), stop=(b == 3))
                ins.then_inc(S("df_pv"), 1)
            phase_over(pe, "df")
            pe.wait_ge(*nth("subln", 1))
            cat_T("ooutc", lambda t: cat1[:, t - 2, :], LATS)
            pe.wait_ge(*nth("ooutc_evA", 2))
            pe.wait_ge(*nth("ooutc_evD", 2))
            gate_rows("o1", 1)
            phase_over(pe, "ocat")
            out_proj("oout", o_out, LATS, 2)
            pe.drain().then_inc(S("moe_read"), MRING)
            phase_over(pe, "omix")
            norm_T("on2", LATS, xn_l)
            pe.wait_ge(*nth("on2_evA", 2))
            pe.wait_ge(*nth("on2_evD", 2))
            for t in range(2):
                for k in range(KB):
                    ins = pe.matmul(ps[:, 4, t * 8:t * 8 + 8], fT[:, k, t * P:t * P + P], router[:, k, :],
                                    start=(k == 0), stop=(k == KB - 1))
            ins.then_inc(S("logits"), 1)
            pe.wait_ge(*nth("selected", 1))
            pe.matmul(ps[:, 5, 0:8], C("before"), sel[:, 0, :], start=True, stop=True)
            pe.matmul(ps[:, 5, 8:16], ones, sel[:, 0, :], start=True, stop=False)
            pe.matmul(ps[:, 5, 8:16], C("before"), sel[:, 1, :], start=False, stop=True)
            pe.matmul(ps[:, 5, 16:24], ones, sel[:, 0, :], start=True, stop=False)
            pe.matmul(ps[:, 5, 16:24], ones, sel[:, 1, :], start=False, stop=True).then_inc(S("positions"), 1)
            phase_over(pe, "route")
            def gather(it):
                pe.wait_ge(*nth("m_pick", it + 1))
                for k in range(KB):
                    for t in range(2):
                        ins = pe.matmul(ps[:, (7, 3)[k // 4], (k % 4) * P:(k % 4 + 1) * P], xn_l[:, t, k * P:k * P + P], pick[:, t, :],
                                        start=(t == 0), stop=(t == 1))
                ins.then_inc(S("m_gath"), 1)

            gather(0)
            pe.wait_ge(*nth("m_xsA", 1))
            n_passes = passes(pe)
            with pe.Fori(0, n_passes) as it:
                pe.wait_ge(*nth("m_xsL", it + 1))

                def split(n):
                    pe.wait_ge(*nth("m_lo", it * UNITS + (n + 1)))

                def hidden_turn(c):
                    pe.wait_ge(*nth("m_h", it * NCHUNK + (c + 1)))
                    pe.wait_ge(*(nth("m_ht", it * NCHUNK + c) if c else nth("m_pte", it + 1)))
                    for j in range(4):
                        ins = turn(6, j, hrow[:, c % 2, j * P:j * P + P])
                    ins.then_inc(S("m_tr"), 1)

                def down(c):
                    for h in range(2):
                        split(UNIT_OF["d", c, h])
                        if h == 0:
                            pe.wait_ge(*nth("m_ht", it * NCHUNK + (c + 1)))
                        wh, wl = parts_of(UNIT_OF["d", c, h], "d")
                        for f in range(2):
                            first, last = c == 0 and h == 0 and f == 0, c == NCHUNK - 1 and h == 1 and f == 1
                            xh, xl = hTH_r[:, c % 2, 2 * h + f, :], hTL_r[:, c % 2, 2 * h + f, :]
                            for n, (x, w) in enumerate(((xh, wh), (xh, wl), (xl, wh))):
                                for o in range(2):
                                    ins = pe.matmul(ps[:, 4 + o, :], x, w[:, f, 512 * o:512 * o + 512],
                                                    start=first and n == 0, stop=last and n == 2)
                        ins.then_inc(S("moe_read"), 1)

                for c in range(NCHUNK):
                    for w in range(2):
                        if w == 1 and c >= 1:
                            hidden_turn(c - 1)
                        if c >= 2:
                            pe.wait_ge(*nth("m_h", it * NCHUNK + (c - 1)))
                        for h in range(2):
                            n = UNIT_OF["gu"[w], c, h]
                            split(n)
                            wh, wl = parts_of(n, "g")
                            for k in range(4):
                                xh, xl = xsH_r[:, 4 * h + k, :], xsL_r[:, 4 * h + k, :]
                                for m, (x, y) in enumerate(((xh, wh), (xh, wl), (xl, wh))):
                                    ins = pe.matmul(ps[:, 2 * (c % 2) + w, :], x, y[:, k, :],
                                                    start=(h == 0 and k == 0 and m == 0), stop=(h == 1 and k == 3 and m == 2))
                            ins.then_inc(S("moe_read"), 1)
                    if c == 0:
                        pe.wait_ge(*nth("m_acc", it + 1))
                        for t in range(2):
                            ins = turn(6, t, pickw[:, t, :])
                        ins.then_inc(S("m_pt"), 1)
                    if c == NCHUNK - 1:
                        gather(it + 1)
                    if c >= 1:
                        down(c - 1)
                hidden_turn(NCHUNK - 1)
                down(NCHUNK - 1)
                pe.wait_ge(*nth("m_y", it + 1))
                pe.wait_ge(*nth("m_xsL", it + 2))
                for t in range(2):
                    for o in range(2):
                        ins = pe.matmul(ps[:, (2, 6)[t] + o, :], pickT[:, t, :], ysb[:, 512 * o:512 * o + 512], start=True, stop=True)
                ins.then_inc(S("m_sc"), 1)
            pe.wait_ge(*nth("moe_done", 1))
            gate_rows("o3", 1)

        @block.scalar
        def _(act):
            def copy(dst, src):
                return act.activation(dst, src, ACT.Copy)

            def new_squares(tag, residual, tiles):
                for n, t in enumerate(tiles):
                    act.wait_ge(*nth(residual + "_new", n + 1))
                    act.wait_ge(*(nth(tag + "_ss", n) if n else nth(residual + "_sq", 2 * len(tiles))))
                    act.activation(sqj, xr[:, t, :].rearrange("p (a b) -> p a b", a=2), ACT.Square,
                                   accum_out=st[:, n:n + 1]).then_inc(S(tag + "_ss"), 1)

            def norm_T(tag, tiles, shift, dst, parts=False, squared=False):
                def square(n):
                    if n:
                        act.wait_ge(*nth(tag + "_ss", n))
                    act.activation(ps[:, 6:8, :], xr[:, tiles[n], :].rearrange("p (a b) -> p a b", a=2), ACT.Square,
                                   accum_out=st[:, n:n + 1]).then_inc(S(tag + "_ss"), 1)
                if not squared:
                    for n in range(len(tiles)):
                        square(n)
                for n, t in enumerate(tiles):
                    act.wait_ge(*nth(tag + "_tr", 2 * n + 1))
                    for k in range(4):
                        ins = act.activation(dst(t)[:, k, :], ps[:, 2 * (n % 2), k * P:k * P + P], ACT.Identity,
                                             bias=modc[:, shift + k, cond_of(t):cond_of(t) + 1],
                                             scale=scaleA[:, k, cond_of(t):cond_of(t) + 1])
                    ins.then_inc(S(tag + "_evA"), 1)
                    if parts:
                        act.wait_ge(*nth(tag + "_evA", n + 1))
                        act.wait_ge(*nth(tag + "_evD", n + 1))
                        copy(aH_r[:, :, t * P:t * P + P], aT[:, :, t * P:t * P + P]).then_inc(S(tag + "_hi"), 1)

            def cat_T(tag, tiles):
                for n, t in enumerate(tiles):
                    act.wait_ge(*nth(tag + "_tr", 2 * n + 1))
                    copy(aT[:, 0:4, t * P:t * P + P], ps[:, 2 * (n % 2), :].rearrange("p (k n) -> p k n", k=4))\
                        .then_inc(S(tag + "_evA"), 1)

            def gate_rows(tag, conds):
                for n in range(2 * conds):
                    act.wait_ge(*nth(tag + "_gr", n + 1))
                    copy(Gb[:, n // 2, 512 * (n % 2):512 * (n % 2) + 512], ps[:, n, :]).then_inc(S(tag + "_gev"), 1)

            def rows(made, ev, dsts, banks=4, before=lambda g: None):
                for g, d in enumerate(dsts):
                    before(g)
                    if g % 2 == 0:
                        act.wait_ge(*nth(made, g + 1))
                        copy(d, ps[:, g % banks, 0:d.shape[-1]]).then_inc(S(ev + "A"), 1)

            def squares(tag, ready, nt):
                for half in range(2):
                    for t in range(nt):
                        act.wait_ge(*nth(tag[0], ready(half, t)))
                        if half or t:
                            act.wait_ge(*nth(tag[1], half * nt + t))
                        act.activation(sqj[:, t % 2, :], ps[:, 4 * half + t, :], ACT.Square,
                                       accum_out=st[:, 4 * half + t:4 * half + t + 1]).then_inc(S(tag[1]), 1)

            def mod_row(tag, u, bank):
                act.wait_ge(*nth(tag + "_prod", u + 1))
                if u >= 2:
                    act.wait_ge(*nth(tag + "_turned", u - 1))
                copy(mrow[:, u % 2, :], ps[0:2, bank, :]).then_inc(S(tag + "_row"), 1)

            def mod_cols(tag, u, bank):
                act.wait_ge(*nth(tag + "_turned", u + 1))
                copy(modn[:, 4 * u:4 * u + 4, :], ps[:, bank, 0:8].rearrange("p (k c) -> p k c", c=2)).then_inc(S(tag + "_cols"), 1)

            sqj = tmp[:, :, 512:1024]
            act.wait_ge(*nth("cols_ready", 1))
            act.activation(scol[:], cols1[:, 0:16].rearrange("p (c k) -> p c k", c=2), ACT.Silu).then_inc(S("silu_c"), 1)
            act.activation(ea[:], alog, ACT.Exp).then_inc(S("ea"), 1)
            for u in range(12):
                mod_row("emod", u, u % 4)
                if u:
                    mod_cols("emod", u - 1, (u - 1) % 4)
            mod_cols("emod", 11, 3)
            phase_over(act, "emod")
            act.wait_ge(*nth("x_in", 32))
            norm_T("en0", ALL, 0, lambda t: aT[:, :, t * P:t * P + P])
            sil_c = tmp[:, :, 0:512]
            for b in range(12 + 2):
                if b < 12:
                    act.wait_ge(*nth("qkvT_made", b + 1))
                    copy(qkvT[:, b, :, 2:258], ps[:, b % 4, :].rearrange("p (s n) -> p s n", s=2)).then_inc(S("qkvT_ev"), 1)
                if 1 <= b < 13:
                    act.wait_ge(*nth("conv", b))
                    if b >= 3:
                        act.wait_ge(*nth("conv_tr", b - 2))
                    act.activation(sil_c[:, (b - 1) % 2, :], tmp[:, (b - 1) % 2, 512:1024], ACT.Silu).then_inc(S("conv_silu"), 1)
                if b >= 2:
                    act.wait_ge(*nth("conv_tr", b - 1))
                    copy(qkvrow[:, :, (b - 2) * P:(b - 2) * P + P], ps[:, 4 + b % 2, :].rearrange("p (t n) -> p t n", t=4))\
                        .then_inc(S("conv_ev"), 1)
            rows("erow_made", "erow_ev", erow_dst)
            phase_over(act, "eproj")
            for t in ALL:
                if t >= 2:
                    act.wait_ge(*nth("qk_red", t - 1))
                act.activation(tmp[:, t % 2, :], qkvrow[:, t, 0:1024], ACT.Square).then_inc(S("qk_sq"), 1)
            act.wait_ge(*nth("g_abs", 1))
            act.activation(ge_[:], ge_[:], ACT.Exp).then_inc(S("g_e"), 1)
            act.wait_ge(*nth("g_e", 1))
            act.activation(gl_[:], ge_[:], ACT.Ln, bias=1.0).then_inc(S("g_ln"), 1)
            act.activation(gbeta[:], rowbuf[:, :, 528:544], ACT.Exp, scale=-1.0).then_inc(S("b_e"), 1)
            phase_over(act, "gprep")
            MOD_ROW, MOD_COLS = [(1, 1), (3, 0), (5, 0)], [(2, 0), (3, 1), (5, 1)]
            for seg in range(2):
                act.wait_ge(*nth("gh_mm", seg + 1))
                act.activation(eall[:], ps[:, 7, 0:96], ACT.Exp).then_inc(S("gh_exp"), 1)
                for tl in range(2):
                    t = 2 * seg + tl
                    dsts = [kTt[0:HD, 0:4, :], qTt[0:HD, 0:4, :], kbgT[:, tl, 0:4, :], qgT[:, tl, 0:4, :]]
                    for n, d in enumerate(dsts):
                        act.wait_ge(*nth("tr_done", 8 * t + 2 * n + 1))
                        copy(d, ps[0:d.shape[0], 2 * n, :].rearrange("p (h n) -> p h n", h=4)).then_inc(S("tr_evA"), 1)
                    for n in range(4):
                        act.wait_ge(*nth("dec_done", 4 * t + n + 1))
                        dst = Lb[:, n % 2] if n < 2 else AT[:, tl, n % 2]
                        act.activation(dst, ps[:, 2 + n, :], ACT.Exp).then_inc(S("dec_exp"), 1)
                    for lv in range(1, 6):
                        for d in range(2):
                            act.wait_ge(*nth("inv_y", 12 * t + 2 * lv + d + 1))
                            if lv > 1:
                                act.wait_ge(*nth("inv_z0", 8 * t + 2 * (lv - 2) + d + 1))
                            copy(Yb[:, d], ps[:, d, :]).then_inc(S("inv_ye"), 1)
                            if (lv, d) in MOD_ROW:
                                mod_row("omod", 3 * t + MOD_ROW.index((lv, d)), 6)
                            if (lv, d) in MOD_COLS:
                                mod_cols("omod", 3 * t + MOD_COLS.index((lv, d)), 6)
                for n in range(4):
                    N = 4 * seg + n
                    if N:
                        act.wait_ge(*nth("sc_ost", N))
                    act.wait_ge(*nth("sc_o1", N + 1))
                    copy(ox, ps[:, 1, :]).then_inc(S("sc_ox"), 1)
                    act.wait_ge(*nth("sc_v", N + 1))
                    if N:
                        act.wait_ge(*nth("sc_o2", N))
                    copy(vn, ps[:, 2, :]).then_inc(S("sc_vn"), 1)
                phase_over(act, f"seg{seg}")
            act.wait_ge(*nth("o_comb", 8))
            for t in ALL:
                act.activation(o_square[:, t, :], qkvrow[:, t, 0:512], ACT.Square).then_inc(S("o_sq"), 1)
            for t in ALL:
                act.activation(z_gate[:, t, :], rowbuf[:, t, 0:512], ACT.Silu).then_inc(S("z_silu"), 1)
            phase_over(act, "gdn")

            def attention(tag, jobs):
                def exp(n):
                    j = jobs[n]
                    act.wait_ge(*nth(tag + "_m", n + 1))
                    if n >= 2:
                        act.wait_ge(*nth(tag + "_t", n - 1))
                    nm = st[:, 8 + n % 4:9 + n % 4]
                    if j["sink"] is not None:
                        act.activation(st[:, 16 + n % 4:17 + n % 4], j["sink"], ACT.Exp, bias=nm)
                    act.activation(prob[:, n % 2, 0:j["nk"]], ps[:, n % 2, 0:j["nk"]], ACT.Exp, bias=nm, scale=j["scale"],
                                   accum_out=st[:, 12 + n % 4:13 + n % 4]).then_inc(S(tag + "_exp"), 1)

                def turned_out(n):
                    nk = jobs[n]["nk"]
                    act.wait_ge(*nth(tag + "_t", n + 1))
                    if n >= 2:
                        act.wait_ge(*nth(tag + "_pv", n - 1))
                    copy(probT[:, n % 2, 0:nk], ps[:, 2 + n % 2, 0:nk]).then_inc(S(tag + "_pt"), 1)

                exp(0)
                exp(1)
                turned_out(0)
                for n in range(len(jobs)):
                    if n + 2 < len(jobs):
                        exp(n + 2)
                    if n + 1 < len(jobs):
                        turned_out(n + 1)

            def turned(tr, ev, dsts):
                for h, d in enumerate(dsts):
                    if h % 2 == 0:
                        act.wait_ge(*nth(tr, h + 1))
                        copy(d, ps[0:d.shape[0], h % 4, 0:d.shape[-1]]).then_inc(S(ev + "A"), 1)

            turned("swtr", "swtr_ev", sw_dst)
            phase_over(act, "swprep")
            attention("sw", sw_jobs)
            phase_over(act, "sw")
            cat_T("eoutc", ALL)
            gate_rows("e1", 2)
            phase_over(act, "ecat")
            squares(("eout_made", "e1_sq"), lambda half, t: 4 * half + t + 1, 4)
            new_squares("en2", "e1", ALL)
            phase_over(act, "eout")
            def gu_high(i):
                arrived(act, e_gu[i])
                if i >= 2:
                    act.wait_ge(*nth("gu_made", 2 * i - 2))
                copy(slot_r[2 + i % 2][:], slot[slot_of[e_gu[i]]]).then_inc(S("gu_hi"), 1)

            def down_high(at):
                arrived(act, e_down[at])
                if at >= 3:
                    act.wait_ge(*nth("down_step", at - 2))
                elif at == 0:
                    act.wait_ge(*nth("gu_made", 20))
                copy(slot_r[DOWN_SPLIT[at]][:], slot[slot_of[e_down[at]]]).then_inc(S("down_hi"), 1)

            def hidden_highs(ks):
                for k in ks:
                    copy(hidden_high(k), hTd[:, k, :]).then_inc(S("hidden_hi"), 1)

            gu_high(0)
            norm_T("en2", ALL, 24, lambda t: aT[:, :, t * P:t * P + P], parts=True, squared=True)
            for b in range(22):
                if b % 2 == 0 and b < 20:
                    gu_high(b // 2 + 1)
                act.wait_ge(*nth("gu_made", b + 1))
                if b >= 2:
                    act.wait_ge(*nth("gu_h", b - 1))
                act.activation(sil[:, b % 2, :], ps[:, b % 2, :], ACT.Silu).then_inc(S("gu_silu"), 1)
                if b == 20:
                    down_high(0)
            gate_rows("e3", 2)
            phase_over(act, "egu")
            hidden_highs(range(0, 8))
            down_high(1)
            hidden_highs(range(8, HIDDEN_SPLIT))
            down_high(3)
            down_high(4)
            squares(("down_step", "e3_sq"), lambda half, t: 3 * half + 3, 4)
            new_squares("on0", "e3", ALL)
            phase_over(act, "edown")

            def oin_high(n):
                arrived(act, o_in[n])
                if n >= 2:
                    act.wait_ge(*nth("orow_made", o_made[n - 2]))
                used = KB * (O_CH[n][1] - O_CH[n][0])
                copy(slot_r[n % 2][:, 0:used], slot[slot_of[o_in[n]]][:, 0:used]).then_inc(S("oin_hi"), 1)

            oin_high(0)
            norm_T("on0", ALL, 0, lambda t: aT[:, :, t * P:t * P + P], parts=True, squared=True)
            oin_high(1)
            rows("orow_made", "orow_ev", orow_dst, before=lambda g: oin_high(OIN_AT[g]) if g in OIN_AT else None)
            phase_over(act, "oproj")
            for t in range(2):
                act.activation(tmp[:, t, 0:384], cq[:, t, :], ACT.Square, accum_out=st[:, t:t + 1])
            for t in ALL:
                ins = act.activation(tmp[:, t % 2, 384 + 256 * (t // 2):640 + 256 * (t // 2)], ckvkr[:, t, 0:256], ACT.Square, accum_out=st[:, 2 + t:3 + t])
            ins.then_inc(S("lr_sq"), 1)
            phase_over(act, "lowr")
            rows("uq_made", "uq_ev", uq_dst)
            rows("ukv_made", "ukv_ev", ukv_dst)
            phase_over(act, "up")
            turned("mtr", "mtr_ev", mtr_dst)
            phase_over(act, "mprep")
            attention("ml", ml_jobs)
            phase_over(act, "ml")
            act.wait_ge(*nth("lam_s", 1))
            act.activation(lam[:, 0:2], lam[:, 0:2], ACT.Exp).then_inc(S("lam_e"), 1)
            turned("dtr", "dtr_ev", dtr_dst)
            phase_over(act, "dprep")

            def dexp(n):
                act.wait_ge(*nth("df_m", n + 1))
                if n >= 2:
                    act.wait_ge(*nth("df_t", n - 1))
                for w in range(2):
                    ins = act.activation(prob1[:, 2 * (n % 2) + w, :], ps[:, 2 * (n % 2) + w, :], ACT.Exp,
                                         bias=st[:, 8 + 2 * (n % 2) + w:9 + 2 * (n % 2) + w], scale=HD ** -0.5,
                                         accum_out=st[:, 12 + 2 * (n % 2) + w:13 + 2 * (n % 2) + w])
                ins.then_inc(S("df_exp"), 1)

            def dturned(n):
                act.wait_ge(*nth("df_t", n + 1))
                if n >= 2:
                    act.wait_ge(*nth("df_pv", n - 1))
                copy(probT1[:, n % 2, :], ps[:, 4 + n % 2, :]).then_inc(S("df_pt"), 1)
            dexp(0)
            dexp(1)
            dturned(0)
            for n in range(8):
                if n + 2 < 8:
                    dexp(n + 2)
                if n + 1 < 8:
                    dturned(n + 1)
            phase_over(act, "df")
            for t in range(2):
                ins = act.activation(tmp[:, t, 0:512], cat1[:, t, 512:1024], ACT.Square)
            ins.then_inc(S("sub_sq"), 1)
            cat_T("ooutc", LATS)
            gate_rows("o1", 1)
            phase_over(act, "ocat")
            squares(("oout_made", "o1_sq"), lambda half, t: 2 * half + t + 1, 2)
            new_squares("on2", "o1", LATS)
            phase_over(act, "omix")
            norm_T("on2", LATS, 24, lambda t: fT[:, :, (t - 2) * P:(t - 1) * P], squared=True)
            act.wait_ge(*nth("lg_sub", 1))
            act.activation(gate, gate, ACT.Exp).then_inc(S("lg_exp"), 1)
            phase_over(act, "route")
            def gathered(it):
                act.wait_ge(*nth("m_gath", it + 1))
                for k in range(4):
                    ins = act.activation(xsT[:, k, :], ps[:, 7, k * P:k * P + P], ACT.Identity,
                                         bias=modc[:, 24 + k, 0:1], scale=scaleA[:, k, 0:1])
                ins.then_inc(S("m_xsA"), 1)
                act.wait_ge(*nth("m_xsA", it + 1))
                act.wait_ge(*nth("m_xsD", it + 1))
                copy(xsH_r, xsT).then_inc(S("m_xsH"), 1)

            gathered(0)
            n_passes = passes(act)
            with act.Fori(0, n_passes) as it:
                def split(n):
                    act.wait_ge(*nth(f"mlanded{n % MRING}", it * (UNITS // MRING * 16) + (16 * (n // MRING) + 16)))
                    act.wait_ge(*nth("moe_read", it * UNITS + (n + 1 + MRING - HRING)))
                    copy(hslot_r[n % HRING], wslot[n % MRING]).then_inc(S("m_hi"), 1)

                for n in range(UNITS):
                    split(n)
                    for c, what in BESIDE[n]:
                        if what == "gated":
                            act.wait_ge(*nth("moe_read", it * UNITS + (MRING + UNIT_OF["u", c, 1] + 1)))
                            if c >= 2:
                                act.wait_ge(*nth("m_h", it * NCHUNK + (c - 1)))
                            act.activation(msil[:, c % 2, :], ps[:, 2 * (c % 2), :], ACT.Silu).then_inc(S("m_silu"), 1)
                        elif what == "weights":
                            act.wait_ge(*nth("m_pt", it + 1))
                            copy(pickT, ps[:, 6, 0:256].rearrange("p (a b) -> p a b", a=2)).then_inc(S("m_pte"), 1)
                        elif what == "gathered":
                            gathered(it + 1)
                        elif what == "turned":
                            act.wait_ge(*nth("m_tr", it * NCHUNK + (c + 1)))
                            if c >= 2:
                                act.wait_ge(*nth("moe_read", it * UNITS + (MRING + UNIT_OF["d", c - 2, 1] + 1)))
                            copy(hTH_r[:, c % 2, :, :], ps[:, 6, :].rearrange("p (a b) -> p a b", a=4)).then_inc(S("m_htH"), 1)
                act.wait_ge(*nth("moe_read", it * UNITS + (MRING + UNITS)))
                for o in range(2):
                    ins = copy(ysb[:, 512 * o:512 * o + 512], ps[:, 4 + o, :])
                ins.then_inc(S("m_y"), 1)
            act.wait_ge(*nth("moe_done", 1))
            for t in range(2):
                act.activation(ps[:, 4 + 2 * t:6 + 2 * t, :], moe[:, t, :].rearrange("p (a b) -> p a b", a=2), ACT.Square,
                               accum_out=st[:, t:t + 1]).then_inc(S("o3_sq"), 1)
            gate_rows("o3", 1)

        @block.vector
        def _(v):
            tallies = {}

            def tally(name):
                if name not in tallies:
                    tallies[name] = Tally(S(name))
                return tallies[name]

            def link(ins, name="dve_order"):
                tally(name).add(ins)
                v.wait_ge(*nth(name, tally(name).n))

            def signal(ins, name):
                tally(name).add(ins)

            def power(dst, src, eps):
                n = src.shape[1] * (src.shape[2] if len(src.shape) == 3 else 1)
                x, y, w = rs[:, 0, 0:n], rs[:, 1, 0:n], rs[:, 2, 0:n]
                like = lambda b: b.rearrange("p (t h) -> p t h", h=src.shape[2]) if len(src.shape) == 3 else b
                link(v.tensor_scalar(like(x), src, eps, None, ALU.add))
                link(v.tensor_scalar(w.bitcast(I32), x.bitcast(I32), 1, None, ALU.logical_shift_right))
                link(v.tensor_scalar(y.bitcast(I32), w.bitcast(I32), -1.0, float(0x5f3759df), ALU.mult, ALU.add))
                for step in range(3):
                    if n == 1:
                        link(v.tensor_scalar(w, y, y, x, ALU.mult, ALU.mult))
                    else:
                        link(v.tensor_tensor(w, y, y, ALU.mult))
                        link(v.tensor_tensor(w, w, x, ALU.mult))
                    link(v.tensor_scalar(w, w, -0.5, 1.5, ALU.mult, ALU.add))
                    link(v.tensor_tensor(dst if step == 2 else like(y), like(y), like(w), ALU.mult))

            def norm_T(tag, tiles, shift, dst, buf=tmp, parts=False):
                def normed(n):
                    if n >= 2:
                        v.wait_ge(*nth(tag + "_tr", 2 * n - 2))
                    signal(v.tensor_scalar(buf[:, n % 2, :], xr[:, tiles[n], :], st[:, 16 + n:17 + n], SQRT_D, ALU.mult, ALU.mult),
                           tag + "_xn")
                def rest(n):
                    ts = slice(tiles[n] * P, tiles[n] * P + P)
                    v.wait_ge(*nth(tag + "_hi", n + 1))
                    signal(v.tensor_tensor(aL_r[:, :, ts], aT[:, :, ts], aH[:, :, ts], ALU.subtract), tag + "_lo")

                v.wait_ge(*nth(tag + "_ss", len(tiles)))
                power(st[:, 16:16 + len(tiles)], st[:, 0:len(tiles)], D * EPS)
                normed(0)
                for n, t in enumerate(tiles):
                    if n + 1 < len(tiles):
                        normed(n + 1)
                    v.wait_ge(*nth(tag + "_tr", 2 * n + 2))
                    c = cond_of(t)
                    for k in range(4, 8):
                        ins = v.tensor_scalar(dst(t)[:, k, :], ps[:, 2 * (n % 2) + 1, (k - 4) * P:(k - 3) * P],
                                              scaleA[:, k, c:c + 1], modc[:, shift + k, c:c + 1], ALU.mult, ALU.add)
                    signal(ins, tag + "_evD")
                    if parts and n:
                        rest(n - 1)
                if parts:
                    rest(len(tiles) - 1)

            def cat_T(tag, tiles):
                for n, t in enumerate(tiles):
                    v.wait_ge(*nth(tag + "_tr", 2 * n + 2))
                    signal(v.tensor_copy(aT[:, 4:8, t * P:t * P + P], ps[:, 2 * (n % 2) + 1, :].rearrange("p (k n) -> p k n", k=4)),
                           tag + "_evD")

            def new_modulation(tag, bias):
                v.wait_ge(*nth(tag + "_cols", 12))
                link(v.tensor_tensor(modc[:], modn[:], bch(bias, 2), ALU.add))

            def scale_columns(at, norms):
                link(v.scalar_tensor_tensor(scaleA[:], modc[:, at:at + 8, :], 1.0, bch(norms, 2), ALU.add, ALU.mult))

            def gate_diag(tag, at, norms, conds):
                link(v.scalar_tensor_tensor(gatec[:], modc[:, at:at + 8, :], SQRT_D, bch(norms, 2), ALU.mult, ALU.mult))
                for c in range(conds):
                    ins = v.tensor_tensor(tmp[:, c, :].rearrange("p (k j) -> p k j", k=KB), bcm(ident, KB),
                                          bch(gatec[:, :, c], P), ALU.mult)
                    (signal if c == conds - 1 else lambda i, _n: link(i))(ins, tag + "_diag")

            def rows(made, ev, dsts, banks=4, before=lambda g: None):
                for g, d in enumerate(dsts):
                    before(g)
                    if g % 2 == 1:
                        v.wait_ge(*nth(made, g + 1))
                        signal(v.tensor_copy(d, ps[:, g % banks, 0:d.shape[-1]]), ev + "D")

            def turned(tr, ev, dsts):
                for h, d in enumerate(dsts):
                    if h % 2 == 1:
                        v.wait_ge(*nth(tr, h + 1))
                        signal(v.tensor_copy(d, ps[0:d.shape[0], h % 4, 0:d.shape[-1]]), ev + "D")

            def residual(tag, tiles, gate_tag, gates, at_once=False):
                nt = len(tiles)
                v.wait_ge(*nth(gate_tag + "_gev", gates))
                for t in range(nt):
                    if t == 0 or not at_once:
                        n = nt if at_once else 1
                        v.wait_ge(*nth(tag, nt + t + n))
                        link(v.tensor_tensor(st[:, 24 + t:24 + t + n], st[:, t:t + n], st[:, 4 + t:4 + t + n], ALU.add))
                        power(st[:, 28 + t:28 + t + n], st[:, 24 + t:24 + t + n], D * EPS)
                    c = cond_of(tiles[t])
                    for half in range(2):
                        hs = slice(512 * half, 512 * half + 512)
                        link(v.scalar_tensor_tensor(tmp[:, half, 0:512], ps[:, 4 * half + t, :], st[:, 28 + t:29 + t],
                                                    Gb[:, c, hs], ALU.mult, ALU.mult))
                        ins = v.tensor_tensor(xr[:, tiles[t], hs], xr[:, tiles[t], hs], tmp[:, half, 0:512], ALU.add)
                        link(ins, gate_tag + "_new") if half else link(ins)

            def rope(x, cos, sin, heads, n, t, b1, b2):
                q = n // 4
                b1v = b1[:, 0:heads * n].rearrange("p (h d) -> p h d", h=heads)
                b2v = b2[:, 0:heads * n].rearrange("p (h a b q) -> p h a b q", h=heads, a=2, b=2)
                xs = x.rearrange("p h (a b q) -> p h a b q", a=2, b=2)
                ss = sin[:, t, :].rearrange("p (a b q) -> p a b q", a=2, b=2)
                link(v.tensor_tensor(b1v, x, bcm(cos[:, t, :], heads), ALU.mult))
                for b in range(2):
                    link(v.tensor_tensor(b2v[:, :, :, b, :], xs[:, :, :, 1 - b, :],
                                         ss[:, :, b, :].unsqueeze(1).to_broadcast([P, heads, 2, q]), ALU.mult))
                link(v.tensor_tensor(x, b1v, b2[:, 0:heads * n].rearrange("p (h d) -> p h d", h=heads), ALU.add))

            v.wait_ge(*nth("cols_tr", 1))
            v.tensor_copy(cols1[:, 0:112], ps[:, 0, 0:112])
            v.tensor_copy(cols2[:, 0:124], ps[:, 0, P:P + 124])
            link(v.tensor_copy(cols3[:, 0:5], ps[:, 0, 256:261]), "cols_ready")
            link(v.tensor_scalar(nsink[:], sink, -1.0, None, ALU.mult))
            link(v.tensor_scalar(gdnw, gdnw, float(np.sqrt(HD)), None, ALU.mult))
            link(v.tensor_scalar(subln, subln, float(np.sqrt(2 * HD)) * (1.0 - LAM_INIT), None, ALU.mult))
            new_modulation("emod", cols1[:, 16:64])
            scale_columns(8, cols2[:, 0:8])
            phase_over(v, "emod")
            v.memset(qkvT[:, :, :, 0:2], 0.0)
            link(v.memset(qkvT[:, :, :, 258:260], 0.0))
            v.wait_ge(*nth("x_in", 32))
            norm_T("en0", ALL, 0, lambda t: aT[:, :, t * P:t * P + P])
            for b in range(12):
                v.wait_ge(*nth("qkvT_ev", b + 1))
                if b >= 2:
                    v.wait_ge(*nth("conv_silu", b - 1))
                else:
                    v.wait_ge(*nth("en0_tr", 8))
                acc = tmp[:, b % 2, 512:1024].rearrange("p (s n) -> p s n", s=2)
                link(v.tensor_scalar(acc, qkvT[:, b, :, 0:256], cols2[:, 64 + b:65 + b], None, ALU.mult))
                for j in range(1, 5):
                    ins = v.scalar_tensor_tensor(acc, qkvT[:, b, :, j:j + 256], cols2[:, 64 + 12 * j + b:65 + 12 * j + b], acc,
                                                 ALU.mult, ALU.add)
                    if j < 4:
                        link(ins)
                signal(ins, "conv")
            rows("erow_made", "erow_ev", erow_dst)
            phase_over(v, "eproj")
            link(v.tensor_tensor(gx[:], rowbuf[:, :, 512:528], bcm(dtb, TILES), ALU.add))
            signal(v.scalar_tensor_tensor(ge_[:], gx[:], -1.0, gx[:], ALU.mult, ALU.min), "g_abs")
            for t in ALL:
                v.wait_ge(*nth("qk_sq", t + 1))
                link(v.tensor_reduce(gst[:, t, :], tmp[:, t % 2, :].rearrange("p (h d) -> p h d", h=16), AXX, ALU.add), "qk_red")
            power(gst[:], gst[:], EPS)
            link(v.tensor_scalar(gst[:, :, 0:8], gst[:, :, 0:8], HD ** -0.5, None, ALU.mult))
            for t in ALL:
                x = qkvrow[:, t, 0:1024].rearrange("p (h d) -> p h d", h=16)
                link(v.tensor_tensor(x, x, bch(gst[:, t, :], HD), ALU.mult))
            v.wait_ge(*nth("g_ln", 1))
            v.wait_ge(*nth("ea", 1))
            link(v.scalar_tensor_tensor(gg[:], gx[:], 0.0, gl_[:], ALU.max, ALU.add))
            link(v.scalar_tensor_tensor(gg[:], gg[:], -1.0, bcm(ea[:], TILES), ALU.mult, ALU.mult))
            v.wait_ge(*nth("b_e", 1))
            link(v.tensor_scalar(gbeta[:], gbeta[:], 1.0, None, ALU.add))
            link(v.reciprocal(gbeta[:], gbeta[:]))
            phase_over(v, "gprep")
            link(v.memset(Sst, 0.0), "sc_s")
            mask_l, mask_a = (C("gt_c"), C("lt_c")), (C("le_c"), C("ge_c"))
            eye_c = C("eye_c")
            for seg in range(2):
                v.wait_ge(*nth("gh_exp", seg + 1))
                for tl in range(2):
                    t = 2 * seg + tl
                    if tl:
                        v.wait_ge(*nth("tr_done", 8 * t))
                    q_, k_, v_ = (qkvrow[:, t, 512 * n:512 * n + 512].rearrange("p (h d) -> p h d", h=HEADS) for n in range(3))
                    link(v.tensor_tensor(bg[:, tl, :], gbeta[:, t, :], eall[:, 32 * tl:32 * tl + 16], ALU.mult))
                    for dst, x, f in ((kbgrow, k_, bg[:, tl, :]), (qgrow, q_, eall[:, 32 * tl:32 * tl + 16])):
                        for d in range(2):
                            ins = v.tensor_tensor(dst[:, :, d, :], x, bch(f[:, 8 * d:8 * d + 8], HD), ALU.mult)
                        signal(ins, "row_ready")
                    for b in range(2):
                        v.wait_ge(*nth("tr_done", 8 * t + 2 * b + 2))
                        signal(v.tensor_copy((kTt, qTt)[b][0:HD, 4:8, :], ps[0:HD, 2 * b + 1, :].rearrange("p (h n) -> p h n", h=4)),
                               "tr_evD")
                    for b in range(2):
                        v.wait_ge(*nth("tr_done", 8 * t + 4 + 2 * b + 2))
                        signal(v.tensor_copy((kbgT, qgT)[b][:, tl, 4:8, :], ps[:, 5 + 2 * b, :].rearrange("p (h n) -> p h n", h=4)),
                               "tr_evD")
                    for n in range(4):
                        d = n % 2
                        signal(v.tensor_tensor(hv(rhsb[n]), bch(gg[:, t, 8 * d:8 * d + 8], CH),
                                               bcm((mask_l, mask_a)[n // 2][d], HEADS), ALU.mult), "rhs_ready")
                    v.wait_ge(*nth("gram_done", 2 * t + 1))
                    for d in range(2):
                        v.wait_ge(*nth("dec_exp", 4 * t + 1 + d))
                        link(v.tensor_tensor(Lb[:, d], Lb[:, d], ps[:, 0, :], ALU.mult))
                        link(v.tensor_tensor(hv(Lb[:, d]), hv(Lb[:, d]), bch(gbeta[:, t, 8 * d:8 * d + 8], CH), ALU.mult))
                    def attend(d):
                        v.wait_ge(*nth("gram_done", 2 * t + 2))
                        v.wait_ge(*nth("dec_exp", 4 * t + 3 + d))
                        link(v.tensor_tensor(AT[:, tl, d], AT[:, tl, d], ps[:, 7, :], ALU.mult))
                        link(v.tensor_tensor(hv(AT[:, tl, d]), hv(AT[:, tl, d]), bcm(mask_a[d], HEADS), ALU.mult))

                    def tails(d):
                        link(v.tensor_tensor(hv(kt[:, tl, d]), k_, bch(eall[:, 32 * tl + 16 + 8 * d:32 * tl + 24 + 8 * d], HD), ALU.mult))
                        for c in range(2):
                            cs = slice(c * CH, c * CH + CH)
                            s = 2 * tl + c if d == 0 else 3 - (2 * tl + c)
                            link(v.tensor_tensor(hv(vbst[cs, s, :]), v_[cs], bch(gbeta[cs, t, 8 * d:8 * d + 8], HD), ALU.mult))

                    def level_blocks(lv, d):
                        link(v.tensor_tensor(hv(Cb[:, d]), hv(Lb[:, d]), bcm(levels[:, d, lv, :], HEADS), ALU.mult), "inv_c")

                    for d in range(2):
                        level_blocks(0, d)
                    for lv in range(6):
                        for d in range(2):
                            v.wait_ge(*nth("inv_y", 12 * t + 2 * lv + d + 1))
                            if lv == 0:
                                link(v.tensor_tensor(hv(Xb[:, d]), bcm(eye_c, HEADS), hv(Cb[:, d]), ALU.subtract), "inv_x0")
                                link(v.tensor_tensor(hv(XT[:, tl, d]), bcm(eye_c, HEADS), hv(ps[:, d, :]), ALU.subtract), "inv_x")
                            if lv < 5:
                                level_blocks(lv + 1, d)
                        if lv < 4:
                            (attend, tails)[lv // 2](lv % 2)
                        if lv == 0:
                            continue
                        for d in range(2):
                            v.wait_ge(*nth("inv_z", 10 * t + 2 * (lv - 1) + d + 1))
                            link(v.tensor_tensor(XT[:, tl, d], XT[:, tl, d], ps[:, 4 + d, :], ALU.subtract), "inv_x")
                        for d in range(2):
                            if lv < 5:
                                v.wait_ge(*nth("inv_z0", 8 * t + 2 * (lv - 1) + d + 1))
                                link(v.tensor_tensor(Xb[:, d], Xb[:, d], ps[:, 2 + d, :], ALU.subtract), "inv_x0")
                for n in range(4):
                    N = 4 * seg + n
                    v.wait_ge(*nth("sc_p", N + 1))
                    signal(v.tensor_tensor(rr, vbst[:, n, :], ps[:, 0, :], ALU.subtract), "sc_r")
                    v.wait_ge(*nth("sc_o1", N + 1))
                    link(v.tensor_tensor(hv(Sst), hv(Sst), bch(eall[:, 64 + 8 * n:72 + 8 * n], HD), ALU.mult))
                    v.wait_ge(*nth("sc_u", N + 1))
                    link(v.tensor_tensor(Sst, Sst, ps[:, 4, :], ALU.add), "sc_s")
                    v.wait_ge(*nth("sc_ox", N + 1))
                    v.wait_ge(*nth("sc_o2", N + 1))
                    link(v.tensor_tensor(ostep[:, n, :], ox, ps[:, 3, :], ALU.add), "sc_ost")
                for s in range(4):
                    cs = slice((s % 2) * CH, (s % 2) * CH + CH)
                    link(v.tensor_tensor(qkvrow[cs, 2 * seg + s // 2, 0:512], ostep[cs, s, :], ostep[cs, 3 - s, :], ALU.add), "o_comb")
                phase_over(v, f"seg{seg}")
            for t in ALL:
                v.wait_ge(*nth("o_sq", t + 1))
                link(v.tensor_reduce(st[:, 8 * t:8 * t + 8], hv(o_square[:, t, :]), AXX, ALU.add))
            power(st[:, 32:64], st[:, 0:32], HD * EPS)
            for t in ALL:
                o = qkvrow[:, t, 0:512]
                link(v.tensor_tensor(hv(o), hv(o), bch(st[:, 32 + 8 * t:40 + 8 * t], HD), ALU.mult))
                link(v.tensor_tensor(hv(o), hv(o), bcm(gdnw, HEADS), ALU.mult))
                v.wait_ge(*nth("z_silu", t + 1))
                link(v.tensor_tensor(o, o, z_gate[:, t, :], ALU.mult), "o_done")
            phase_over(v, "gdn")

            def attention(tag, jobs):
                def maxes(n):
                    j = jobs[n]
                    v.wait_ge(*nth(tag + "_s", n + 1))
                    if j["mask"] is not None:
                        link(v.tensor_tensor(ps[:, n % 2, 256:512], ps[:, n % 2, 256:512], j["mask"], ALU.add))
                    link(v.tensor_reduce(st[:, 24 + n % 4:25 + n % 4], ps[:, n % 2, 0:j["nk"]], AXX, ALU.max))
                    nm, mx = st[:, 8 + n % 4:9 + n % 4], st[:, 24 + n % 4:25 + n % 4]
                    if j["sink"] is not None:
                        signal(v.tensor_scalar(nm, mx, -j["scale"], j["nsink"], ALU.mult, ALU.min), tag + "_m")
                    else:
                        signal(v.tensor_scalar(nm, mx, -j["scale"], None, ALU.mult), tag + "_m")
                maxes(0)
                maxes(1)
                for n, j in enumerate(jobs):
                    if n + 2 < len(jobs):
                        maxes(n + 2)
                    v.wait_ge(*nth(tag + "_exp", n + 1))
                    den = st[:, 12 + n % 4:13 + n % 4]
                    if j["sink"] is not None:
                        link(v.tensor_tensor(st[:, 28 + n % 4:29 + n % 4], den, st[:, 16 + n % 4:17 + n % 4], ALU.add))
                        den = st[:, 28 + n % 4:29 + n % 4]
                    link(v.reciprocal(st[:, 20 + n % 4:21 + n % 4], den))
                    v.wait_ge(*nth(tag + "_pv", n + 1))
                    signal(v.tensor_scalar(j["out"], ps[:, 4 + n % 2, 0:j["vw"]], st[:, 20 + n % 4:21 + n % 4], None, ALU.mult),
                           tag + "_o")

            for t in LATS:
                rope(rowbuf[:, t, 544:1184].rearrange("p (h d) -> p h d", h=10), cos64, sin64, 10, HD, t - 2, rt1, rt2)
            v.drain().then_inc(S("swrope"), 1)
            turned("swtr", "swtr_ev", sw_dst)
            phase_over(v, "swprep")
            attention("sw", sw_jobs)
            phase_over(v, "sw")
            cat_T("eoutc", ALL)
            gate_diag("e1", 16, cols2[:, 8:16], 2)
            phase_over(v, "ecat")
            residual("e1_sq", ALL, "e1", 4)
            scale_columns(32, cols2[:, 16:24])
            phase_over(v, "eout")
            def gu_rest(i):
                v.wait_ge(*nth("gu_hi", i + 1))
                s = slot_of[e_gu[i]]
                signal(v.tensor_tensor(slot_r[s][:], slot[s], slot_r[2 + i % 2].bitcast(F32), ALU.subtract), "gu_lo")

            def down_rest(at):
                v.wait_ge(*nth("down_hi", list(DOWN_SPLIT).index(at) + 1))
                s = slot_of[e_down[at]]
                signal(v.tensor_tensor(slot_r[s][:], slot[s], slot_r[DOWN_SPLIT[at]].bitcast(F32), ALU.subtract), "down_lo")

            def hidden_rests(ks):
                for k in ks:
                    v.wait_ge(*nth("hidden_hi", k + 1))
                    signal(v.tensor_tensor(hidL_r[:, k, :], hTd[:, k, :], hidden_high(k).bitcast(F32), ALU.subtract), "hidden_lo")

            gu_rest(0)
            norm_T("en2", ALL, 24, lambda t: aT[:, :, t * P:t * P + P], parts=True)
            for b in range(22):
                if b % 2 == 0 and b < 20:
                    gu_rest(b // 2 + 1)
                v.wait_ge(*nth("gu_silu", b + 1))
                signal(v.tensor_tensor(hTd[:, b, :], sil[:, b % 2, :], ps[:, 4 + b % 2, :], ALU.mult), "gu_h")
                if b == 20:
                    down_rest(0)
            gate_diag("e3", 40, cols2[:, 24:32], 2)
            phase_over(v, "egu")
            hidden_rests(range(0, 8))
            down_rest(1)
            hidden_rests(range(8, HIDDEN_SPLIT))
            down_rest(3)
            down_rest(4)
            residual("e3_sq", ALL, "e3", 4, at_once=True)
            new_modulation("omod", cols1[:, 64:112])
            scale_columns(8, cols2[:, 32:40])
            phase_over(v, "edown")

            def oin_rest(n):
                v.wait_ge(*nth("oin_hi", n + 1))
                s, used = slot_of[o_in[n]], KB * (O_CH[n][1] - O_CH[n][0])
                signal(v.tensor_tensor(slot_r[s][:, 0:used], slot[s][:, 0:used], slot_r[n % 2][:, 0:used].bitcast(F32), ALU.subtract),
                       "oin_lo")

            oin_rest(0)
            norm_T("on0", ALL, 0, lambda t: aT[:, :, t * P:t * P + P], parts=True)
            oin_rest(1)
            rows("orow_made", "orow_ev", orow_dst, before=lambda g: oin_rest(OIN_AT[g]) if g in OIN_AT else None)
            phase_over(v, "oproj")
            v.wait_ge(*nth("lr_sq", 1))
            power(st[:, 16:18], st[:, 0:2], 384 * EPS)
            power(st[:, 18:22], st[:, 2:6], 256 * EPS)
            for t in range(2):
                link(v.tensor_scalar(cq[:, t, :], cq[:, t, :], st[:, 16 + t:17 + t], float(np.sqrt(384)), ALU.mult, ALU.mult))
            for t in ALL:
                ins = v.tensor_scalar(ckvkr[:, t, 0:256], ckvkr[:, t, 0:256], st[:, 18 + t:19 + t], 16.0, ALU.mult, ALU.mult)
                (signal if t == 3 else lambda i, _n: link(i))(ins, "lowrank")
            v.wait_ge(*nth("lr_tr", 1))
            for j in range(3):
                link(v.tensor_scalar(cqT[:, j, :], ps[:, j, 0:256], cols3[:, j:j + 1], None, ALU.mult))
            v.wait_ge(*nth("lr_tr", 2))
            for j in range(2):
                link(v.tensor_scalar(ckvT[:, j, :], ps[:, 3 + j, :], cols3[:, 3 + j:4 + j], None, ALU.mult))
            phase_over(v, "lowr")
            rows("uq_made", "uq_ev", uq_dst)
            rows("ukv_made", "ukv_ev", ukv_dst)
            phase_over(v, "up")
            for t in range(2):
                rope(rowq[:, t, :].rearrange("p (h d) -> p h d", h=HEADS)[:, :, 64:96], cos32, sin32, HEADS, 32, t, rt3, rt4)
                rope(ckvkr[:, 2 + t, 256:288].rearrange("p (h d) -> p h d", h=1), cos32, sin32, 1, 32, t, rt3, rt4)
                rope(hv(dq[:, t, :]), cos64, sin64, HEADS, HD, t, rt3, rt4)
                rope(hv(dk[:, 2 + t, :]), cos64, sin64, HEADS, HD, t, rt3, rt4)
            for t in ALL:
                link(v.tensor_copy(k96[:, t, :, 0:64], hv(rowkv[:, t, :])[:, :, 0:64]))
                ins = v.tensor_copy(k96[:, t, :, 64:96], bcm(ckvkr[:, t, 256:288], HEADS))
                (signal if t == 3 else lambda i, _n: link(i))(ins, "k96_ready")
            turned("mtr", "mtr_ev", mtr_dst)
            phase_over(v, "mprep")
            attention("ml", ml_jobs)
            phase_over(v, "ml")
            lp = lamv.rearrange("p (a b d) -> p a b d", a=2, b=2)
            lbuf = M(BZ + 7168, 2, HD)
            link(v.tensor_tensor(lbuf, lp[:, :, 0, :], lp[:, :, 1, :], ALU.mult))
            signal(v.tensor_reduce(lam[:, 0:2], lbuf, AXX, ALU.add), "lam_s")
            v.wait_ge(*nth("lam_e", 1))
            link(v.tensor_tensor(lam[:, 2:3], lam[:, 1:2], lam[:, 0:1], ALU.subtract))
            link(v.tensor_scalar(lam[:, 3:4], lam[:, 2:3], -LAM_INIT, None, ALU.add))
            turned("dtr", "dtr_ev", dtr_dst)
            phase_over(v, "dprep")

            def dmax(n):
                v.wait_ge(*nth("df_s", n + 1))
                b = 2 * (n % 2)
                link(v.tensor_reduce(st[:, 24 + b:26 + b], ps[:, b:b + 2, :], AXX, ALU.max))
                signal(v.tensor_scalar(st[:, 8 + b:10 + b], st[:, 24 + b:26 + b], -HD ** -0.5, None, ALU.mult), "df_m")

            def dcombine(n):
                b = 2 * (n % 2)
                v.wait_ge(*nth("df_exp", n + 1))
                link(v.reciprocal(st[:, 16:18], st[:, 12 + b:14 + b]))
                link(v.tensor_tensor(st[:, 18:19], st[:, 17:18], lam[:, 3:4], ALU.mult))
                link(v.tensor_scalar(prob1[:, b, :], prob1[:, b, :], st[:, 16:17], None, ALU.mult))
                link(v.scalar_tensor_tensor(prob1[:, b, :], prob1[:, b + 1, :], st[:, 18:19], prob1[:, b, :], ALU.mult, ALU.add), "df_a")
            dmax(0)
            dmax(1)
            dcombine(0)
            for n in range(8):
                h, t = n // 2, n % 2
                if n + 2 < 8:
                    dmax(n + 2)
                if n + 1 < 8:
                    dcombine(n + 1)
                v.wait_ge(*nth("df_pv", n + 1))
                signal(v.tensor_copy(cat1[:, t, 512 + h * P:512 + h * P + P], ps[:, 6 + n % 2, 0:P]), "df_o")
            phase_over(v, "df")
            v.wait_ge(*nth("sub_sq", 1))
            for t in range(2):
                link(v.tensor_reduce(st[:, 32 + 4 * t:36 + 4 * t], tmp[:, t, 0:512].rearrange("p (h d) -> p h d", h=4), AXX, ALU.add))
            power(st[:, 40:48], st[:, 32:40], 2 * HD * EPS)
            for t in range(2):
                o = cat1[:, t, 512:1024].rearrange("p (h d) -> p h d", h=4)
                link(v.tensor_tensor(o, o, bch(st[:, 40 + 4 * t:44 + 4 * t], P), ALU.mult))
                ins = v.tensor_tensor(o, o, bcm(subln, 4), ALU.mult)
                (signal if t == 1 else lambda i, _n: link(i))(ins, "subln")
            cat_T("ooutc", LATS)
            gate_diag("o1", 16, cols2[:, 40:48], 1)
            phase_over(v, "ocat")
            residual("o1_sq", LATS, "o1", 2)
            scale_columns(32, cols2[:, 48:56])
            phase_over(v, "omix")
            norm_T("on2", LATS, 24, lambda t: fT[:, :, (t - 2) * P:(t - 1) * P], xn_l)
            v.wait_ge(*nth("logits", 1))
            link(v.tensor_copy(logit[:], ps[:, 4, 0:16].rearrange("p (t e) -> p t e", t=2)))
            for t in range(2):
                l = logit[:, t, :]
                p0, p1 = (pair[:, n, :].rearrange("p (e j) -> p e j", e=8) for n in range(2))
                link(v.tensor_tensor(p0, bcm(l, 8), bch(l, 8), ALU.is_gt))
                link(v.tensor_tensor(p1, bcm(l, 8), bch(l, 8), ALU.is_equal))
                link(v.tensor_tensor(pair[:, 1, :], pair[:, 1, :], C("earlier"), ALU.mult))
                link(v.tensor_tensor(pair[:, 0, :], pair[:, 0, :], pair[:, 1, :], ALU.add))
                link(v.tensor_reduce(rank[:, t, :], p0, AXX, ALU.add))
                link(v.tensor_reduce(st[:, 50 + t:51 + t], l, AXX, ALU.max))
                link(v.tensor_scalar(gate[:, t, :], l, st[:, 50 + t:51 + t], None, ALU.subtract))
            signal(v.tensor_scalar(sel, rank[:], 1.5, None, ALU.is_lt), "selected")
            v.wait_ge(*nth("selected", 1))
            v.drain().then_inc(S("lg_sub"), 1)
            v.wait_ge(*nth("lg_exp", 1))
            link(v.tensor_tensor(gate, gate, sel, ALU.mult))
            link(v.tensor_reduce(st[:, 52:54], gate, AXX, ALU.add))
            link(v.reciprocal(st[:, 54:56], st[:, 52:54]))
            link(v.tensor_tensor(gate, gate, bch(st[:, 54:56], 8), ALU.mult))
            v.wait_ge(*nth("positions", 1))
            link(v.tensor_copy(posn, ps[:, 5, 0:16].rearrange("p (t e) -> p t e", t=2)))
            link(v.memset(moe[:], 0.0))
            big, nth_big, weighed = plan_w[:, 0:8], plan_w[:, 8:16], plan_w[:, 16:24]
            count_to = C("iota")[0:1, 0:EXPERTS]
            link(v.tensor_scalar(big, ps[0:1, 5, 16:24], float(P), None, ALU.is_gt))
            link(v.tensor_tensor(by_pair, bcm(big, 8), C("earlier")[0:1].rearrange("p (e j) -> p e j", e=8), ALU.mult))
            link(v.tensor_reduce(nth_big, by_pair, AXX, ALU.add))
            link(v.tensor_tensor(weighed, big, count_to, ALU.mult))
            again = MAX_PASSES - EXPERTS
            link(v.tensor_tensor(by_pair[:, 0:again], bcm(nth_big, again), bch(C("iota")[0:1, 0:again], 8), ALU.is_equal))
            link(v.tensor_tensor(by_pair[:, 0:again], by_pair[:, 0:again], bcm(weighed, again), ALU.mult))
            link(v.memset(plan[:], 0.0))
            link(v.tensor_copy(plan[:, 0:8], count_to))
            link(v.tensor_copy(plan[:, 16:24], count_to))
            link(v.tensor_reduce(plan[:, 8:8 + again], by_pair[:, 0:again], AXX, ALU.add))
            link(v.tensor_scalar(plan[:, 24:24 + again], plan[:, 8:8 + again], float(EXPERTS), None, ALU.add))
            link(v.tensor_reduce(st[0:1, 56:57], big, AXX, ALU.add))
            link(v.tensor_scalar(plan[:, 15:16], st[0:1, 56:57], float(EXPERTS), None, ALU.add))
            link(v.tensor_copy(plan_i[:], plan[:]), "plan_ready")
            v.tensor_copy(sel16[:, :, 8:16], sel)
            v.tensor_copy(gate16[:, :, 8:16], gate)
            link(v.tensor_scalar(posn16[:, :, 8:16], posn, float(-P), None, ALU.add))
            phase_over(v, "route")
            def pick_tokens(it, e):
                for t in range(2):
                    v.tensor_scalar(pick[:, t, :], C("iota"), posn16[:, t, bass.ds(e, 1)], sel16[:, t, bass.ds(e, 1)],
                                    ALU.is_equal, ALU.mult).then_inc(S("m_p1"), 1)
                v.wait_ge(*nth("m_p1", it * 2 + 2))
                for t in range(2):
                    ins = v.tensor_scalar(pickw[:, t, :], pick[:, t, :], gate16[:, t, bass.ds(e, 1)], None, ALU.mult)
                ins.then_inc(S("m_pick"), 1)

            def gathered(it):
                v.wait_ge(*nth("m_gath", it + 1))
                for k in range(4, 8):
                    ins = v.tensor_scalar(xsT[:, k, :], ps[:, 3, (k - 4) * P:(k - 3) * P], scaleA[:, k, 0:1],
                                          modc[:, 24 + k, 0:1], ALU.mult, ALU.add)
                ins.then_inc(S("m_xsD"), 1)
                v.wait_ge(*nth("m_xsH", it + 1))
                v.tensor_tensor(xsL_r, xsT, xsH, ALU.subtract).then_inc(S("m_xsL"), 1)

            def add_pass(it):
                v.wait_ge(*nth("m_sc", it + 1))
                for t in range(2):
                    m2 = moe[:, t, :].rearrange("p (a b) -> p a b", a=2)
                    ins = v.tensor_tensor(m2, m2, ps[:, SCATTER_BANKS[t], :], ALU.add)
                ins.then_inc(S("m_acc"), 1)

            pick_tokens(0, 0)
            gathered(0)
            v.wait_ge(*nth("m_xsL", 1))
            for t in range(2):
                ins = v.memset(ps[:, SCATTER_BANKS[t], :], 0.0)
                ins.then_inc(S("m_sc0"), 1)
            v.wait_ge(*nth("m_sc0", 2))
            v.drain().then_inc(S("m_sc"), 1)
            n_passes = passes(v)
            with v.Fori(0, n_passes) as it:
                e_next = v.value_load(plan_i[0:1, bass.ds(it + 17, 1)], min_val=0, max_val=2 * EXPERTS - 1)
                for n in range(UNITS):
                    v.wait_ge(*nth("m_hi", it * UNITS + (n + 1)))
                    w = wslot[n % MRING]
                    v.tensor_tensor(wslot_r[n % MRING], w, hslot[n % HRING], ALU.subtract).then_inc(S("m_lo"), 1)
                    for c, what in BESIDE[n]:
                        if what == "gated":
                            v.wait_ge(*nth("m_silu", it * NCHUNK + (c + 1)))
                            if c >= 2:
                                v.wait_ge(*nth("m_tr", it * NCHUNK + (c - 1)))
                            v.tensor_tensor(hrow[:, c % 2, :], msil[:, c % 2, :], ps[:, 2 * (c % 2) + 1, :], ALU.mult)\
                                .then_inc(S("m_h"), 1)
                        elif what == "sum":
                            add_pass(it)
                        elif what == "pick":
                            v.wait_ge(*nth("m_pt", it + 1))
                            pick_tokens(it + 1, e_next)
                        elif what == "gathered":
                            gathered(it + 1)
                        elif what == "turned":
                            v.wait_ge(*nth("m_htH", it * NCHUNK + (c + 1)))
                            v.tensor_tensor(hTL_r[:, c % 2, :, :], ps[:, 6, :].rearrange("p (a b) -> p a b", a=4),
                                            hTH[:, c % 2, :, :], ALU.subtract).then_inc(S("m_ht"), 1)
            add_pass(n_passes)
            link(v.drain(), "moe_done")
            gate_diag("o3", 40, cols2[:, 56:64], 1)
            v.wait_ge(*nth("o3_gev", 2))
            v.wait_ge(*nth("o3_sq", 2))
            power(st[:, 16:18], st[:, 0:2], D * EPS)
            for t in range(2):
                link(v.scalar_tensor_tensor(mtmp, moe[:, t, :], st[:, 16 + t:17 + t], Gb[:, 0, :], ALU.mult, ALU.mult))
                link(v.tensor_tensor(xr[:, 2 + t, :], xr[:, 2 + t, :], mtmp, ALU.add), "result")


_INS = ['x', 'c', 'ctx', 'c_ctx', 'e_mod_w', 'e_mod_b', 'e_norms', 'e_w_in', 'e_conv_w', 'e_a_log', 'e_dt_bias',
        'e_gdn_norm', 'e_sink', 'e_w_out', 'e_ffn_gate', 'e_ffn_up', 'e_ffn_down', 'o_mod_w', 'o_mod_b', 'o_norms',
        'o_w_in', 'o_q_norm', 'o_kv_norm', 'o_w_uq', 'o_w_ukv', 'o_lambda', 'o_subln', 'o_w_out', 'o_router',
        'o_exp_gate', 'o_exp_up', 'o_exp_down']


def kernel(**inputs):
    import numpy as _np
    import concourse.bacc as _bacc
    from concourse import mybir as _mybir
    from concourse.bass_utils import run_bass_kernel_spmd as _run

    nc = _bacc.Bacc("TRN2", target_bir_lowering=False, num_devices=1)
    arrays, aps = {}, {}
    for name in _INS:
        arr = _np.ascontiguousarray(inputs[name])
        arrays[f"in_{name}"] = arr
        aps[name] = nc.dram_tensor(f"in_{name}", arr.shape, _mybir.dt.from_np(arr.dtype), kind="ExternalInput").ap()
    arrays["shape_consts"] = shape_constants()
    aps["consts"] = nc.dram_tensor("shape_consts", (P, N_CONST), F32, kind="ExternalInput").ap()
    out = nc.dram_tensor("out", (1, 256, D), F32, kind="ExternalOutput").ap()
    hybrid_trunk(nc, aps, out)
    r = _run(nc, [arrays], core_ids=[0])
    return r.results[0]["out"]
```
